# Optimizing a Trainium2 kernel written in Bass

```python
import jax, jax.numpy as jnp
from jax import lax
import numpy as np
import math

D_MODEL = 1024
BATCH = 1
SEQ = 512
DEPTH = 1

ATTN_HEADS = 8
HEAD_DIM = 64
ATTN_WIDTH = ATTN_HEADS * HEAD_DIM
CONV_WIDTH = D_MODEL - ATTN_WIDTH
CONV_KERNEL = 31
D_FF = 2816
FFN_KERNEL = 3
BLOCK_Q = 128
IN_WIDTH = 3 * ATTN_WIDTH + 2 * CONV_WIDTH
EPS = 1e-6


def rms_norm(x, g):
    xf = x.astype(jnp.float32)
    y = xf * lax.rsqrt(jnp.mean(xf * xf, axis=-1, keepdims=True) + EPS)
    return (y * g.astype(jnp.float32)).astype(x.dtype)

def layer_norm(x, g, b):
    xf = x.astype(jnp.float32)
    mu = jnp.mean(xf, axis=-1, keepdims=True)
    xc = xf - mu
    var = jnp.mean(xc * xc, axis=-1, keepdims=True)
    y = xc * lax.rsqrt(var + EPS) * g.astype(jnp.float32) + b.astype(jnp.float32)
    return y.astype(x.dtype)

def causal_depthwise_conv(x, w, b):
    k_width, channels = w.shape
    y = lax.conv_general_dilated(
        x, w[:, None, :].astype(x.dtype),
        window_strides=(1,), padding=[(k_width - 1, 0)],
        dimension_numbers=("NWC", "WIO", "NWC"),
        feature_group_count=channels)
    return y + b.astype(x.dtype)

def stick_breaking_attention(q, k, v):
    seq = q.shape[1]
    scale = q.shape[-1] ** -0.5
    outs = []
    for start in range(0, seq, BLOCK_Q):
        end = min(start + BLOCK_Q, seq)
        qb = q[:, start:end].astype(jnp.float32)
        kb = k[:, :end].astype(jnp.float32)
        vb = v[:, :end].astype(jnp.float32)
        z = jnp.einsum("bqhd,bkhd->bhqk", qb, kb) * scale
        t_idx = start + jnp.arange(end - start)[:, None]
        s_idx = jnp.arange(end)[None, :]
        mask = s_idx < t_idx
        log_beta = jax.nn.log_sigmoid(z)
        log_one_minus = jnp.where(mask, jax.nn.log_sigmoid(-z), 0.0)
        tail = lax.cumsum(log_one_minus, axis=3, reverse=True) - log_one_minus
        weights = jnp.where(mask, jnp.exp(log_beta + tail), 0.0)
        outs.append(jnp.einsum("bhqk,bkhd->bqhd", weights, vb))
    return jnp.concatenate(outs, axis=1).astype(v.dtype)

def first_inputs(seed: int = 0) -> dict:
    key = jax.random.key(seed)
    ks = jax.random.split(key, 16)
    f32 = jnp.float32
    out_scale = (2.0 * DEPTH) ** -0.5

    def nrm(k, shape, s):
        return jax.random.normal(k, shape, f32) * s

    return {
        "x": jax.random.normal(ks[0], (BATCH, SEQ, D_MODEL), f32),
        "norm1_g": 1.0 + nrm(ks[1], (DEPTH, D_MODEL), 0.02),
        "w_in": nrm(ks[2], (DEPTH, D_MODEL, IN_WIDTH), D_MODEL ** -0.5),
        "q_norm_g": 1.0 + nrm(ks[3], (DEPTH, HEAD_DIM), 0.02),
        "k_norm_g": 1.0 + nrm(ks[4], (DEPTH, HEAD_DIM), 0.02),
        "conv_dw_w": nrm(ks[5], (DEPTH, CONV_KERNEL, CONV_WIDTH), CONV_KERNEL ** -0.5),
        "conv_dw_b": nrm(ks[6], (DEPTH, CONV_WIDTH), 0.01),
        "conv_ln_g": 1.0 + nrm(ks[7], (DEPTH, CONV_WIDTH), 0.02),
        "conv_ln_b": nrm(ks[8], (DEPTH, CONV_WIDTH), 0.01),
        "w_out": nrm(ks[9], (DEPTH, D_MODEL, D_MODEL), D_MODEL ** -0.5 * out_scale),
        "norm2_g": 1.0 + nrm(ks[10], (DEPTH, D_MODEL), 0.02),
        "w_up": nrm(ks[11], (DEPTH, D_MODEL, 2 * D_FF), D_MODEL ** -0.5),
        "ffn_dw_w": nrm(ks[12], (DEPTH, FFN_KERNEL, D_FF), FFN_KERNEL ** -0.5),
        "ffn_dw_b": nrm(ks[13], (DEPTH, D_FF), 0.01),
        "w_down": nrm(ks[14], (DEPTH, D_FF, D_MODEL), D_FF ** -0.5 * out_scale),
    }

def first_block(x, norm1_g, w_in, q_norm_g, k_norm_g, conv_dw_w, conv_dw_b,
              conv_ln_g, conv_ln_b, w_out, norm2_g, w_up, ffn_dw_w, ffn_dw_b,
              w_down):
    bsz, seq, _ = x.shape
    splits = [ATTN_WIDTH, 2 * ATTN_WIDTH, 3 * ATTN_WIDTH, 3 * ATTN_WIDTH + CONV_WIDTH]
    for layer in range(DEPTH):
        h = rms_norm(x, norm1_g[layer])
        proj = h @ w_in[layer]
        q, k, v, glu_a, glu_b = jnp.split(proj, splits, axis=-1)
        q = rms_norm(q.reshape(bsz, seq, ATTN_HEADS, HEAD_DIM), q_norm_g[layer])
        k = rms_norm(k.reshape(bsz, seq, ATTN_HEADS, HEAD_DIM), k_norm_g[layer])
        v = v.reshape(bsz, seq, ATTN_HEADS, HEAD_DIM)
        attn = stick_breaking_attention(q, k, v).reshape(bsz, seq, ATTN_WIDTH)

        c = glu_a * jax.nn.sigmoid(glu_b)
        c = causal_depthwise_conv(c, conv_dw_w[layer], conv_dw_b[layer])
        c = jax.nn.silu(layer_norm(c, conv_ln_g[layer], conv_ln_b[layer]))

        mixed = jnp.concatenate([attn, c], axis=-1) @ w_out[layer]
        x = x + mixed

        h = rms_norm(x, norm2_g[layer])
        gate, val = jnp.split(h @ w_up[layer], 2, axis=-1)
        gate = jax.nn.silu(causal_depthwise_conv(gate, ffn_dw_w[layer], ffn_dw_b[layer]))
        x = x + (gate * val) @ w_down[layer]
    return x


Q_BLOCK = 128
DA_HEADS = 4
DA_DIM = 64
NSA_HEADS = 8
NSA_GROUPS = 2
NSA_DIM = 64
NSA_CMP_BLOCK = 32
NSA_SEL_BLOCK = 64
NSA_TOPN = 16
NSA_WINDOW = 512
NSA_CMP_HIDDEN = 256
MEM_LEN = 256
CA_HEADS = 4
CA_DIM = 128
PEER_HEADS = 8
PEER_NKEYS = 128
PEER_EXPERTS = PEER_NKEYS * PEER_NKEYS
PEER_DKEY = 256
PEER_TOPK = 16
PEER_CHUNK = 128

DA_QK = DA_HEADS * 2 * DA_DIM
DA_V = DA_HEADS * 2 * DA_DIM
NSA_Q = NSA_HEADS * NSA_DIM
NSA_KV = 6 * NSA_GROUPS * NSA_DIM
NSA_G = NSA_HEADS * 3
IN_SIZES = (DA_QK, DA_QK, DA_V, NSA_Q, NSA_KV, NSA_G, D_MODEL, D_MODEL)
IN_TOTAL = DA_QK * 2 + DA_V + NSA_Q + NSA_KV + NSA_G + 2 * D_MODEL


def rms_norm_2(x, g, eps=1e-6):
    xf = x.astype(jnp.float32)
    y = xf * lax.rsqrt(jnp.mean(xf * xf, axis=-1, keepdims=True) + eps)
    return (y * g.astype(jnp.float32)).astype(x.dtype)

def alibi_slopes(n_heads):
    return 2.0 ** (-8.0 * jnp.arange(1, n_heads + 1, dtype=jnp.float32) / n_heads)

def diff_attention(q, k, v, lam_params, subln_g, lambda_init):
    B, S, H, _, d = q.shape
    nqb = S // Q_BLOCK
    lam = (jnp.exp(jnp.sum(lam_params[0] * lam_params[1]).astype(jnp.float32))
           - jnp.exp(jnp.sum(lam_params[2] * lam_params[3]).astype(jnp.float32)) + lambda_init)
    slopes = alibi_slopes(H)
    scale = d ** -0.5
    kpos = jnp.arange(S)
    qb = q.reshape(B, nqb, Q_BLOCK, H, 2, d).transpose(1, 0, 2, 3, 4, 5)

    def block(args):
        qi, i = args
        qpos = i * Q_BLOCK + jnp.arange(Q_BLOCK)
        dist = (qpos[:, None] - kpos[None, :]).astype(jnp.float32)
        s = jnp.einsum('bqhcd,bkhcd->bhcqk', qi, k).astype(jnp.float32) * scale
        s = s - slopes[None, :, None, None, None] * dist
        s = jnp.where(dist >= 0, s, -jnp.inf)
        p = jax.nn.softmax(s, axis=-1)
        a = p[:, :, 0] - lam * p[:, :, 1]
        return jnp.einsum('bhqk,bkhe->bqhe', a.astype(v.dtype), v)

    o = lax.map(block, (qb, jnp.arange(nqb)))
    o = o.transpose(1, 0, 2, 3, 4).reshape(B, S, H, 2 * d)
    o = rms_norm_2(o, subln_g) * (1.0 - lambda_init)
    return o.reshape(B, S, H * 2 * d)

def nsa_attention(q, kv, gates, cmp_pos, ck_w1, ck_w2, cv_w1, cv_w2):
    B, S, G, R, dh = q.shape
    slopes = alibi_slopes(G * R).reshape(G, R)
    scale = dh ** -0.5
    pos = jnp.arange(S)
    k_c, v_c, k_s, v_s, k_w, v_w = [kv[:, :, j] for j in range(6)]

    nc = S // NSA_CMP_BLOCK

    def compress(t, w1, w2):
        tb = t.reshape(B, nc, NSA_CMP_BLOCK, G, dh) + cmp_pos[None, None, :, None, :]
        tb = tb.transpose(0, 1, 3, 2, 4).reshape(B, nc, G, NSA_CMP_BLOCK * dh)
        return jax.nn.gelu(tb @ w1, approximate=False) @ w2

    kc = compress(k_c, ck_w1, ck_w2)
    vc = compress(v_c, cv_w1, cv_w2)
    cpos = jnp.arange(nc) * NSA_CMP_BLOCK + (NSA_CMP_BLOCK - 1)
    dist_c = (pos[:, None] - cpos[None, :]).astype(jnp.float32)
    valid_c = dist_c >= 0
    s = jnp.einsum('bsgrd,bcgd->bgrsc', q, kc).astype(jnp.float32) * scale
    s = s - slopes[None, :, :, None, None] * dist_c
    s = jnp.where(valid_c, s, -1e30)
    p_cmp = jax.nn.softmax(s, axis=-1) * valid_c
    o_cmp = jnp.einsum('bgrsc,bcgd->bsgrd', p_cmp.astype(vc.dtype), vc)

    nsb = S // NSA_SEL_BLOCK
    ratio = NSA_SEL_BLOCK // NSA_CMP_BLOCK
    p_slc = p_cmp.sum(axis=2).reshape(B, G, S, nsb, ratio).sum(-1)
    blk = jnp.arange(nsb)
    cur = pos // NSA_SEL_BLOCK
    valid_b = blk[None, :] <= cur[:, None]
    forced = (blk[None, :] == 0) | (blk[None, :] == cur[:, None]) | (blk[None, :] == cur[:, None] - 1)
    score = jnp.where(forced, 1e4, jnp.where(valid_b, p_slc, -1e9))
    n_sel = min(NSA_TOPN, nsb)
    _, idx = lax.top_k(score, n_sel)

    nqb = S // Q_BLOCK
    ksb = k_s.reshape(B, nsb, NSA_SEL_BLOCK, G, dh).transpose(0, 3, 1, 2, 4)
    vsb = v_s.reshape(B, nsb, NSA_SEL_BLOCK, G, dh).transpose(0, 3, 1, 2, 4)
    q_blocks = q.reshape(B, nqb, Q_BLOCK, G, R, dh).transpose(1, 0, 2, 3, 4, 5)
    idx_blocks = idx.reshape(B, G, nqb, Q_BLOCK, n_sel).transpose(2, 0, 1, 3, 4)
    b_ix = jnp.arange(B)[:, None, None, None]
    g_ix = jnp.arange(G)[None, :, None, None]
    off = jnp.arange(NSA_SEL_BLOCK)

    def sel_block(args):
        qi, ii, i = args
        kg = ksb[b_ix, g_ix, ii]
        vg = vsb[b_ix, g_ix, ii]
        qpos = i * Q_BLOCK + jnp.arange(Q_BLOCK)
        kpos = ii[..., None] * NSA_SEL_BLOCK + off
        dist = (qpos[None, None, :, None, None] - kpos).astype(jnp.float32)[:, :, None]
        ss = jnp.einsum('bqgrd,bgqnld->bgrqnl', qi, kg).astype(jnp.float32) * scale
        ss = ss - slopes[None, :, :, None, None, None] * dist
        ss = jnp.where(dist >= 0, ss, -jnp.inf)
        pp = jax.nn.softmax(ss.reshape(B, G, R, Q_BLOCK, n_sel * NSA_SEL_BLOCK), axis=-1)
        pp = pp.reshape(B, G, R, Q_BLOCK, n_sel, NSA_SEL_BLOCK).astype(vg.dtype)
        return jnp.einsum('bgrqnl,bgqnld->bqgrd', pp, vg)

    o_slc = lax.map(sel_block, (q_blocks, idx_blocks, jnp.arange(nqb)))
    o_slc = o_slc.transpose(1, 0, 2, 3, 4, 5).reshape(B, S, G, R, dh)

    wb = NSA_WINDOW // Q_BLOCK
    pad = jnp.zeros((B, NSA_WINDOW, G, dh), k_w.dtype)
    kwp = jnp.concatenate([pad, k_w], axis=1).reshape(B, nqb + wb, Q_BLOCK, G, dh)
    vwp = jnp.concatenate([pad, v_w], axis=1).reshape(B, nqb + wb, Q_BLOCK, G, dh)
    kwin = jnp.concatenate([kwp[:, j:j + nqb] for j in range(wb + 1)], axis=2)
    vwin = jnp.concatenate([vwp[:, j:j + nqb] for j in range(wb + 1)], axis=2)
    qblk = q.reshape(B, nqb, Q_BLOCK, G, R, dh)
    qpos = jnp.arange(nqb)[:, None] * Q_BLOCK + jnp.arange(Q_BLOCK)
    kpos = jnp.arange(nqb)[:, None] * Q_BLOCK - NSA_WINDOW + jnp.arange((wb + 1) * Q_BLOCK)
    dist = (qpos[:, :, None] - kpos[:, None, :]).astype(jnp.float32)
    valid = (dist >= 0) & (dist < NSA_WINDOW) & (kpos[:, None, :] >= 0)
    sw = jnp.einsum('bnqgrd,bnkgd->bngrqk', qblk, kwin).astype(jnp.float32) * scale
    sw = sw - slopes[None, None, :, :, None, None] * dist[None, :, None, None]
    sw = jnp.where(valid[None, :, None, None], sw, -jnp.inf)
    pw = jax.nn.softmax(sw, axis=-1).astype(vwin.dtype)
    o_win = jnp.einsum('bngrqk,bnkgd->bnqgrd', pw, vwin).reshape(B, S, G, R, dh)

    o = gates[..., 0:1] * o_cmp + gates[..., 1:2] * o_slc + gates[..., 2:3] * o_win
    return o.reshape(B, S, G * R * dh)

def memory_cross_attention(u, m, wq, wkv, wo):
    B, S, _ = u.shape
    M = m.shape[1]
    q = (u @ wq).reshape(B, S, CA_HEADS, CA_DIM)
    kv = (m @ wkv).reshape(B, M, 2, CA_HEADS, CA_DIM)
    s = jnp.einsum('bshd,bmhd->bhsm', q, kv[:, :, 0]).astype(jnp.float32) * (CA_DIM ** -0.5)
    p = jax.nn.softmax(s, axis=-1).astype(u.dtype)
    o = jnp.einsum('bhsm,bmhd->bshd', p, kv[:, :, 1]).reshape(B, S, CA_HEADS * CA_DIM)
    return o @ wo

def peer_ffn(u, w_q, sub_keys, u_tab, v_tab):
    B, S, D = u.shape
    T = B * S
    K = PEER_TOPK
    H = PEER_HEADS
    xt = u.reshape(T, D)
    q = (xt @ w_q).reshape(T, H, 2, PEER_DKEY // 2)
    s = jnp.einsum('thcd,hcnd->thcn', q, sub_keys).astype(jnp.float32)
    top_s, top_i = lax.top_k(s, K)
    cand = (top_s[:, :, 0, :, None] + top_s[:, :, 1, None, :]).reshape(T, H, K * K)
    cand_i = (top_i[:, :, 0, :, None] * PEER_NKEYS + top_i[:, :, 1, None, :]).reshape(T, H, K * K)
    best_s, best_j = lax.top_k(cand, K)
    expert = jnp.take_along_axis(cand_i, best_j, axis=-1)
    g = jax.nn.softmax(best_s, axis=-1).astype(u.dtype)
    nch = T // PEER_CHUNK

    def chunk(args):
        xc, ec, gc = args
        act = jax.nn.gelu(jnp.einsum('cd,chkd->chk', xc, u_tab[ec]), approximate=False)
        return jnp.einsum('chk,chkd->cd', gc * act, v_tab[ec])

    out = lax.map(chunk, (xt.reshape(nch, PEER_CHUNK, D),
                          expert.reshape(nch, PEER_CHUNK, H, K),
                          g.reshape(nch, PEER_CHUNK, H, K)))
    return out.reshape(B, S, D)

def second_inputs(seed: int = 0) -> dict:
    key = jax.random.key(seed)
    ks = jax.random.split(key, 32)
    L, D = DEPTH, D_MODEL

    def nrm(k, shape, scale):
        return jax.random.normal(k, shape, jnp.float32) * scale

    def gain(k, shape):
        return 1.0 + 0.02 * jax.random.normal(k, shape, jnp.float32)

    return {
        "x": nrm(ks[0], (BATCH, SEQ, D), 1.0),
        "mem": nrm(ks[1], (BATCH, MEM_LEN, D), 1.0),
        "norm_mix": gain(ks[2], (L, D)),
        "w_in": nrm(ks[3], (L, D, IN_TOTAL), D ** -0.5),
        "diff_lambda": nrm(ks[4], (L, 4, DA_DIM), 0.1),
        "diff_subln": gain(ks[5], (L, 2 * DA_DIM)),
        "nsa_cmp_pos": nrm(ks[6], (L, NSA_CMP_BLOCK, NSA_DIM), 0.1),
        "nsa_ck_w1": nrm(ks[7], (L, NSA_CMP_BLOCK * NSA_DIM, NSA_CMP_HIDDEN), (NSA_CMP_BLOCK * NSA_DIM) ** -0.5),
        "nsa_ck_w2": nrm(ks[8], (L, NSA_CMP_HIDDEN, NSA_DIM), NSA_CMP_HIDDEN ** -0.5),
        "nsa_cv_w1": nrm(ks[9], (L, NSA_CMP_BLOCK * NSA_DIM, NSA_CMP_HIDDEN), (NSA_CMP_BLOCK * NSA_DIM) ** -0.5),
        "nsa_cv_w2": nrm(ks[10], (L, NSA_CMP_HIDDEN, NSA_DIM), NSA_CMP_HIDDEN ** -0.5),
        "w_branch_a": nrm(ks[11], (L, DA_V, D), DA_V ** -0.5),
        "w_branch_b": nrm(ks[12], (L, NSA_Q, D), NSA_Q ** -0.5),
        "w_out": nrm(ks[13], (L, D, D), D ** -0.5),
        "norm_cross": gain(ks[14], (L, D)),
        "norm_mem": gain(ks[15], (L, D)),
        "w_cross_q": nrm(ks[16], (L, D, CA_HEADS * CA_DIM), D ** -0.5),
        "w_cross_kv": nrm(ks[17], (L, D, 2 * CA_HEADS * CA_DIM), D ** -0.5),
        "w_cross_o": nrm(ks[18], (L, CA_HEADS * CA_DIM, D), (CA_HEADS * CA_DIM) ** -0.5),
        "norm_ffn": gain(ks[19], (L, D)),
        "peer_wq": nrm(ks[20], (L, D, PEER_HEADS * PEER_DKEY), D ** -0.5),
        "peer_subkeys": nrm(ks[21], (L, PEER_HEADS, 2, PEER_NKEYS, PEER_DKEY // 2), (PEER_DKEY // 2) ** -0.5),
        "peer_u": nrm(ks[22], (L, PEER_EXPERTS, D), D ** -0.5),
        "peer_v": nrm(ks[23], (L, PEER_EXPERTS, D), (PEER_HEADS * PEER_TOPK) ** -0.5),
        "norm_final": gain(ks[24], (D,)),
    }

def second_block(x, mem, norm_mix, w_in, diff_lambda, diff_subln, nsa_cmp_pos, nsa_ck_w1, nsa_ck_w2,
              nsa_cv_w1, nsa_cv_w2, w_branch_a, w_branch_b, w_out, norm_cross, norm_mem,
              w_cross_q, w_cross_kv, w_cross_o, norm_ffn, peer_wq, peer_subkeys, peer_u, peer_v,
              norm_final):
    B, S, D = x.shape
    split_at = np.cumsum(IN_SIZES)[:-1].tolist()
    h = x
    for l in range(DEPTH):
        lambda_init = 0.8 - 0.6 * math.exp(-0.3 * l)
        u = rms_norm_2(h, norm_mix[l])
        qa, ka, va, qb, kvb, gb, gate_a, gate_b = jnp.split(u @ w_in[l], split_at, axis=-1)
        o_a = diff_attention(qa.reshape(B, S, DA_HEADS, 2, DA_DIM),
                             ka.reshape(B, S, DA_HEADS, 2, DA_DIM),
                             va.reshape(B, S, DA_HEADS, 2 * DA_DIM),
                             diff_lambda[l], diff_subln[l], lambda_init)
        R = NSA_HEADS // NSA_GROUPS
        o_b = nsa_attention(qb.reshape(B, S, NSA_GROUPS, R, NSA_DIM),
                            kvb.reshape(B, S, 6, NSA_GROUPS, NSA_DIM),
                            jax.nn.sigmoid(gb).reshape(B, S, NSA_GROUPS, R, 3),
                            nsa_cmp_pos[l], nsa_ck_w1[l], nsa_ck_w2[l], nsa_cv_w1[l], nsa_cv_w2[l])
        merged = (jax.nn.sigmoid(gate_a) * (o_a @ w_branch_a[l])
                  + jax.nn.sigmoid(gate_b) * (o_b @ w_branch_b[l]))
        h = h + merged @ w_out[l]
        h = h + memory_cross_attention(rms_norm_2(h, norm_cross[l]), rms_norm_2(mem, norm_mem[l]),
                                       w_cross_q[l], w_cross_kv[l], w_cross_o[l])
        h = h + peer_ffn(rms_norm_2(h, norm_ffn[l]), peer_wq[l], peer_subkeys[l], peer_u[l], peer_v[l])
    return rms_norm_2(h, norm_final)


def setup_inputs(seed=0):
    out = dict(first_inputs(seed))
    for name, value in second_inputs(seed + 1).items():
        if name != "x":
            out[name + "_2"] = value
    return out


def reference(
    x, norm1_g, w_in, q_norm_g, k_norm_g, conv_dw_w, conv_dw_b, conv_ln_g, conv_ln_b, w_out,
    norm2_g, w_up, ffn_dw_w, ffn_dw_b, w_down, mem_2, norm_mix_2, w_in_2, diff_lambda_2,
    diff_subln_2, nsa_cmp_pos_2, nsa_ck_w1_2, nsa_ck_w2_2, nsa_cv_w1_2, nsa_cv_w2_2,
    w_branch_a_2, w_branch_b_2, w_out_2, norm_cross_2, norm_mem_2, w_cross_q_2, w_cross_kv_2,
    w_cross_o_2, norm_ffn_2, peer_wq_2, peer_subkeys_2, peer_u_2, peer_v_2, norm_final_2,
):
    x = first_block(
        x, norm1_g, w_in, q_norm_g, k_norm_g, conv_dw_w, conv_dw_b, conv_ln_g, conv_ln_b, w_out,
        norm2_g, w_up, ffn_dw_w, ffn_dw_b, w_down,
    )
    return second_block(
        x, mem_2, norm_mix_2, w_in_2, diff_lambda_2, diff_subln_2, nsa_cmp_pos_2, nsa_ck_w1_2,
        nsa_ck_w2_2, nsa_cv_w1_2, nsa_cv_w2_2, w_branch_a_2, w_branch_b_2, w_out_2,
        norm_cross_2, norm_mem_2, w_cross_q_2, w_cross_kv_2, w_cross_o_2, norm_ffn_2, peer_wq_2,
        peer_subkeys_2, peer_u_2, peer_v_2, norm_final_2,
    )


_drawn_inputs = setup_inputs


def setup_inputs(seed=0):
    import zlib

    import numpy as np

    out = dict(_drawn_inputs(seed))
    spreads = {}
    factors = {'norm1_g': 4.583,
     'q_norm_g': 8.0,
     'k_norm_g': 8.0,
     'conv_dw_b': 5.653,
     'conv_ln_g': 5.972,
     'conv_ln_b': 8.0,
     'norm2_g': 4.765,
     'ffn_dw_b': 8.0,
     'norm_mix_2': 4.492,
     'diff_subln_2': 6.786,
     'nsa_cmp_pos_2': 3.713,
     'nsa_ck_w2_2': 2.725,
     'norm_cross_2': 8.0,
     'norm_mem_2': 8.0,
     'norm_ffn_2': 64.0,
     'norm_final_2': 8.061}
    for name, (base, spread) in spreads.items():
        noise = np.random.default_rng([zlib.crc32(name.encode()), seed]).standard_normal(out[name].shape)
        drawn = base * np.exp(spread * noise) if base else spread * noise
        out[name] = __import__('jax').numpy.asarray(drawn.astype(out[name].dtype))
    for name, factor in factors.items():
        out[name] = (out[name] * factor).astype(out[name].dtype)
    return out
```

```python
import math
from contextlib import ExitStack

import numpy as np

import concourse.bass as bass
from concourse import mybir

F32 = mybir.dt.float32
F32R = mybir.dt.float32r
BF16 = mybir.dt.bfloat16
U32 = mybir.dt.uint32
ALU = mybir.AluOpType
ACT = mybir.ActivationFunctionType
AX_X = mybir.AxisListType.X

P = 128
S = 512
QT = S // P
D = 1024
KD = D // P
EPS = 1e-6

HEADS = 8
HD = 64
AW = HEADS * HD
CW = D - AW
CT = CW // P
TAPS = 31
FF = 2816
FT = FF // P
FTAPS = 3
FHALF = (12, 10)

DA_H = 4
NSA_H, NSA_G, NSA_R = 8, 2, 4
CMP = 32
NCMP = S // CMP
CMP_HID = 256
MEM = 256
CA_H = 4
PH, PK = 8, 16
NK = 128
LAMBDA_INIT = 0.8 - 0.6 * math.exp(-0.3 * 0)
NEG = -1e30

BLK = 2048

LAYERS = [
    ("in_fm", 8, KD, 2, 256, 2),
    ("in_v", 2, KD, QT, 256, 2),
    ("out1", 4, KD, 2, 256, 2),
    ("up0", FHALF[0], KD, 2, 256, 2),
    ("down0", 8, FHALF[0], 1, 128, 4),
    ("up1", FHALF[1], KD, 2, 256, 2),
    ("down1", 8, FHALF[1], 1, 128, 4),
    ("mix_fm", 8, KD, 2, 256, 2),
    ("mix_tm", 4, KD, QT, 256, 2),
    ("gates", 8, KD, 2, 256, 2),
    ("branch", 4, KD, 4, 256, 2),
    ("out2", 4, KD, 2, 256, 2),
    ("cross_q", 2, KD, 2, 256, 2),
    ("cross_k", 2, KD, 2, 256, 2),
    ("cross_v", 2, KD, MEM // P, 256, 2),
    ("cross_o", 2, AW // P, 4, 512, 2),
    ("peer_q", 8, KD, 2, 256, 2),
]


def layer_table():
    table, ends, block, tile = {}, [], 0, 0
    for name, nb, kt, tiles, cols, unroll in LAYERS:
        table[name] = dict(nb=nb, kt=kt, tiles=tiles, cols=cols, unroll=unroll, block=block, tile=tile)
        for _ in range(nb):
            tile += tiles
            ends.append(tile)
        block += nb
    return table, ends


LAYER, TILES_AFTER = layer_table()

PARAMS = [("norm1", KD), ("norm2", KD), ("norm_mix", KD), ("norm_cross", KD), ("norm_mem", KD), ("norm_ffn", KD),
          ("norm_final", KD), ("q_norm", 1), ("k_norm", 1), ("conv_w", CT * TAPS), ("conv_b", CT), ("ln_g", CT),
          ("ln_b", CT), ("ffn_w", FT * FTAPS), ("ffn_b", FT), ("subln", 1), ("cmp_pos", CMP), ("lam", 4)]
PCOL, NPAR = {}, 0
for _n, _w in PARAMS:
    PCOL[_n] = NPAR
    NPAR += _w

INPUTS = [
    ("x_t", (P, KD, S)), ("mem_t", (P, KD, MEM)), ("params", (P, NPAR)),
    ("w_small", (len(TILES_AFTER), P, BLK)),
    ("cmp_w1", (2, P, CMP // 2, CMP_HID)), ("cmp_w2", (2, P, CMP_HID // P, HD)),
    ("subkeys_t", (P, 2 * PH, NK)),
    ("expert_u", (NK, P, KD, P)), ("expert_v", (NK, P, D)),
]

OUTPUTS = [("out_t", (P, KD, S))]

KB = 1024
BASE = 16512
RES, XH, XL = BASE, BASE + 16 * KB, BASE + 32 * KB
RAW, WH, WL = BASE + 48 * KB, BASE + 64 * KB, BASE + 80 * KB
CONST = BASE + 96 * KB
SCR = CONST + 13 * KB


def build_program(nc, io):
    with ExitStack() as ctx:
        sems = {}

        def sem(name):
            if name not in sems:
                sems[name] = ctx.enter_context(nc.semaphore(name))
            return sems[name]

        def at(name, shape, offset, dt=F32):
            return nc.alloc_sbuf_tensor_at(name, list(shape), dt, offset=offset)

        cursor = [CONST]

        def const(name, shape, dt=F32):
            size = int(np.prod(shape[1:])) * (2 if dt == BF16 else 4)
            t = at(name, shape, cursor[0], dt)
            cursor[0] += (size + 31) // 32 * 32
            assert cursor[0] <= SCR
            return t

        psum = [ctx.enter_context(nc.psum_tensor(f"bank{i}", [P, S], F32)) for i in range(8)]
        lin_bank, att_bank = psum[:4], psum[4:]

        resid = at("resid", [P, KD, S], RES)
        xh = at("xh", [P, KD, S], XH, F32R)
        xl = at("xl", [P, KD, S], XL, F32R)
        raw = [at(f"w_raw{i}", [P, BLK], RAW + i * 8 * KB) for i in range(2)]
        wh = [at(f"w_hi{i}", [P, BLK], WH + i * 8 * KB, F32R) for i in range(2)]
        wl = [at(f"w_lo{i}", [P, BLK], WL + i * 8 * KB, F32R) for i in range(2)]

        params = const("params_sb", [P, NPAR])
        ident = const("ident", [P, P])
        ones = const("ones", [P, P])
        later_key = const("later_key", [P, P])
        causal = const("causal", [P, P])
        dist = const("dist", [P, S])
        cmp_dist = const("cmp_dist", [P, QT, NCMP])
        cmp_valid = const("cmp_valid", [P, QT, NCMP])
        head_sum = const("head_sum", [P, 8, 16])
        iota16 = const("iota16", [P, PK])
        iota_key = const("iota_key", [P, NK])
        eps = const("eps", [P, 1])
        qg = const("qg", [P, 1])
        subln_g = const("subln_g", [P, 1])
        lam_prod = const("lam_prod", [P, 2])
        lam_exp = const("lam_exp", [P, 2])
        lam = const("lam_col", [P, 1])
        gates24 = const("gates24", [P, QT, NSA_H * 3])

        def col(name, i=0):
            return params[:, PCOL[name] + i:PCOL[name] + i + 1]

        qk = at("qk", [P, 8, S], SCR)
        vtok = at("vtok", [P, QT, AW], SCR + 16 * KB)
        PADW = S + TAPS - 1
        cpad = at("cpad", [P, CT, PADW], SCR + 24 * KB)
        cacc = at("cacc", [P, CT, S], SCR + 33 * KB)
        attn = at("attn", [P, CT, S], SCR + 41 * KB)
        NW = 1280
        KOFF = [0, 512, 1024, 896]
        STK = SCR + 49 * KB
        ln1 = at("ln1", [P, NW], STK)
        soft = [at(f"soft{i}", [P, NW], STK + (5 + 5 * i) * KB) for i in range(2)]
        lbeta = [at(f"lbeta{i}", [P, NW], STK + (15 + 5 * i) * KB) for i in range(2)]
        wgt = [at(f"wgt{i}", [P, NW], STK + (25 + 5 * i) * KB) for i in range(2)]
        qk_sq = at("qk_sq", [P, 8, S], STK)
        std16 = at("std16", [16, S], STK + 16 * KB)
        rstd16 = at("rstd16", [16, S], STK + 18 * KB)
        glu_sig = [at(f"glu_sig{i}", [P, S], STK + (20 + 2 * i) * KB) for i in range(2)]
        head_spread = at("head_spread", [16, 8 * P], STK + 35 * KB)
        ln_sq = at("ln_sq", [P, CT, S], STK)
        ln_std = at("ln_std", [P, S], STK + 8 * KB)
        ln_rstd = at("ln_rstd", [P, S], STK + 10 * KB)

        fh = at("fh", [P, FHALF[0], S], SCR, F32R)
        fl = at("fl", [P, FHALF[0], S], SCR + 24 * KB, F32R)
        f_conv = [at(f"f_conv{i}", [P, S], SCR + (48 + 2 * i) * KB) for i in range(2)]
        f_silu = [at(f"f_silu{i}", [P, S], SCR + (52 + 2 * i) * KB) for i in range(2)]
        f_out = [at(f"f_out{i}", [P, S], SCR + (56 + 2 * i) * KB) for i in range(2)]

        class Chain:

            def __init__(self, eng, name):
                self.eng, self.sem, self.n = eng, sem(name), 0

            def link(self, ins):
                self.n += 1
                ins.then_inc(self.sem, 1)
                self.eng.wait_ge(self.sem, self.n)

        def wait(eng, *needs):
            for name, value in needs:
                if value > 0:
                    eng.wait_ge(sem(name), value)

        NB = len(TILES_AFTER)

        def load_blocks(sp, first, last):
            for g in range(first, last):
                sp.wait_ge(sem("lo_done"), g + 1)
                n = size_of(g)
                sp.dma_start(raw[g % 2][:, :n], io["w_small"][g, :, :n]).then_inc(sem(f"raw_loaded{g % 2}"), 16)

        def size_of(g):
            for t in LAYER.values():
                if t["block"] <= g < t["block"] + t["nb"]:
                    return t["kt"] * t["cols"]

        def split_hi(act, g):
            if g >= NB:
                return
            wait(act, (f"raw_loaded{g % 2}", 16 * (g // 2 + 1)))
            if g >= 2:
                wait(act, ("lin_done", TILES_AFTER[g - 2]))
            n = size_of(g)
            act.activation(wh[g % 2][:, :n], raw[g % 2][:, :n], ACT.Copy).then_inc(sem("hi_done"), 1)

        def split_lo(pool, g):
            n = size_of(g)
            pool.wait_ge(sem("hi_done"), g + 1)
            pool.tensor_tensor(wl[g % 2][:, :n], raw[g % 2][:, :n], wh[g % 2][:, :n].bitcast(F32),
                               ALU.subtract).then_inc(sem("lo_done"), 1)

        def products(pe, out, pairs):
            for k, (ah, al, bh, bl) in enumerate(pairs):
                pe.matmul(out, al, bh, start=(k == 0), stop=False)
                pe.matmul(out, ah, bl, start=False, stop=False)
                last = pe.matmul(out, ah, bh, start=False, stop=(k == len(pairs) - 1))
            return last

        def linear_pe(pe, name, pairs_of, ncols):
            t = LAYER[name]
            u, tiles = t["unroll"], t["tiles"]

            def step(i):
                for s in range(u):
                    pe.wait_ge(sem("lo_done"), i * u + (t["block"] + s + 3))
                    for m in range(tiles):
                        n = s * tiles + m
                        pe.wait_ge(sem("bank_free"), i * (u * tiles) + (t["tile"] + n + 1))
                        out = lin_bank[n % 4][:, :ncols]
                        products(pe, out, pairs_of(s % 2, m)).then_inc(sem("lin_done"), 1)

            assert t["tile"] % 4 == 0 and t["block"] % 2 == 0 and u * tiles % 4 == 0 and t["nb"] % u == 0
            if t["nb"] == u:
                step(0)
            else:
                with pe.Fori(0, t["nb"] // u) as i:
                    step(i)

        def weights_first(name, hi, lo, n=S):
            t = LAYER[name]
            kt, cols = t["kt"], t["cols"]

            def pairs(slot, m):
                def w(x, k):
                    return x[slot][:, k * cols + m * P:k * cols + m * P + P]
                return [(w(wh, k), w(wl, k), hi[:, k, :n], lo[:, k, :n]) for k in range(kt)]
            return pairs

        def tokens_first(name, hi, lo):
            t = LAYER[name]
            kt, cols = t["kt"], t["cols"]

            def pairs(slot, m):
                def w(x, k):
                    return x[slot][:, k * cols:(k + 1) * cols]
                return [(hi[:, k, m * P:m * P + P], lo[:, k, m * P:m * P + P], w(wh, k), w(wl, k)) for k in range(kt)]
            return pairs

        def tile_ready(eng, name, n):
            eng.wait_ge(sem("lin_done"), LAYER[name]["tile"] + n + 1)
            return lin_bank[n % 4]

        NORMS = ["n1", "n2", "n3", "nm", "n4", "n5"]

        def before(st, per_norm):
            return NORMS.index(st) * per_norm

        def norm_done(eng, st):
            eng.wait_ge(sem("norm_lo"), before(st, KD) + KD)

        def norm_act(act, st, src, sq, std, hi, n, needs):
            wait(act, *needs)
            for k in range(KD):
                act.activation(sq[:, k, :n], src[:, k, :n], ACT.Square).then_inc(sem("norm_sq"), 1)
            act.wait_ge(sem("norm_sum"), before(st, 1) + 1)
            act.activation(std[:, :n], att_bank[0][:, :n], ACT.Sqrt, bias=eps[:, 0:1], scale=1.0 / D)\
               .then_inc(sem("norm_std"), 1)
            for k in range(KD):
                act.wait_ge(sem("norm_h"), before(st, KD) + k + 1)
                act.activation(hi[:, k, :n], sq[:, k, :n], ACT.Copy).then_inc(sem("norm_hi"), 1)

        def norm_pe(pe, st, sq, n):
            for k in range(KD):
                pe.wait_ge(sem("norm_sq"), before(st, KD) + k + 1)
                last = pe.matmul(att_bank[0][:, :n], ones[:, :], sq[:, k, :n], start=(k == 0), stop=(k == KD - 1))
            last.then_inc(sem("norm_sum"), 1)

        def norm_dve(dve, chain, st, src, sq, std, rstd, hi, lo, gain, n):
            dve.wait_ge(sem("norm_std"), before(st, 1) + 1)
            chain.link(dve.reciprocal(rstd[:, :n], std[:, :n]))
            for k in range(KD):
                dve.scalar_tensor_tensor(out=sq[:, k, :n], in0=src[:, k, :n], scalar=col(gain, k), in1=rstd[:, :n],
                                         op0=ALU.mult, op1=ALU.mult).then_inc(sem("norm_h"), 1)
            for k in range(KD):
                dve.wait_ge(sem("norm_hi"), before(st, KD) + k + 1)
                dve.tensor_tensor(lo[:, k, :n], sq[:, k, :n], hi[:, k, :n].bitcast(F32), ALU.subtract)\
                   .then_inc(sem("norm_lo"), 1)

        NRM1, RS1 = STK, STK + 24 * KB
        nrm1 = at("nrm1", [P, KD, S], NRM1)
        std1 = at("std1", [P, S], RS1)
        rstd1 = at("rstd1", [P, S], RS1 + 2 * KB)
        nrm2 = at("nrm2", [P, KD, S], SCR + 60 * KB)
        std2 = at("std2", [P, S], SCR + 76 * KB)
        rstd2 = at("rstd2", [P, S], SCR + 78 * KB)

        PIECES = [(0, 512), (512, 512), (1024, 256)]

        def regions(kb):
            off = KOFF[kb]
            return off // S, off % S, S - kb * P

        CONV_OPS = [(tap, ct) for tap in range(TAPS) for ct in range(CT)]

        def conv_steps(dve, first, last):
            for n in range(first, min(last, len(CONV_OPS))):
                tap, ct = CONV_OPS[n]
                w = col("conv_w", ct * TAPS + tap)
                x = cpad[:, ct, tap:tap + S]
                if n >= CT:
                    dve.wait_ge(sem("conv"), n - CT + 1)
                    ins = dve.scalar_tensor_tensor(out=cacc[:, ct, :], in0=x, scalar=w, in1=cacc[:, ct, :],
                                                   op0=ALU.mult, op1=ALU.add)
                else:
                    ins = dve.tensor_scalar(cacc[:, ct, :], x, w, col("conv_b", ct), ALU.mult, ALU.add)
                ins.then_inc(sem("conv"), 1)

        def block1_act(act):
            wait(act, ("x_loaded", 16), ("consts", N_CONST))
            norm_act(act, "n1", resid, nrm1, std1, xh, S, [])
            split_hi(act, 0)
            split_hi(act, 1)
            base = LAYER["in_fm"]["block"]
            for b in range(4):
                split_hi(act, base + b + 2)
            for j in range(CT):
                bank = tile_ready(act, "in_fm", 8 + 2 * j + 1)
                if j >= 2:
                    act.wait_ge(sem("bank_free"), 4 + 8 + 2 * (j - 1))
                act.activation(glu_sig[j % 2][:, :], bank[:, :], ACT.Sigmoid).then_inc(sem("glu_sig"), 1)
                split_hi(act, base + 4 + j + 2)
            for b in range(2):
                split_hi(act, LAYER["in_v"]["block"] + b + 2)
            act.wait_ge(sem("bank_free"), 4 + 16)
            for j in range(8):
                act.activation(qk_sq[:, j, :], qk[:, j, :], ACT.Square).then_inc(sem("qk_sq"), 1)
            act.wait_ge(sem("qk_sum"), 1)
            act.activation(std16[:, :], att_bank[0][0:16, :], ACT.Sqrt, bias=eps[0:16, 0:1], scale=1.0 / HD)\
               .then_inc(sem("qk_std"), 1)

            def pre(h):
                act.wait_ge(sem("st_z"), h + 1)
                if h >= 1:
                    act.wait_ge(sem("st_zread"), h)
                for b, (off, w) in enumerate(PIECES):
                    ins = act.activation(ln1[:, off:off + w], att_bank[b][:, :w], ACT.Abs)
                ins.then_inc(sem("st_act"), 1)
                act.wait_ge(sem("st_act"), 2 * h + 1)
                act.activation(ln1[:, :], ln1[:, :], ACT.Exp, scale=-1.0).then_inc(sem("st_act"), 1)
                act.wait_ge(sem("st_act"), 2 * h + 2)
                act.activation(ln1[:, :], ln1[:, :], ACT.Ln, bias=1.0).then_inc(sem("st_ln"), 1)

            pre(0)
            for h in range(HEADS):
                if h + 1 < HEADS:
                    pre(h + 1)
                act.wait_ge(sem("st_logw"), h + 1)
                act.activation(wgt[h % 2][:, :], wgt[h % 2][:, :], ACT.Exp).then_inc(sem("st_w"), 1)
                r = h % 2 * HD
                act.wait_ge(sem("st_pv"), h + 1)
                act.activation(attn[r:r + HD, h // 2, :], lin_bank[3][r:r + HD, :], ACT.Copy).then_inc(sem("st_o"), 1)
            act.wait_ge(sem("ln_xc"), CT)
            for k in range(CT):
                act.activation(ln_sq[:, k, :], cacc[:, k, :], ACT.Square).then_inc(sem("ln_sq"), 1)
            act.wait_ge(sem("ln_var"), 1)
            act.activation(ln_std[:, :], att_bank[1][:, :], ACT.Sqrt, bias=eps[:, 0:1], scale=1.0 / CW)\
               .then_inc(sem("ln_std"), 1)
            for k in range(CT):
                act.activation(xh[:, k, :], attn[:, k, :], ACT.Copy).then_inc(sem("mix1_hi"), 1)
            for k in range(CT):
                act.wait_ge(sem("ln_y"), k + 1)
                act.activation(cacc[:, k, :], cacc[:, k, :], ACT.Silu, bias=col("ln_b", k), scale=col("ln_g", k))\
                   .then_inc(sem("ln_c"), 1)
                act.wait_ge(sem("ln_c"), k + 1)
                act.activation(xh[:, CT + k, :], cacc[:, k, :], ACT.Copy).then_inc(sem("mix1_hi"), 1)
            for b in range(4):
                split_hi(act, LAYER["out1"]["block"] + b + 2)
            after = LAYER["out1"]["tile"] + 8
            norm_act(act, "n2", resid, nrm2, std2, xh, S, [("bank_free", 4 + after)])
            j = 0
            for half in range(2):
                up, down = LAYER[f"up{half}"], LAYER[f"down{half}"]
                for b in range(FHALF[half]):
                    act.wait_ge(sem("ff_conv"), j + 1)
                    act.activation(f_silu[j % 2][:, :], f_conv[j % 2][:, :], ACT.Silu).then_inc(sem("ff_silu"), 1)
                    act.wait_ge(sem("bank_free"), 4 + up["tile"] + 2 * (b + 1))
                    act.activation(fh[:, b, :], f_out[j % 2][:, :], ACT.Copy).then_inc(sem("ff_hi"), 1)
                    split_hi(act, up["block"] + b + 2)
                    j += 1
                for b in range(8):
                    split_hi(act, down["block"] + b + 2)

        def block1_pool(pool):
            for b in range(LAYER["up0"]["block"] + 2):
                split_lo(pool, b)
            j = 0
            for half in range(2):
                up, down = LAYER[f"up{half}"], LAYER[f"down{half}"]
                for b in range(FHALF[half]):
                    pool.wait_ge(sem("ff_hi"), j + 1)
                    pool.tensor_tensor(fl[:, b, :], f_out[j % 2][:, :], fh[:, b, :].bitcast(F32), ALU.subtract)\
                        .then_inc(sem("ff_lo"), 1)
                    split_lo(pool, up["block"] + b + 2)
                    j += 1
                for b in range(8):
                    split_lo(pool, down["block"] + b + 2)

        def block1_pe(pe):
            wait(pe, ("consts", N_CONST))
            norm_pe(pe, "n1", nrm1, S)
            norm_done(pe, "n1")
            linear_pe(pe, "in_fm", weights_first("in_fm", xh, xl), S)
            linear_pe(pe, "in_v", tokens_first("in_v", xh, xl), 256)
            for j in range(8):
                pe.wait_ge(sem("qk_sq"), j + 1)
                last = pe.matmul(att_bank[0][0:16, :], head_sum[:, j, :], qk_sq[:, j, :], start=(j == 0), stop=(j == 7))
            last.then_inc(sem("qk_sum"), 1)
            pe.wait_ge(sem("qk_rstd"), 1)
            for j in range(8):
                if j >= 2:
                    pe.wait_ge(sem("qk_ready"), j - 1)
                pe.matmul(att_bank[1 + j % 2][:, :], head_spread[:, j * P:(j + 1) * P], rstd16[:, :],
                          start=True, stop=True).then_inc(sem("qk_spread"), 1)

            def scores(h):
                r, t = h % 2 * HD, h // 2
                pe.wait_ge(sem("qk_ready"), 8)
                if h >= 1:
                    pe.wait_ge(sem("st_zread"), h)
                for kb in range(QT):
                    b, c, w = regions(kb)
                    last = pe.matmul(att_bank[b][:, c:c + w], qk[r:r + HD, 4 + t, kb * P:(kb + 1) * P],
                                     qk[r:r + HD, t, kb * P:S], start=True, stop=True)
                last.then_inc(sem("st_z"), 1)

            def tails(h):
                pe.wait_ge(sem("st_soft"), h + 1)
                if h >= 1:
                    pe.wait_ge(sem("st_logw"), h)
                else:
                    pe.wait_ge(sem("bank_free"), 4 + LAYER["in_v"]["tile"] + 8)
                for kb in range(QT):
                    b, c, w = regions(kb)
                    for jb in range(kb, QT):
                        wj = S - jb * P
                        last = pe.matmul(lin_bank[b][:, c + w - wj:c + w], later_key[:, :] if jb == kb else ones[:, :],
                                         soft[h % 2][:, KOFF[jb]:KOFF[jb] + wj], start=(jb == kb), stop=(jb == QT - 1))
                last.then_inc(sem("st_tail"), 1)

            def values(h):
                r = h % 2 * HD
                pe.wait_ge(sem("st_wm"), h + 1)
                if h >= 2:
                    pe.wait_ge(sem("st_o"), h - 1)
                for kb in range(QT):
                    last = pe.matmul(lin_bank[3][r:r + HD, kb * P:S], vtok[:, kb, h * HD:(h + 1) * HD],
                                     wgt[h % 2][:, KOFF[kb]:KOFF[kb] + S - kb * P], start=(kb == 0), stop=(kb == QT - 1))
                last.then_inc(sem("st_pv"), 1)

            scores(0)
            for h in range(HEADS):
                if h + 1 < HEADS:
                    scores(h + 1)
                tails(h)
                values(h)
            pe.wait_ge(sem("conv"), len(CONV_OPS))
            pe.wait_ge(sem("st_zread"), HEADS)
            for k in range(CT):
                last = pe.matmul(att_bank[0][:, :], ones[:, :], cacc[:, k, :], start=(k == 0), stop=(k == CT - 1))
            last.then_inc(sem("ln_mean"), 1)
            for k in range(CT):
                pe.wait_ge(sem("ln_sq"), k + 1)
                last = pe.matmul(att_bank[1][:, :], ones[:, :], ln_sq[:, k, :], start=(k == 0), stop=(k == CT - 1))
            last.then_inc(sem("ln_var"), 1)
            pe.wait_ge(sem("mix1_lo"), KD)
            linear_pe(pe, "out1", weights_first("out1", xh, xl), S)
            norm_pe(pe, "n2", nrm2, S)
            norm_done(pe, "n2")
            done = 0
            for half in range(2):
                linear_pe(pe, f"up{half}", weights_first(f"up{half}", xh, xl), S)
                done += FHALF[half]
                pe.wait_ge(sem("ff_lo"), done)
                linear_pe(pe, f"down{half}", weights_first(f"down{half}", fh, fl), S)

        def add_to_resid(dve, name):
            for n in range(KD):
                bank = tile_ready(dve, name, n)
                dve.tensor_tensor(resid[:, n, :], bank[:, :], resid[:, n, :], ALU.add).then_inc(sem("bank_free"), 1)

        def block1_dve(dve, chain):
            wait(dve, ("params_loaded", 16), ("x_loaded", 16))
            chain.link(dve.tensor_scalar(qg[:, :], col("q_norm"), HD ** -0.5, None, ALU.mult))
            norm_dve(dve, chain, "n1", resid, nrm1, std1, rstd1, xh, xl, "norm1", S)
            for n in range(8):
                bank = tile_ready(dve, "in_fm", n)
                dve.tensor_copy(qk[:, n, :], bank[:, :]).then_inc(sem("bank_free"), 1)
            for j in range(CT):
                bank = tile_ready(dve, "in_fm", 8 + 2 * j)
                dve.wait_ge(sem("glu_sig"), j + 1)
                dve.tensor_tensor(cpad[:, j, TAPS - 1:], bank[:, :], glu_sig[j % 2][:, :], ALU.mult)\
                   .then_inc(sem("bank_free"), 2)
            for n in range(8):
                bank = tile_ready(dve, "in_v", n)
                dve.tensor_copy(vtok[:, n % QT, n // QT * 256:(n // QT + 1) * 256], bank[:, :256])\
                   .then_inc(sem("bank_free"), 1)
            dve.wait_ge(sem("qk_std"), 1)
            dve.reciprocal(rstd16[:, :], std16[:, :]).then_inc(sem("qk_rstd"), 1)
            for j in range(8):
                dve.wait_ge(sem("qk_spread"), j + 1)
                gain = qg[:, 0:1] if j < 4 else col("k_norm")
                dve.scalar_tensor_tensor(out=qk[:, j, :], in0=qk[:, j, :], scalar=gain, in1=att_bank[1 + j % 2][:, :],
                                         op0=ALU.mult, op1=ALU.mult).then_inc(sem("qk_ready"), 1)

            def diag(x, kb):
                return x[:, KOFF[kb]:KOFF[kb] + P]

            def softplus(h):
                dve.wait_ge(sem("st_ln"), h + 1)
                if h >= 2:
                    dve.wait_ge(sem("st_tail"), h - 1)
                for b, (off, w) in enumerate(PIECES):
                    ins = dve.scalar_tensor_tensor(out=soft[h % 2][:, off:off + w], in0=att_bank[b][:, :w], scalar=0.0,
                                                   in1=ln1[:, off:off + w], op0=ALU.max, op1=ALU.add)
                chain.link(ins)
                for kb in range(QT):
                    ins = dve.tensor_tensor(diag(soft[h % 2], kb), diag(soft[h % 2], kb), causal[:, :], ALU.mult)
                ins.then_inc(sem("st_soft"), 1)
                for b, (off, w) in enumerate(PIECES):
                    ins = dve.scalar_tensor_tensor(out=lbeta[h % 2][:, off:off + w], in0=att_bank[b][:, :w], scalar=0.0,
                                                   in1=ln1[:, off:off + w], op0=ALU.min, op1=ALU.subtract)
                ins.then_inc(sem("st_zread"), 1)

            softplus(0)
            per_head = -(-len(CONV_OPS) // HEADS)
            for h in range(HEADS):
                if h + 1 < HEADS:
                    softplus(h + 1)
                dve.wait_ge(sem("st_tail"), h + 1)
                dve.wait_ge(sem("st_zread"), h + 1)
                if h >= 2:
                    dve.wait_ge(sem("st_pv"), h - 1)
                for b, (off, w) in enumerate(PIECES):
                    ins = dve.tensor_tensor(wgt[h % 2][:, off:off + w], lbeta[h % 2][:, off:off + w],
                                            lin_bank[b][:, :w], ALU.subtract)
                ins.then_inc(sem("st_logw"), 1)
                conv_steps(dve, h * per_head, (h + 1) * per_head)
                dve.wait_ge(sem("st_w"), h + 1)
                for kb in range(QT):
                    ins = dve.tensor_tensor(diag(wgt[h % 2], kb), diag(wgt[h % 2], kb), causal[:, :], ALU.mult)
                ins.then_inc(sem("st_wm"), 1)
            dve.wait_ge(sem("conv"), len(CONV_OPS))
            dve.wait_ge(sem("ln_mean"), 1)
            for k in range(CT):
                dve.scalar_tensor_tensor(out=cacc[:, k, :], in0=att_bank[0][:, :], scalar=-1.0 / CW, in1=cacc[:, k, :],
                                         op0=ALU.mult, op1=ALU.add).then_inc(sem("ln_xc"), 1)
            dve.wait_ge(sem("ln_std"), 1)
            chain.link(dve.reciprocal(ln_rstd[:, :], ln_std[:, :]))
            for k in range(CT):
                dve.tensor_tensor(cacc[:, k, :], cacc[:, k, :], ln_rstd[:, :], ALU.mult).then_inc(sem("ln_y"), 1)
            for k in range(KD):
                src = attn[:, k, :] if k < CT else cacc[:, k - CT, :]
                dve.wait_ge(sem("mix1_hi"), k + 1)
                dve.tensor_tensor(xl[:, k, :], src, xh[:, k, :].bitcast(F32), ALU.subtract).then_inc(sem("mix1_lo"), 1)
            add_to_resid(dve, "out1")
            norm_dve(dve, chain, "n2", resid, nrm2, std2, rstd2, xh, xl, "norm2", S)
            j = 0
            for half in range(2):
                for b in range(FHALF[half]):
                    gate = tile_ready(dve, f"up{half}", 2 * b)
                    y = f_conv[j % 2]

                    def tap(k):
                        return col("ffn_w", j * FTAPS + k)
                    chain.link(dve.tensor_scalar(y[:, :], gate[:, :], tap(2), col("ffn_b", j), ALU.mult, ALU.add))
                    chain.link(dve.scalar_tensor_tensor(out=y[:, 1:], in0=gate[:, :S - 1], scalar=tap(1), in1=y[:, 1:],
                                                        op0=ALU.mult, op1=ALU.add))
                    dve.scalar_tensor_tensor(out=y[:, 2:], in0=gate[:, :S - 2], scalar=tap(0), in1=y[:, 2:],
                                             op0=ALU.mult, op1=ALU.add).then_inc(sem("ff_conv"), 1)
                    value = tile_ready(dve, f"up{half}", 2 * b + 1)
                    dve.wait_ge(sem("ff_silu"), j + 1)
                    if j >= 2:
                        dve.wait_ge(sem("ff_lo"), j - 1)
                    dve.tensor_tensor(f_out[j % 2][:, :], value[:, :], f_silu[j % 2][:, :], ALU.mult)\
                       .then_inc(sem("bank_free"), 2)
                    j += 1
                add_to_resid(dve, f"down{half}")

        N_CONST = 21

        def make_consts(pool):
            done = [0]

            def step(ins):
                done[0] += 1
                ins.then_inc(sem("consts"), 1)
                pool.wait_ge(sem("consts"), done[0])

            pool.nop().then_inc(sem("bank_free"), 4)
            pool.nop().then_inc(sem("lo_done"), 2)
            peer_credits(pool)
            step(pool.memset(eps[:, :], EPS))
            step(pool.memset(ones[:, :], 1.0))
            step(pool.memset(head_sum[:, :, :], 0.0))
            step(pool.memset(head_spread[:, :], 1.0))
            step(pool.memset(cpad[:, :, 0:TAPS - 1], 0.0))
            step(pool.memset(cmp_valid[:, :, :], 1.0))
            step(pool.iota(iota16[:, :], [[1, PK]], base=0, channel_multiplier=0, allow_small_or_imprecise_dtypes=True))
            step(pool.iota(iota_key[:, :], [[1, NK]], base=0, channel_multiplier=0,
                           allow_small_or_imprecise_dtypes=True))
            step(pool.iota(dist[:, :], [[1, S]], base=P - S, channel_multiplier=-1,
                           allow_small_or_imprecise_dtypes=True))
            step(pool.iota(cmp_dist[:, :, :], [[-P, QT], [CMP, NCMP]], base=CMP - 1, channel_multiplier=-1,
                           allow_small_or_imprecise_dtypes=True))
            step(pool.memset(ident[:, :], 0.0))
            step(pool.affine_select(out=ident[:, :], in_=ident[:, :], compare_op=ALU.not_equal, fill=1.0, base=0,
                                    pattern=[[-1, P]], channel_multiplier=1))
            step(pool.affine_select(out=later_key[:, :], in_=ones[:, :], compare_op=ALU.is_gt, fill=0.0, base=0,
                                    pattern=[[-1, P]], channel_multiplier=1))
            step(pool.affine_select(out=causal[:, :], in_=ones[:, :], compare_op=ALU.is_gt, fill=0.0, base=0,
                                    pattern=[[1, P]], channel_multiplier=-1))
            step(pool.affine_select(out=dist[:, :], in_=dist[:, :], compare_op=ALU.is_ge, fill=NEG, base=S - P,
                                    pattern=[[-1, S]], channel_multiplier=1))
            step(pool.affine_select(out=cmp_dist[:, :, :], in_=cmp_dist[:, :, :], compare_op=ALU.is_ge, fill=NEG,
                                    base=1 - CMP, pattern=[[P, QT], [-CMP, NCMP]], channel_multiplier=1))
            step(pool.affine_select(out=cmp_valid[:, :, :], in_=cmp_valid[:, :, :], compare_op=ALU.is_ge, fill=0.0,
                                    base=1 - CMP, pattern=[[P, QT], [-CMP, NCMP]], channel_multiplier=1))
            sums = head_sum[:, :, :].rearrange("p j c -> p (j c)")
            step(pool.memset(sums[0:HD, 0:P:18], 1.0))
            step(pool.memset(sums[HD:P, 1:P:18], 1.0))
            step(pool.affine_select(out=head_spread[:, :], in_=head_spread[:, :], compare_op=ALU.is_ge, fill=0.0, base=0,
                                    pattern=[[1, 8 * P]], channel_multiplier=-HD))
            step(pool.affine_select(out=head_spread[:, :], in_=head_spread[:, :], compare_op=ALU.is_ge, fill=0.0,
                                    base=HD - 1, pattern=[[-1, 8 * P]], channel_multiplier=HD))
            assert done[0] == N_CONST

        def scr(kb):
            return SCR + int(kb * KB)

        qa = at("qa", [P, DA_H, S], scr(0))
        ka = at("ka", [P, DA_H, S], scr(8))
        qb = at("qb", [P, NSA_H // 2, S], scr(16))
        ks = [at(f"ks{i}", [P, S], scr(24 + 2 * i)) for i in range(2)]
        kw = [at(f"kw{i}", [P, S], scr(28 + 2 * i)) for i in range(2)]
        va = at("va", [P, QT, AW], scr(32))
        vsw = at("vsw", [P, QT, 256], scr(40))
        cmp_in = [at(f"cmp_in{i}", [P, CMP // 2, NSA_G, NCMP], scr(44 + 2 * i)) for i in range(2)]
        slope_dist = [at(f"slope_dist{i}", [P, S], scr(44 + 2 * i)) for i in range(2)]
        cmp_hid = [at(f"cmp_hid{i}", [P, 2, NSA_G * NCMP], scr(48 + 0.25 * i)) for i in range(2)]
        kc_t = at("kc_t", [P, NSA_G * NCMP], scr(48.5))
        cmp_stat = at("cmp_stat", [P, QT, NSA_H], scr(48.75))
        cmp_rec = at("cmp_rec", [P, QT, NSA_H], scr(48.875))
        vc_blk = at("vc_blk", [P, NSA_H, HD], scr(49))
        cmp_bias = at("cmp_bias", [P, QT, NSA_H, NCMP], scr(51))
        cmp_s = at("cmp_s", [P, QT, NSA_H, NCMP], scr(53))
        cmp_p = at("cmp_p", [P, QT, NSA_H, 32], scr(55))
        cmp_pt = at("cmp_pt", [P, QT, NSA_G, P], scr(51))
        cmp_w1 = [at(f"cmp_w1_{i}", [P, CMP // 2, CMP_HID], scr(60 + 16 * i)) for i in range(2)]
        cmp_w2 = [at(f"cmp_w2_{i}", [P, 2, HD], scr(92 + 0.5 * i)) for i in range(2)]
        att_e = [at(f"att_e{i}", [P, 2, S], scr(60 + 4 * i)) for i in range(3)]
        att_pt = [at(f"att_pt{i}", [P, 2, S], scr(72 + 4 * i)) for i in range(2)]
        oab = at("oab", [P, KD, S], scr(80))
        stat = at("att_stat", [P, 3, 4, 2], scr(96))
        sub_sq = at("sub_sq", [P, DA_H, S], scr(60))
        sub_std = at("sub_std", [P, DA_H, S], scr(68))
        sig = at("sig", [P, 2 * KD, S], scr(0))
        mh = at("mh", [P, KD, S], scr(32), F32R)
        ml = at("ml", [P, KD, S], scr(48), F32R)
        part_a = [at(f"part_a{i}", [P, S], scr(64 + 2 * i)) for i in range(2)]
        part_b = [at(f"part_b{i}", [P, S], scr(68 + 2 * i)) for i in range(2)]
        mem = at("mem", [P, KD, MEM], scr(0))
        mem_n = at("mem_n", [P, KD, MEM], scr(8))
        mem_std = at("mem_std", [P, MEM], scr(16))
        mem_rstd = at("mem_rstd", [P, MEM], scr(17))
        mem_h = at("mem_h", [P, KD, MEM], scr(18), F32R)
        mem_l = at("mem_l", [P, KD, MEM], scr(26), F32R)
        cq = at("cq", [P, CA_H, S], scr(34))
        ck = at("ck", [P, CA_H, MEM], scr(42))
        cv = at("cv", [P, MEM // P, CA_H * P], scr(46))
        ca_e = [at(f"ca_e{i}", [P, MEM], scr(50 + i)) for i in range(3)]
        ca_pt = [at(f"ca_pt{i}", [P, MEM], scr(53 + i)) for i in range(2)]
        ca_stat = at("ca_stat", [P, 3, 4], scr(55))

        CA_SCALE = (CA_H * P // CA_H) ** -0.5
        MIXED = LAYER["mix_tm"]["tile"] + 16

        UNITS = [("a", h, i) for h in range(DA_H) for i in range(QT)] + [("b", h, i) for h in range(NSA_H) for i in range(QT)]
        N_A = DA_H * QT
        NU = len(UNITS)

        def items(u):
            return [u] if u < N_A else [N_A + 2 * (u - N_A), N_A + 2 * (u - N_A) + 1]

        def head_no(u):
            return u // QT

        def unit_maps(u):
            kind, h, i = UNITS[u]
            if kind == "a":
                return [(qa[c * HD:(c + 1) * HD, h, i * P:(i + 1) * P], ka[c * HD:(c + 1) * HD, h, :]) for c in range(2)]
            r = h % 2 * HD
            swap = 0 if h // NSA_R == h % 2 else 1
            q = qb[r:r + HD, h // 2, i * P:(i + 1) * P]
            return [(q, ks[swap][r:r + HD, :]), (q, kw[swap][r:r + HD, :])]

        def slope(u):
            kind, h, _ = UNITS[u]
            return 2.0 ** (-8.0 * (h + 1) / (DA_H if kind == "a" else NSA_H))

        def block2_pool(pool):
            for b in range(LAYER["mix_fm"]["block"] + 2, LAYER["peer_q"]["block"] + 2):
                if b == LAYER["mix_fm"]["block"] + 2:
                    norm_done(pool, "n3")
                    pool.memset(vc_blk[:, :, :], 0.0).then_inc(sem("cmp_zero"), 1)
                    pool.memset(cmp_p[:, :, :, :], 0.0).then_inc(sem("cmp_zero"), 1)
                split_lo(pool, b)

        def block2_act(act):
            def splits(name, first=0, last=None):
                t = LAYER[name]
                for b in range(first, t["nb"] if last is None else last):
                    split_hi(act, t["block"] + b + 2)

            norm_act(act, "n3", resid, nrm2, std2, xh, S, [("bank_free", 4 + LAYER["mix_fm"]["tile"])])
            splits("mix_fm")
            splits("mix_tm", 0, 3)
            act.wait_ge(sem("bank_free"), 4 + LAYER["mix_tm"]["tile"] + 3 * QT)
            for n in range(QT):
                bank = tile_ready(act, "mix_tm", 3 * QT + n)
                act.activation(gates24[:, n, :], bank[:, :NSA_H * 3], ACT.Sigmoid).then_inc(sem("bank_free"), 1)
            splits("mix_tm", 3)
            act.wait_ge(sem("lam_sum"), 1)
            act.activation(lam_exp[:, :], att_bank[3][:, 0:2], ACT.Exp).then_inc(sem("lam_exp"), 1)
            for v in range(2):
                act.wait_ge(sem("cmp_h"), v + 1)
                act.activation(cmp_hid[v][:, :, :].rearrange("p m n -> p (m n)"), att_bank[v][:, 0:2 * NSA_G * NCMP],
                               ACT.Gelu).then_inc(sem("cmp_hid"), 1)
            act.wait_ge(sem("cmp_sub"), 1)
            act.activation(cmp_s[:, :, :, :], cmp_s[:, :, :, :], ACT.Exp).then_inc(sem("cmp_exp"), 1)

            def exps(u):
                w = (UNITS[u][2] + 1) * P
                act.wait_ge(sem("at_nm"), u + 1)
                for c in range(2):
                    e = att_e[u % 3][:, c, :w]
                    act.activation(e, e, ACT.Exp, bias=stat[:, u % 3, 1, c:c + 1],
                                   accum_out=stat[:, u % 3, 2, c:c + 1]).then_inc(sem("at_exp"), 1)

            def transposed(u):
                w = (UNITS[u][2] + 1) * P
                if u >= 2:
                    act.wait_ge(sem("at_pv"), u - 1)
                for c, n in enumerate(items(u)):
                    act.wait_ge(sem("at_t"), n + 1)
                    act.activation(att_pt[u % 2][:, c, :w], lin_bank[n % 2][:, :w], ACT.Copy).then_inc(sem("at_pt"), 1)

            def outputs(u):
                kind, h, i = UNITS[u]
                if i < QT - 1:
                    return
                act.wait_ge(sem("at_pv"), u + 1)
                bank = lin_bank[2 + head_no(u) % 2]
                if kind == "a":
                    ins = act.activation(oab[:, h, :], bank[:, :], ACT.Copy)
                else:
                    r = h % 2 * HD
                    ins = act.activation(oab[r:r + HD, DA_H + h // 2, :], bank[r:r + HD, :], ACT.Copy)
                ins.then_inc(sem("at_o"), 1)

            for s in range(NU + 2):
                if s < NU:
                    exps(s)
                if 1 <= s <= NU:
                    transposed(s - 1)
                if s >= 2:
                    outputs(s - 2)
            for h in range(DA_H):
                act.activation(sub_sq[:, h, :], oab[:, h, :], ACT.Square).then_inc(sem("sub_sq"), 1)
            for h in range(DA_H):
                act.wait_ge(sem("sub_sum"), h + 1)
                act.activation(sub_std[:, h, :], att_bank[h][:, :], ACT.Sqrt, bias=eps[:, 0:1], scale=1.0 / P)\
                   .then_inc(sem("sub_std"), 1)
            for b in range(8):
                for n in range(2):
                    bank = tile_ready(act, "gates", 2 * b + n)
                    act.activation(sig[:, 2 * b + n, :], bank[:, :], ACT.Sigmoid).then_inc(sem("bank_free"), 1)
                split_hi(act, LAYER["gates"]["block"] + b + 2)
            for k in range(KD):
                if k < DA_H:
                    act.wait_ge(sem("sub_y"), k + 1)
                act.activation(xh[:, k, :], oab[:, k, :], ACT.Copy).then_inc(sem("oab_hi"), 1)
            for m in range(KD):
                act.wait_ge(sem("br_sum"), m + 1)
                act.activation(mh[:, m, :], part_a[m % 2][:, :], ACT.Copy).then_inc(sem("br_hi"), 1)
                if m % 2:
                    split_hi(act, LAYER["branch"]["block"] + m // 2 + 2)
            splits("out2")
            norm_act(act, "nm", mem, mem_n, mem_std, mem_h, MEM, [("mem_loaded", 16)])
            norm_act(act, "n4", resid, nrm2, std2, xh, S, [("bank_free", 4 + LAYER["out2"]["tile"] + KD)])
            for name in ("cross_q", "cross_k", "cross_v"):
                splits(name)

            def ca_exp(u):
                act.wait_ge(sem("ca_nm"), u + 1)
                act.activation(ca_e[u % 3][:, :], att_bank[u % 4][:, :MEM], ACT.Exp, bias=ca_stat[:, u % 3, 1:2],
                               scale=CA_SCALE, accum_out=ca_stat[:, u % 3, 2:3]).then_inc(sem("ca_exp"), 1)

            def ca_transposed(u):
                if u >= 2:
                    act.wait_ge(sem("ca_pv"), u - 1)
                act.wait_ge(sem("ca_t"), u + 1)
                act.activation(ca_pt[u % 2][:, :], lin_bank[u % 2][:, :MEM], ACT.Copy).then_inc(sem("ca_pt"), 1)

            for s in range(CA_H * QT + 2):
                if s < CA_H * QT:
                    ca_exp(s)
                if 1 <= s <= CA_H * QT:
                    ca_transposed(s - 1)
                u = s - 2
                if u >= 0 and u % QT == QT - 1:
                    h = u // QT
                    act.wait_ge(sem("ca_pv"), u + 1)
                    act.activation(xh[:, h, :], lin_bank[2 + h % 2][:, :], ACT.Copy).then_inc(sem("ca_hi"), 1)
            splits("cross_o")

        def block2_pe(pe):
            norm_pe(pe, "n3", nrm2, S)
            pe.wait_ge(sem("lam_prod"), 1)
            pe.matmul(att_bank[3][:, 0:2], ones[0:HD, :], lam_prod[0:HD, :], start=True, stop=True)\
              .then_inc(sem("lam_sum"), 1)
            norm_done(pe, "n3")
            linear_pe(pe, "mix_fm", weights_first("mix_fm", xh, xl), S)
            linear_pe(pe, "mix_tm", tokens_first("mix_tm", xh, xl), 256)
            wait(pe, ("cmp_loaded", 64), ("cmp_in", 8))
            NC2 = NSA_G * NCMP
            for v in range(2):
                for m in range(2):
                    for lp in range(CMP // 2):
                        last = pe.matmul(att_bank[v][:, m * NC2:(m + 1) * NC2], cmp_w1[v][:, lp, m * P:(m + 1) * P],
                                         cmp_in[v][:, lp, :, :].rearrange("p g b -> p (g b)"),
                                         start=(lp == 0), stop=(lp == CMP // 2 - 1))
                last.then_inc(sem("cmp_h"), 1)
            pe.wait_ge(sem("cmp_hid"), 1)
            for m in range(2):
                last = pe.matmul(att_bank[2][0:HD, 0:NC2], cmp_w2[0][:, m, :], cmp_hid[0][:, m, :],
                                 start=(m == 0), stop=(m == 1))
            last.then_inc(sem("cmp_k"), 1)
            pe.wait_ge(sem("cmp_hid"), 2)
            pe.wait_ge(sem("lam_exp"), 1)
            for g in range(NSA_G):
                for m in range(2):
                    last = pe.matmul(att_bank[3][0:NCMP, g * HD:(g + 1) * HD], cmp_hid[1][:, m, g * NCMP:(g + 1) * NCMP],
                                     cmp_w2[1][:, m, :], start=(m == 0), stop=(m == 1))
            last.then_inc(sem("cmp_v"), 1)
            pe.wait_ge(sem("cmp_kc"), 2)
            for i in range(QT):
                for h in range(NSA_H):
                    r, g = h % 2 * HD, h // NSA_R
                    n = (i * NSA_H // 2 + h // 2) * NCMP
                    last = pe.matmul(att_bank[h % 2][:, n:n + NCMP], qb[r:r + HD, h // 2, i * P:(i + 1) * P],
                                     kc_t[r:r + HD, g * NCMP:(g + 1) * NCMP], start=True, stop=True)
            last.then_inc(sem("cmp_scores"), 1)
            pe.wait_ge(sem("cmp_p"), 1)
            for i in range(QT):
                for g in range(NSA_G):
                    n = i * NSA_G + g
                    src = cmp_p[:, i, g * NSA_R:(g + 1) * NSA_R, :].rearrange("p h c -> p (h c)")
                    last = pe.transpose(att_bank[1 + n // 4][:, n % 4 * P:(n % 4 + 1) * P], src, ident[:, :])
            last.then_inc(sem("cmp_t"), 1)

            def scores(u):
                w = (UNITS[u][2] + 1) * P
                for c, (q, k) in enumerate(unit_maps(u)):
                    if u >= 2:
                        pe.wait_ge(sem("at_max"), 2 * (u - 2) + c + 1)
                    pe.matmul(att_bank[2 * (u % 2) + c][:, :w], q, k[:, :w], start=True, stop=True)\
                      .then_inc(sem("at_s"), 1)

            def transposes(u):
                for c, n in enumerate(items(u)):
                    pe.wait_ge(sem("at_p"), n + 1)
                    if n >= 2:
                        pe.wait_ge(sem("at_pt"), n - 1)
                    for kb in range(UNITS[u][2] + 1):
                        last = pe.transpose(lin_bank[n % 2][:, kb * P:(kb + 1) * P],
                                            att_e[u % 3][:, c, kb * P:(kb + 1) * P], ident[:, :])
                    last.then_inc(sem("at_t"), 1)

            def values(u):
                kind, h, i = UNITS[u]
                pe.wait_ge(sem("at_pt"), items(u)[-1] + 1)
                if i == 0 and head_no(u) >= 2:
                    pe.wait_ge(sem("at_o"), head_no(u) - 1)
                bank = lin_bank[2 + head_no(u) % 2]
                if kind == "a":
                    out = bank[:, i * P:(i + 1) * P]
                    ops = [(va[:, kb, h * P:(h + 1) * P], att_pt[u % 2][:, 0, kb * P:(kb + 1) * P]) for kb in range(i + 1)]
                else:
                    r, g = h % 2 * HD, h // NSA_R
                    out = bank[r:r + HD, i * P:(i + 1) * P]
                    ops = [(vc_blk[:, h, :], cmp_pt[:, i, g, :])]
                    ops += [(vsw[:, kb, c * P + g * HD:c * P + (g + 1) * HD], att_pt[u % 2][:, c, kb * P:(kb + 1) * P])
                            for c in range(2) for kb in range(i + 1)]
                for n, (v, p) in enumerate(ops):
                    last = pe.matmul(out, v, p, start=(n == 0), stop=(n == len(ops) - 1))
                last.then_inc(sem("at_pv"), 1)

            wait(pe, ("bank_free", 4 + MIXED), ("cmp_pt", 2))
            for s in range(NU + 2):
                if s < NU:
                    scores(s)
                if 1 <= s <= NU:
                    transposes(s - 1)
                if s >= 2:
                    values(s - 2)
            pe.wait_ge(sem("at_max"), 2 * NU)
            for h in range(DA_H):
                pe.wait_ge(sem("sub_sq"), h + 1)
                pe.matmul(att_bank[h][:, :], ones[:, :], sub_sq[:, h, :], start=True, stop=True)\
                  .then_inc(sem("sub_sum"), 1)
            pe.wait_ge(sem("at_o"), DA_H + NSA_H)
            linear_pe(pe, "gates", weights_first("gates", xh, xl), S)
            pe.wait_ge(sem("oab_lo"), KD)

            def branch_pairs(slot, m):
                half, out = m % 2, m // 2
                ks_ = range(4 * half, 4 * half + 4)
                return [(wh[slot][:, k * 256 + out * P:k * 256 + out * P + P],
                         wl[slot][:, k * 256 + out * P:k * 256 + out * P + P], xh[:, k, :], xl[:, k, :]) for k in ks_]

            linear_pe(pe, "branch", branch_pairs, S)
            pe.wait_ge(sem("br_lo"), KD)
            linear_pe(pe, "out2", weights_first("out2", mh, ml), S)
            norm_pe(pe, "nm", mem_n, MEM)
            pe.wait_ge(sem("norm_std"), before("nm", 1) + 1)
            norm_pe(pe, "n4", nrm2, S)
            norm_done(pe, "n4")
            linear_pe(pe, "cross_q", weights_first("cross_q", xh, xl), S)
            norm_done(pe, "nm")
            linear_pe(pe, "cross_k", weights_first("cross_k", mem_h, mem_l, MEM), MEM)
            linear_pe(pe, "cross_v", tokens_first("cross_v", mem_h, mem_l), 256)
            pe.wait_ge(sem("bank_free"), 4 + LAYER["cross_o"]["tile"])
            n_ca = CA_H * QT
            for s in range(n_ca + 2):
                if s < n_ca:
                    h, i = s // QT, s % QT
                    if s >= 4:
                        pe.wait_ge(sem("ca_exp"), s - 3)
                    pe.matmul(att_bank[s % 4][:, :MEM], cq[:, h, i * P:(i + 1) * P], ck[:, h, :], start=True, stop=True)\
                      .then_inc(sem("ca_s"), 1)
                u = s - 1
                if 0 <= u < n_ca:
                    pe.wait_ge(sem("ca_p"), u + 1)
                    if u >= 2:
                        pe.wait_ge(sem("ca_pt"), u - 1)
                    for mt in range(MEM // P):
                        last = pe.transpose(lin_bank[u % 2][:, mt * P:(mt + 1) * P], ca_e[u % 3][:, mt * P:(mt + 1) * P],
                                            ident[:, :])
                    last.then_inc(sem("ca_t"), 1)
                u = s - 2
                if u >= 0:
                    h, i = u // QT, u % QT
                    pe.wait_ge(sem("ca_pt"), u + 1)
                    if i == 0 and h >= 2:
                        pe.wait_ge(sem("ca_lo"), h - 1)
                    for mt in range(MEM // P):
                        last = pe.matmul(lin_bank[2 + h % 2][:, i * P:(i + 1) * P], cv[:, mt, h * P:(h + 1) * P],
                                         ca_pt[u % 2][:, mt * P:(mt + 1) * P], start=(mt == 0), stop=(mt == 1))
                    last.then_inc(sem("ca_pv"), 1)
            pe.wait_ge(sem("ca_lo"), CA_H)
            linear_pe(pe, "cross_o", weights_first("cross_o", xh, xl), S)

        def block2_dve(dve, chain):
            p0 = PCOL["lam"]
            dve.tensor_tensor(lam_prod[:, :], params[:, p0:p0 + 4:2], params[:, p0 + 1:p0 + 4:2], ALU.mult)\
               .then_inc(sem("lam_prod"), 1)
            chain.link(dve.tensor_scalar(subln_g[:, :], col("subln"), 1.0 - LAMBDA_INIT, None, ALU.mult))
            norm_dve(dve, chain, "n3", resid, nrm2, std2, rstd2, xh, xl, "norm_mix", S)
            scale = HD ** -0.5
            for n in range(12):
                bank = tile_ready(dve, "mix_fm", n)
                out = (qa, ka, qb)[n // 4][:, n % 4, :]
                if n // 4 == 1:
                    ins = dve.tensor_copy(out, bank[:, :])
                else:
                    ins = dve.tensor_scalar(out, bank[:, :], scale, None, ALU.mult)
                ins.then_inc(sem("bank_free"), 1)
            for v in range(2):
                bank = tile_ready(dve, "mix_fm", 12 + v)
                for g in range(NSA_G):
                    rows = slice(g * HD, (g + 1) * HD)
                    tokens = bank[rows, :].rearrange("p (b l) -> p l b", l=CMP)
                    pos = params[rows, PCOL["cmp_pos"]:PCOL["cmp_pos"] + CMP]
                    for par in range(2):
                        dve.tensor_tensor(
                            cmp_in[v][par * HD:(par + 1) * HD, :, g, :], tokens[:, par::2, :],
                            pos[:, par::2].unsqueeze(2).to_broadcast([HD, CMP // 2, NCMP]), ALU.add)\
                           .then_inc(sem("cmp_in"), 1)
                dve.wait_ge(sem("cmp_in"), 4 * (v + 1))
                dve.sem_inc(sem("bank_free"), 1)
            for n, x in ((14, ks), (15, kw)):
                bank = tile_ready(dve, "mix_fm", n)
                dve.tensor_copy(x[0][:, :], bank[:, :])
                dve.tensor_copy(x[1][0:HD, :], bank[HD:P, :])
                dve.tensor_copy(x[1][HD:P, :], bank[0:HD, :]).then_inc(sem("bank_free"), 1)
            for n in range(3 * QT):
                bank = tile_ready(dve, "mix_tm", n)
                b, tt = n // QT, n % QT
                out = va[:, tt, b * 256:(b + 1) * 256] if b < 2 else vsw[:, tt, :]
                dve.tensor_copy(out, bank[:, :256]).then_inc(sem("bank_free"), 1)
            for h in range(NSA_H):
                dve.tensor_scalar(cmp_bias[:, :, h, :], cmp_dist[:, :, :], 2.0 ** -(h + 1), None, ALU.mult)
            dve.wait_ge(sem("lam_exp"), 1)
            chain.link(dve.tensor_scalar(lam[:, :], lam_exp[:, 0:1], lam_exp[:, 1:2], LAMBDA_INIT, ALU.subtract, ALU.add))
            dve.wait_ge(sem("cmp_k"), 1)
            for half in range(2):
                dve.tensor_copy(kc_t[half * HD:(half + 1) * HD, :], att_bank[2][0:HD, 0:NSA_G * NCMP])\
                   .then_inc(sem("cmp_kc"), 1)
            wait(dve, ("cmp_v", 1), ("cmp_zero", 2))
            for h in range(NSA_H):
                g, r = h // NSA_R, h % NSA_R
                ins = dve.tensor_copy(vc_blk[32 * r:32 * r + NCMP, h, :], att_bank[3][0:NCMP, g * HD:(g + 1) * HD])
            chain.link(ins)
            dve.wait_ge(sem("cmp_scores"), 1)
            flat = "p i h c -> p (i h) c"
            s3, b3 = cmp_s[:, :, :, :].rearrange(flat), cmp_bias[:, :, :, :].rearrange(flat)
            stat2, rec2 = cmp_stat[:, :, :].rearrange("p i h -> p (i h)"), cmp_rec[:, :, :].rearrange("p i h -> p (i h)")
            NIH = QT * NSA_H

            def spread(x):
                return x.unsqueeze(2).to_broadcast([P, NIH, NCMP])

            for odd in range(2):
                by_parity = "p i (h o) c -> p o (i h) c"
                ins = dve.tensor_tensor(cmp_s[:, :, :, :].rearrange(by_parity, o=2)[:, odd],
                                        att_bank[odd][:, :S // 2].rearrange("p (n c) -> p n c", c=NCMP),
                                        cmp_bias[:, :, :, :].rearrange(by_parity, o=2)[:, odd], ALU.add)
            chain.link(ins)
            chain.link(dve.tensor_reduce(stat2, s3, AX_X, ALU.max))
            dve.tensor_tensor(s3, s3, spread(stat2), ALU.subtract).then_inc(sem("cmp_sub"), 1)
            dve.wait_ge(sem("cmp_exp"), 1)
            chain.link(dve.tensor_reduce(stat2, s3, AX_X, ALU.add))
            chain.link(dve.reciprocal(rec2, stat2))
            chain.link(dve.tensor_tensor(cmp_rec[:, :, :], cmp_rec[:, :, :], gates24[:, :, 0::3], ALU.mult))
            for i in range(QT):
                ins = dve.tensor_tensor(cmp_s[:, i, :, :], cmp_s[:, i, :, :],
                                        cmp_valid[:, i, :].unsqueeze(1).to_broadcast([P, NSA_H, NCMP]), ALU.mult)
            chain.link(ins)
            padded = cmp_p[:, :, :, :].rearrange(flat)
            dve.tensor_tensor(padded[:, :, 0:NCMP], s3, spread(rec2), ALU.mult).then_inc(sem("cmp_p"), 1)
            dve.wait_ge(sem("cmp_t"), 1)
            turned = cmp_pt[:, :, :, :].rearrange("p i g t -> p (i g t)")
            for b in range(2):
                dve.tensor_copy(turned[:, b * S:(b + 1) * S], att_bank[1 + b][:, :]).then_inc(sem("cmp_pt"), 1)

            def maxima(u):
                kind, h, i = UNITS[u]
                w = (i + 1) * P
                sd = slope_dist[head_no(u) % 2]
                if i == 0:
                    chain.link(dve.tensor_scalar(sd[:, :], dist[:, :], slope(u), None, ALU.mult))
                if u >= 3:
                    dve.wait_ge(sem("at_t"), items(u - 3)[-1] + 1)
                for c in range(2):
                    dve.wait_ge(sem("at_s"), 2 * u + c + 1)
                    dve.tensor_tensor_reduce(out=att_e[u % 3][:, c, :w], in0=att_bank[2 * (u % 2) + c][:, :w],
                                             in1=sd[:, S - w:], scale=1.0, scalar=-3.0e38, op0=ALU.add, op1=ALU.max,
                                             accum_out=stat[:, u % 3, 0, c:c + 1]).then_inc(sem("at_max"), 1)
                dve.wait_ge(sem("at_max"), 2 * u + 2)
                dve.tensor_scalar(stat[:, u % 3, 1, :], stat[:, u % 3, 0, :], -1.0, None, ALU.mult).then_inc(sem("at_nm"), 1)

            def weights(u):
                kind, h, i = UNITS[u]
                w = (i + 1) * P
                e, factor = att_e[u % 3], stat[:, u % 3, 3, :]
                dve.wait_ge(sem("at_exp"), 2 * u + 2)
                chain.link(dve.reciprocal(factor, stat[:, u % 3, 2, :]))
                if kind == "a":
                    chain.link(dve.tensor_scalar(factor[:, 1:2], factor[:, 1:2], lam[:, 0:1], None, ALU.mult))
                    chain.link(dve.tensor_scalar(e[:, 1, :w], e[:, 1, :w], factor[:, 1:2], None, ALU.mult))
                    dve.scalar_tensor_tensor(out=e[:, 0, :w], in0=e[:, 0, :w], scalar=factor[:, 0:1], in1=e[:, 1, :w],
                                             op0=ALU.mult, op1=ALU.subtract).then_inc(sem("at_p"), 1)
                else:
                    chain.link(dve.tensor_tensor(factor, factor, gates24[:, i, 3 * h + 1:3 * h + 3], ALU.mult))
                    for c in range(2):
                        dve.tensor_scalar(e[:, c, :w], e[:, c, :w], factor[:, c:c + 1], None, ALU.mult)\
                           .then_inc(sem("at_p"), 1)

            for s in range(NU + 1):
                if s < NU:
                    maxima(s)
                if s >= 1:
                    weights(s - 1)
            for h in range(DA_H):
                dve.wait_ge(sem("sub_std"), h + 1)
                chain.link(dve.reciprocal(sub_std[:, h, :], sub_std[:, h, :]))
                dve.scalar_tensor_tensor(out=oab[:, h, :], in0=oab[:, h, :], scalar=subln_g[:, 0:1],
                                         in1=sub_std[:, h, :], op0=ALU.mult, op1=ALU.mult).then_inc(sem("sub_y"), 1)
            for k in range(KD):
                dve.wait_ge(sem("oab_hi"), k + 1)
                dve.tensor_tensor(xl[:, k, :], oab[:, k, :], xh[:, k, :].bitcast(F32), ALU.subtract)\
                   .then_inc(sem("oab_lo"), 1)
            for m in range(KD):
                a = tile_ready(dve, "branch", 2 * m)
                b = tile_ready(dve, "branch", 2 * m + 1)
                if m >= 2:
                    dve.wait_ge(sem("br_hi"), m - 1)
                dve.tensor_tensor(part_a[m % 2][:, :], a[:, :], sig[:, 2 * m, :], ALU.mult)
                dve.tensor_tensor(part_b[m % 2][:, :], b[:, :], sig[:, 2 * m + 1, :], ALU.mult)\
                   .then_inc(sem("bank_free"), 2)
                dve.wait_ge(sem("bank_free"), 4 + LAYER["branch"]["tile"] + 2 * (m + 1))
                dve.tensor_tensor(part_a[m % 2][:, :], part_a[m % 2][:, :], part_b[m % 2][:, :], ALU.add)\
                   .then_inc(sem("br_sum"), 1)
                dve.wait_ge(sem("br_hi"), m + 1)
                dve.tensor_tensor(ml[:, m, :], part_a[m % 2][:, :], mh[:, m, :].bitcast(F32), ALU.subtract)\
                   .then_inc(sem("br_lo"), 1)
            add_to_resid(dve, "out2")
            norm_dve(dve, chain, "nm", mem, mem_n, mem_std, mem_rstd, mem_h, mem_l, "norm_mem", MEM)
            norm_dve(dve, chain, "n4", resid, nrm2, std2, rstd2, xh, xl, "norm_cross", S)
            for n in range(CA_H):
                bank = tile_ready(dve, "cross_q", n)
                dve.tensor_copy(cq[:, n, :], bank[:, :]).then_inc(sem("bank_free"), 1)
            for n in range(CA_H):
                bank = tile_ready(dve, "cross_k", n)
                dve.tensor_copy(ck[:, n, :], bank[:, :MEM]).then_inc(sem("bank_free"), 1)
            for n in range(4):
                bank = tile_ready(dve, "cross_v", n)
                dve.tensor_copy(cv[:, n % 2, n // 2 * 256:(n // 2 + 1) * 256], bank[:, :256]).then_inc(sem("bank_free"), 1)
            n_ca = CA_H * QT
            for s in range(n_ca + 3):
                if s < n_ca:
                    dve.wait_ge(sem("ca_s"), s + 1)
                    chain.link(dve.tensor_reduce(ca_stat[:, s % 3, 0:1], att_bank[s % 4][:, :MEM], AX_X, ALU.max))
                    if s >= 3:
                        dve.wait_ge(sem("ca_t"), s - 2)
                    dve.tensor_scalar(ca_stat[:, s % 3, 1:2], ca_stat[:, s % 3, 0:1], -CA_SCALE, None, ALU.mult)\
                       .then_inc(sem("ca_nm"), 1)
                u = s - 1
                if 0 <= u < n_ca:
                    dve.wait_ge(sem("ca_exp"), u + 1)
                    chain.link(dve.reciprocal(ca_stat[:, u % 3, 3:4], ca_stat[:, u % 3, 2:3]))
                    dve.tensor_scalar(ca_e[u % 3][:, :], ca_e[u % 3][:, :], ca_stat[:, u % 3, 3:4], None, ALU.mult)\
                       .then_inc(sem("ca_p"), 1)
                u = s - 3
                if u >= 0 and u % QT == QT - 1:
                    h = u // QT
                    dve.wait_ge(sem("ca_hi"), h + 1)
                    dve.tensor_tensor(xl[:, h, :], lin_bank[2 + h % 2][:, :], xh[:, h, :].bitcast(F32), ALU.subtract)\
                       .then_inc(sem("ca_lo"), 1)
            add_to_resid(dve, "cross_o")

        def block12_loads(sp, last=NB):
            first = LAYER["mix_fm"]["block"] + 2
            load_blocks(sp, 0, first)
            norm_done(sp, "n3")
            for v in range(2):
                sp.dma_start(cmp_w1[v][:, :, :], io["cmp_w1"][v]).then_inc(sem("cmp_loaded"), 16)
                sp.dma_start(cmp_w2[v][:, :, :], io["cmp_w2"][v]).then_inc(sem("cmp_loaded"), 16)
            load_blocks(sp, first, LAYER["out2"]["block"] + 2)
            sp.wait_ge(sem("br_lo"), KD)
            sp.dma_start(mem[:, :, :], io["mem_t"]).then_inc(sem("mem_loaded"), 16)
            load_blocks(sp, LAYER["out2"]["block"] + 2, last)

        HC = 2 * PH
        TG = 64
        NPAIR = NK // 2
        g_dram = nc.dram_tensor("g_scratch", (S // TG, NPAIR, P, 2, TG), F32).ap()

        qp = at("qp", [P, HC, S], scr(0))
        s_all = at("s_all", [P, QT * HC * NK], scr(64))
        subkeys = at("subkeys", [P, HC, NK], WL)
        cand = at("cand", [P, PH, PK, PK], scr(0))
        one_hot = at("one_hot", [P, PH, PK, PK], scr(8))
        top_s = at("top_s", [P, PH, 2, PK], scr(16))
        top_i = at("top_i", [P, PH, 2, PK], scr(17), U32)
        top_f = at("top_f", [P, PH, 2, PK], scr(18))
        best_s = at("best_s", [P, PH, PK], scr(19))
        best_j = at("best_j", [P, PH * PK], scr(19.5), U32)
        best_row = at("best_row", [P, PH * PK], scr(20), U32)
        j_half = at("j_half", [P, 2, PH * PK], scr(20.5))
        j_all = at("j_all", [P, PH * PK], scr(21.5))
        g_stat = at("g_stat", [P, 2, PH], scr(22))
        dec = at("dec", [P, 3, PH * PK], scr(22.5))
        stage = [at("stage0", [P, NK, TG], scr(32)), at("stage1", [P, NK, TG], RAW)]
        turned3 = at("turned3", [P, 3, S], WL)
        ab = [at(f"ab{i}", [P, 2, 4, NK], WL + (6 + 4 * i) * KB) for i in range(2)]
        u_raw = [at(f"u_raw{i}", [P, KD, P], scr(64 + 4 * i)) for i in range(4)]
        v_raw = [at(f"v_raw{i}", [P, D], scr(80 + 4 * i)) for i in range(4)]
        u_hi = [at(f"u_hi{i}", [P, KD, P], RAW + 4 * i * KB, F32R) for i in range(4)]
        u_lo = [at(f"u_lo{i}", [P, KD, P], WH + 4 * i * KB, F32R) for i in range(4)]
        v_hi = [at(f"v_hi{i}", [P, D], scr(4 * i), F32R) for i in range(4)]
        v_lo = [at(f"v_lo{i}", [P, D], scr(16 + 4 * i), F32R) for i in range(4)]
        g_in = [at(f"g_in{i}", [P, S // TG, 2, TG], scr(32 + 4 * i)) for i in range(2)]
        h_raw = [at(f"h_raw{i}", [P, S], scr(40 + 2 * i)) for i in range(4)]
        h_hi = [at(f"h_hi{i}", [P, S], scr(48 + 2 * i), F32R) for i in range(4)]
        h_lo = [at(f"h_lo{i}", [P, S], scr(56 + 2 * i), F32R) for i in range(4)]
        out_sq = at("out_sq", [P, KD, S], scr(0))
        out_std = at("out_std", [P, S], scr(16))
        out_rstd = at("out_rstd", [P, S], scr(18))

        BG = P // 4
        QUADS = NK // 4
        LOWEST = -3.0e38

        def peer_credits(pool):
            for name, n in (("g_done", 2), ("g_free", 4), ("pk_t", 1), ("pk_idx", 1), ("g_stored0", 16), ("g_stored1", 16),
                            ("u_lo", 4), ("v_lo", 4), ("ge", 4), ("out_done", 16), ("out_free", 4), ("h_f", 4), ("h_lo", 4)):
                pool.nop().then_inc(sem(name), n)

        def peer_loads(sp):
            load_blocks(sp, LAYER["peer_q"]["block"] + 2, NB)
            sp.wait_ge(sem("bank_free"), 4 + TILES_AFTER[-1])
            sp.dma_start(subkeys[:, :, :], io["subkeys_t"]).then_inc(sem("subkeys_loaded"), 16)
            with sp.Fori(0, QT) as i:
                for q in range(2):
                    sp.wait_ge(sem("g_free"), i * BG + (16 * (q + 1) + 4))
                    sp.dma_start(g_dram[bass.ds(i * 2 + q, 1)].rearrange("o n p c t -> p (o n) c t"),
                                 stage[q][:, :, :].rearrange("p (n c) t -> p n c t", c=2)).then_inc(sem(f"g_stored{q}"), 16)
            sp.wait_ge(sem("pk_t"), 1 + QT)
            for c in range(2):
                load_u(sp, 0, c)
            wait(sp, ("g_stored0", 16 + 16 * QT), ("g_stored1", 16 + 16 * QT))

            def quad(i, last):
                for s in range(4):
                    load_v(sp, i, s)
                    if not last or s < 2:
                        load_u(sp, i, s + 2)
                    if s % 2 == 0:
                        load_g(sp, i, s // 2)

            with sp.Fori(0, QUADS - 1) as i:
                quad(i, False)
            quad(QUADS - 1, True)

        def load_u(sp, i, n):
            sp.wait_ge(sem("u_lo"), i * 4 + (n + 1))
            sp.dma_start(u_raw[n % 4][:, :, :], io["expert_u"][at_chunk(i, n)]).then_inc(sem(f"u_loaded{n % 4}"), 16)

        def load_v(sp, i, n):
            sp.wait_ge(sem("v_lo"), i * 4 + (n + 1))
            sp.dma_start(v_raw[n % 4][:, :], io["expert_v"][at_chunk(i, n)]).then_inc(sem(f"v_loaded{n % 4}"), 16)

        def load_g(sp, i, b):
            sp.wait_ge(sem("h_f"), i * 4 + (2 * b + 2))
            n = i * 2 + b
            src = g_dram[:, n] if isinstance(n, int) else g_dram[:, bass.ds(n, 1)].rearrange("g o p c t -> g (o p) c t")
            sp.dma_start(g_in[b][:, :, :, :], src.rearrange("g p c t -> p g c t")).then_inc(sem(f"g_loaded{b}"), 16)

        def at_chunk(i, n):
            return i * 4 + n

        def split_u_hi(act, i, n):
            act.wait_ge(sem(f"u_loaded{n % 4}"), i * 16 + 16 * (n // 4 + 1))
            act.activation(u_hi[n % 4][:, :, :], u_raw[n % 4][:, :, :], ACT.Copy).then_inc(sem("u_hi"), 1)

        def split_u_lo(pool, i, n):
            pool.wait_ge(sem("u_hi"), i * 4 + (n + 1))
            pool.tensor_tensor(u_lo[n % 4][:, :, :], u_raw[n % 4][:, :, :], u_hi[n % 4][:, :, :].bitcast(F32), ALU.subtract)\
                .then_inc(sem("u_lo"), 1)

        def block3_pool(pool):
            for b in range(LAYER["peer_q"]["block"] + 2, NB):
                split_lo(pool, b)
            with pool.Fori(0, QT) as i:
                for n in range(BG):
                    pool.wait_ge(sem("ab_done"), i * BG + (n + 1))
                    b = ab[n % 2][:, 1, :, :]
                    pool.tensor_tensor(b, b, turned3[:, 2, bass.ds(i * P + 4 * n, 4)].unsqueeze(2).to_broadcast([P, 4, NK]),
                                       ALU.mult).then_inc(sem("g_rows"), 1)

            for n in range(2):
                split_u_lo(pool, 0, n)

            def quad(i, last):
                for s in range(4):
                    pool.wait_ge(sem("v_hi"), i * 4 + (s + 1))
                    pool.tensor_tensor(v_lo[s][:, :], v_raw[s][:, :], v_hi[s][:, :].bitcast(F32), ALU.subtract)\
                        .then_inc(sem("v_lo"), 1)
                    if not last or s < 2:
                        split_u_lo(pool, i, s + 2)

            with pool.Fori(0, QUADS - 1) as i:
                quad(i, False)
            quad(QUADS - 1, True)

        def block3_act(act):
            norm_act(act, "n5", resid, nrm2, std2, xh, S, [("bank_free", 4 + LAYER["peer_q"]["tile"])])
            for b in range(LAYER["peer_q"]["nb"]):
                split_hi(act, LAYER["peer_q"]["block"] + b + 2)
            for k in range(QT * 4):
                act.wait_ge(sem("pk_s"), k + 1)
                act.activation(s_all[:, k * S:(k + 1) * S], psum[k % 8][:, :], ACT.Copy).then_inc(sem("pk_sc"), 1)
            with act.Fori(0, QT) as i:
                act.wait_ge(sem("pk_gsub"), i + 1)
                act.activation(best_s[:, :, :], best_s[:, :, :], ACT.Exp).then_inc(sem("pk_gexp"), 1)
                act.wait_ge(sem("pk_t"), i + 2)
                act.activation(turned3[:, :, bass.ds(i * P, P)], att_bank[0][:, :3 * P].rearrange("p (j t) -> p j t", j=3),
                               ACT.Copy).then_inc(sem("pk_idx"), 1)
                for n in range(BG):
                    q = n // 16
                    if n % 16 == 0:
                        act.wait_ge(sem(f"g_stored{q}"), i * 16 + 16)
                    act.wait_ge(sem("g_done"), i * BG + (n + 3))
                    t = n % 16 * 4
                    act.activation(stage[q][:, :, t:t + 4], lin_bank[n % 4][:, :].rearrange("p (t c) -> p c t", t=4),
                                   ACT.Copy).then_inc(sem("g_free"), 1)
            wait(act, ("g_stored0", 16 + 16 * QT), ("g_stored1", 16 + 16 * QT))
            for n in range(2):
                split_u_hi(act, 0, n)

            def quad(i, last):
                for s in range(4):
                    act.wait_ge(sem(f"v_loaded{s}"), i * 16 + 16)
                    act.wait_ge(sem("out_done"), i * 16 + 8 * (s // 2 + 1))
                    act.activation(v_hi[s][:, :], v_raw[s][:, :], ACT.Copy).then_inc(sem("v_hi"), 1)
                    if not last or s < 2:
                        split_u_hi(act, i, s + 2)
                    act.wait_ge(sem("act_done"), i * 4 + (s + 1))
                    act.wait_ge(sem("h_lo"), i * 4 + (s + 1))
                    act.activation(h_raw[s][:, :], lin_bank[s][:, :], ACT.Gelu).then_inc(sem("ge"), 1)
                    act.wait_ge(sem("h_f"), i * 4 + (s + 5))
                    act.activation(h_hi[s][:, :], h_raw[s][:, :], ACT.Copy).then_inc(sem("h_hi"), 1)

            with act.Fori(0, QUADS - 1) as i:
                quad(i, False)
            quad(QUADS - 1, True)
            act.wait_ge(sem("out_free"), 4 + 8 * NPAIR)
            for k in range(KD):
                act.activation(out_sq[:, k, :], resid[:, k, :], ACT.Square).then_inc(sem("n6_sq"), 1)
            act.wait_ge(sem("n6_sum"), 1)
            act.activation(out_std[:, :], lin_bank[0][:, :], ACT.Sqrt, bias=eps[:, 0:1], scale=1.0 / D)\
               .then_inc(sem("n6_std"), 1)

        def block3_pe(pe):
            norm_pe(pe, "n5", nrm2, S)
            norm_done(pe, "n5")
            linear_pe(pe, "peer_q", weights_first("peer_q", xh, xl), S)
            wait(pe, ("bank_free", 4 + TILES_AFTER[-1]), ("subkeys_loaded", 16))
            for k in range(QT * 4):
                if k >= 8:
                    pe.wait_ge(sem("pk_sc"), k - 7)
                tt = k // 4
                for j in range(4):
                    hc = k % 4 * 4 + j
                    last = pe.matmul(psum[k % 8][:, j * NK:(j + 1) * NK], qp[:, hc, tt * P:(tt + 1) * P], subkeys[:, hc, :],
                                     start=True, stop=True)
                last.then_inc(sem("pk_s"), 1)
            pe.wait_ge(sem("pk_sc"), QT * 4)
            with pe.Fori(0, QT) as i:
                pe.wait_ge(sem("pk_dec"), i + 1)
                pe.wait_ge(sem("pk_idx"), i + 1)
                for j in range(3):
                    last = pe.transpose(att_bank[0][:, j * P:(j + 1) * P], dec[:, j, :], ident[:, :])
                last.then_inc(sem("pk_t"), 1)
                for n in range(BG):
                    pe.wait_ge(sem("g_rows"), i * BG + (n + 1))
                    pe.wait_ge(sem("g_free"), i * BG + (n + 1))
                    for t in range(4):
                        last = pe.matmul(lin_bank[n % 4][:, t * P:(t + 1) * P], ab[n % 2][:, 0, t, :], ab[n % 2][:, 1, t, :],
                                         start=True, stop=True)
                    last.then_inc(sem("g_done"), 1)
            pe.wait_ge(sem("g_free"), 4 + QT * BG)

            def activations(i, n):
                pe.wait_ge(sem("u_lo"), i * 4 + (n + 5))
                pe.wait_ge(sem("ge"), i * 4 + (n + 1))
                s = n % 4
                pairs = [(u_hi[s][:, k, :], u_lo[s][:, k, :], xh[:, k, :], xl[:, k, :]) for k in range(KD)]
                products(pe, lin_bank[s][:, :], pairs).then_inc(sem("act_done"), 1)

            def outputs(i, b):
                pe.wait_ge(sem("v_lo"), i * 4 + (2 * b + 6))
                pe.wait_ge(sem("h_lo"), i * 4 + (2 * b + 6))
                for m in range(KD):
                    pe.wait_ge(sem("out_free"), i * 16 + (8 * b + m + 1))
                    cols = slice(m * P, (m + 1) * P)
                    pairs = [(v_hi[s][:, cols], v_lo[s][:, cols], h_hi[s][:, :], h_lo[s][:, :]) for s in (2 * b, 2 * b + 1)]
                    products(pe, att_bank[m % 4][:, :], pairs).then_inc(sem("out_done"), 1)

            def quad(i, last):
                activations(i, 2)
                activations(i, 3)
                outputs(i, 0)
                if not last:
                    activations(i, 4)
                    activations(i, 5)
                outputs(i, 1)

            activations(0, 0)
            activations(0, 1)
            with pe.Fori(0, QUADS - 1) as i:
                quad(i, False)
            quad(QUADS - 1, True)
            for k in range(KD):
                pe.wait_ge(sem("n6_sq"), k + 1)
                last = pe.matmul(lin_bank[0][:, :], ones[:, :], out_sq[:, k, :], start=(k == 0), stop=(k == KD - 1))
            last.then_inc(sem("n6_sum"), 1)

        TOPK_LINKS = 20

        def top_keys(dve, i):
            links = [0]

            def link(ins):
                links[0] += 1
                ins.then_inc(sem("topk"), 1)
                dve.wait_ge(sem("topk"), i * TOPK_LINKS + links[0])

            def best16(n, values, best, index):
                for j in range(n):
                    ins = dve.max(best(j)[:, 0:8], values(j))
                link(ins)
                for j in range(n):
                    dve.max_index(index(j)[:, 0:8], best(j)[:, 0:8], values(j))
                for j in range(n):
                    ins = dve.match_replace(values(j), best(j)[:, 0:8], values(j), LOWEST)
                link(ins)
                for j in range(n):
                    ins = dve.max(best(j)[:, 8:16], values(j))
                link(ins)
                for j in range(n):
                    ins = dve.max_index(index(j)[:, 8:16], best(j)[:, 8:16], values(j))
                link(ins)

            best16(HC, lambda j: s_all[:, (i * HC + j) * NK:(i * HC + j + 1) * NK], lambda j: top_s[:, j // 2, j % 2, :],
                   lambda j: top_i[:, j // 2, j % 2, :])
            dve.tensor_copy(top_f[:, :, :, :], top_i[:, :, :, :])
            grid = [P, PH, PK, PK]
            link(dve.tensor_tensor(cand[:, :, :, :], top_s[:, :, 0, :].unsqueeze(3).to_broadcast(grid),
                                   top_s[:, :, 1, :].unsqueeze(2).to_broadcast(grid), ALU.add))
            best16(PH, lambda j: cand[:, j, :, :].rearrange("p a b -> p (a b)"), lambda j: best_s[:, j, :],
                   lambda j: best_j[:, j * PK:(j + 1) * PK])
            dve.tensor_copy(g_stat[:, 0, :], best_s[:, :, 0])
            dve.tensor_scalar(best_row[:, :], best_j[:, :], 4, None, ALU.logical_shift_right)
            link(dve.tensor_copy(j_all[:, :], best_j[:, :]))
            dve.tensor_tensor(best_s[:, :, :], best_s[:, :, :], g_stat[:, 0, :].unsqueeze(2).to_broadcast([P, PH, PK]),
                              ALU.subtract).then_inc(sem("pk_gsub"), 1)
            link(dve.tensor_copy(j_half[:, 0, :], best_row[:, :]))
            link(dve.scalar_tensor_tensor(out=j_half[:, 1, :], in0=j_half[:, 0, :], scalar=-float(PK), in1=j_all[:, :],
                                          op0=ALU.mult, op1=ALU.add))
            dve.wait_ge(sem("pk_t"), i + 1)
            for half in range(2):
                choice = j_half[:, half, :].rearrange("p (h k) -> p h k", h=PH).unsqueeze(3).to_broadcast(grid)
                link(dve.tensor_tensor(one_hot[:, :, :, :], iota16[:, :].unsqueeze(1).unsqueeze(1).to_broadcast(grid), choice,
                                       ALU.is_equal))
                link(dve.tensor_tensor(one_hot[:, :, :, :], one_hot[:, :, :, :],
                                       top_f[:, :, half, :].unsqueeze(2).to_broadcast(grid), ALU.mult))
                link(dve.tensor_reduce(dec[:, half, :].rearrange("p (h k) -> p h k", h=PH), one_hot[:, :, :, :], AX_X, ALU.add))
            dve.wait_ge(sem("pk_gexp"), i + 1)
            link(dve.tensor_reduce(g_stat[:, 0, :], best_s[:, :, :], AX_X, ALU.add))
            link(dve.reciprocal(g_stat[:, 1, :], g_stat[:, 0, :]))
            dve.tensor_tensor(dec[:, 2, :].rearrange("p (h k) -> p h k", h=PH), best_s[:, :, :],
                              g_stat[:, 1, :].unsqueeze(2).to_broadcast([P, PH, PK]), ALU.mult).then_inc(sem("pk_dec"), 1)
            return links[0]

        def block3_dve(dve, chain):
            norm_dve(dve, chain, "n5", resid, nrm2, std2, rstd2, xh, xl, "norm_ffn", S)
            for n in range(HC):
                bank = tile_ready(dve, "peer_q", n)
                dve.tensor_copy(qp[:, n, :], bank[:, :]).then_inc(sem("bank_free"), 1)
            dve.wait_ge(sem("pk_sc"), QT * 4)
            for i in range(QT):
                links = top_keys(dve, i)
                assert links == TOPK_LINKS, links
                dve.wait_ge(sem("pk_idx"), i + 2)
                with dve.Fori(0, BG // 2) as pair:
                    for n in range(2):
                        dve.wait_ge(sem("g_done"), pair * 2 + (i * BG + n + 1))
                        shape = [P, 2, 4, NK]
                        dve.tensor_tensor(ab[n][:, :, :, :], iota_key[:, :].unsqueeze(1).unsqueeze(1).to_broadcast(shape),
                                          turned3[:, 0:2, bass.ds(pair * 8 + (i * P + 4 * n), 4)].unsqueeze(3).to_broadcast(shape),
                                          ALU.is_equal).then_inc(sem("ab_done"), 1)

            def weighted(i, n):
                s = n % 4
                dve.wait_ge(sem("ge"), i * 4 + (n + 5))
                if s % 2 == 0:
                    dve.wait_ge(sem(f"g_loaded{s // 2}"), i * 16 + 16 * (n // 4 + 1))
                h = h_raw[s][:, :].rearrange("p (g t) -> p g t", t=TG)
                dve.tensor_tensor(h, h, g_in[s // 2][:, :, s % 2, :], ALU.mult).then_inc(sem("h_f"), 1)
                dve.wait_ge(sem("h_hi"), i * 4 + (n + 1))
                dve.tensor_tensor(h_lo[s][:, :], h_raw[s][:, :], h_hi[s][:, :].bitcast(F32), ALU.subtract)\
                   .then_inc(sem("h_lo"), 1)

            def add_outputs(i, b):
                for m in range(KD):
                    dve.wait_ge(sem("out_done"), i * 16 + (16 + 8 * b + m + 1))
                    dve.tensor_tensor(resid[:, m, :], att_bank[m % 4][:, :], resid[:, m, :], ALU.add)\
                       .then_inc(sem("out_free"), 1)

            def quad(i, last):
                weighted(i, 2)
                weighted(i, 3)
                add_outputs(i, 0)
                if not last:
                    weighted(i, 4)
                    weighted(i, 5)
                add_outputs(i, 1)

            weighted(0, 0)
            weighted(0, 1)
            with dve.Fori(0, QUADS - 1) as i:
                quad(i, False)
            quad(QUADS - 1, True)
            dve.wait_ge(sem("n6_std"), 1)
            chain.link(dve.reciprocal(out_rstd[:, :], out_std[:, :]))
            for k in range(KD):
                dve.scalar_tensor_tensor(out=out_sq[:, k, :], in0=resid[:, k, :], scalar=col("norm_final", k),
                                         in1=out_rstd[:, :], op0=ALU.mult, op1=ALU.mult).then_inc(sem("n6_out"), 1)

        def store_output(sp):
            for k in range(KD):
                sp.wait_ge(sem("n6_out"), k + 1)
                sp.dma_start(io["out_t"][:, k, :], out_sq[:, k, :]).then_inc(sem("out_stored"), 16)
            sp.wait_ge(sem("out_stored"), 16 * KD)
        block = ctx.enter_context(nc.Block())
        @block.sync
        def _(sp):
            sp.dma_start(resid[:, :, :], io["x_t"]).then_inc(sem("x_loaded"), 16)
            sp.dma_start(params[:, :], io["params"]).then_inc(sem("params_loaded"), 16)
            block12_loads(sp, LAYER["peer_q"]["block"] + 2)
            peer_loads(sp)
            store_output(sp)

        @block.gpsimd
        def _(pool):
            make_consts(pool)
            block1_pool(pool)
            block2_pool(pool)
            block3_pool(pool)

        @block.scalar
        def _(act):
            block1_act(act)
            block2_act(act)
            block3_act(act)

        @block.vector
        def _(dve):
            chain = Chain(dve, "dve_step")
            block1_dve(dve, chain)
            block2_dve(dve, chain)
            block3_dve(dve, chain)

        @block.tensor
        def _(pe):
            block1_pe(pe)
            block2_pe(pe)
            block3_pe(pe)


def blocks_of(w, kt, columns):
    w = np.asarray(w).reshape(kt, P, -1)
    return [np.concatenate([w[:, :, a:b] for a, b in part], axis=2).transpose(1, 0, 2).reshape(P, -1) for part in columns]


def lay_out(i):
    f = {k: np.asarray(v) for k, v in i.items()}
    w_in, w_mix, w_up, w_down = f["w_in"][0], f["w_in_2"][0], f["w_up"][0], f["w_down"][0]

    def runs(first, n, width):
        return [[(first + width * b, first + width * (b + 1))] for b in range(n)]

    def side_by_side(a, b, n):
        return [[(a + P * j, a + P * (j + 1)), (b + P * j, b + P * (j + 1))] for j in range(n)]

    A = AW
    kv = 4 * A
    gb = kv + 6 * P
    ga = gb + NSA_H * 3
    branches = np.concatenate([f["w_branch_a_2"][0], f["w_branch_b_2"][0]])
    split = FHALF[0] * P
    parts = {
        "in_fm": blocks_of(w_in, KD, runs(0, 4, 256) + side_by_side(3 * A, 3 * A + CW, CT)),
        "in_v": blocks_of(w_in, KD, runs(2 * A, 2, 256)),
        "out1": blocks_of(f["w_out"][0], KD, runs(0, 4, 256)),
        "up0": blocks_of(w_up, KD, side_by_side(0, FF, FT)[:FHALF[0]]),
        "down0": blocks_of(w_down[:split], FHALF[0], runs(0, 8, P)),
        "up1": blocks_of(w_up, KD, side_by_side(0, FF, FT)[FHALF[0]:]),
        "down1": blocks_of(w_down[split:], FHALF[1], runs(0, 8, P)),
        "mix_fm": blocks_of(w_mix, KD, runs(0, 4, 256) + runs(3 * A, 2, 256) + [
            [(kv, kv + 2 * P)], [(kv + 2 * P, kv + 3 * P), (kv + 4 * P, kv + 5 * P)]]),
        "mix_tm": blocks_of(w_mix, KD, runs(2 * A, 2, 256) + [
            [(kv + 3 * P, kv + 4 * P), (kv + 5 * P, kv + 6 * P)], [(gb, gb + 256)]]),
        "gates": blocks_of(w_mix, KD, side_by_side(ga, ga + D, KD)),
        "branch": blocks_of(branches, KD, runs(0, 4, 256)),
        "out2": blocks_of(f["w_out_2"][0], KD, runs(0, 4, 256)),
        "cross_q": blocks_of(f["w_cross_q_2"][0], KD, runs(0, 2, 256)),
        "cross_k": blocks_of(f["w_cross_kv_2"][0], KD, runs(0, 2, 256)),
        "cross_v": blocks_of(f["w_cross_kv_2"][0], KD, runs(AW, 2, 256)),
        "cross_o": blocks_of(f["w_cross_o_2"][0], AW // P, runs(0, 2, 512)),
        "peer_q": blocks_of(f["peer_wq_2"][0], KD, runs(0, 8, 256)),
    }
    w_small = np.zeros((len(TILES_AFTER), P, BLK), np.float32)
    for name, blocks in parts.items():
        for b, w in enumerate(blocks):
            w_small[LAYER[name]["block"] + b, :, :w.shape[1]] = w

    def tiles(v):
        return v.reshape(-1, P).T

    def channel_taps(v):
        return v.reshape(v.shape[0], -1, P).transpose(2, 1, 0).reshape(P, -1)

    def twice(v):
        return np.concatenate([v, v])

    params = np.concatenate([
        tiles(f["norm1_g"]), tiles(f["norm2_g"]), tiles(f["norm_mix_2"]), tiles(f["norm_cross_2"]),
        tiles(f["norm_mem_2"]), tiles(f["norm_ffn_2"]), tiles(f["norm_final_2"]),
        twice(f["q_norm_g"].T), twice(f["k_norm_g"].T), channel_taps(f["conv_dw_w"][0]), tiles(f["conv_dw_b"]),
        tiles(f["conv_ln_g"]), tiles(f["conv_ln_b"]), channel_taps(f["ffn_dw_w"][0]), tiles(f["ffn_dw_b"]),
        tiles(f["diff_subln_2"]), twice(f["nsa_cmp_pos_2"][0].T), twice(f["diff_lambda_2"][0].T)], axis=1)

    def feature_major(x):
        return x.T.reshape(KD, P, -1).transpose(1, 0, 2)

    def both(k, v, shape):
        return np.stack([f[k][0].reshape(shape).transpose(1, 0, 2), f[v][0].reshape(shape).transpose(1, 0, 2)])

    return {
        "x_t": feature_major(f["x"][0]), "mem_t": feature_major(f["mem_2"][0]), "params": params, "w_small": w_small,
        "cmp_w1": both("nsa_ck_w1_2", "nsa_cv_w1_2", (CMP // 2, P, CMP_HID)),
        "cmp_w2": both("nsa_ck_w2_2", "nsa_cv_w2_2", (CMP_HID // P, P, HD)),
        "subkeys_t": f["peer_subkeys_2"][0].reshape(2 * PH, NK, P).transpose(2, 0, 1),
        "expert_u": f["peer_u_2"][0].reshape(NK, NK, KD, P).transpose(1, 3, 2, 0),
        "expert_v": f["peer_v_2"][0].reshape(NK, NK, D).transpose(1, 0, 2),
    }


def kernel(**inputs):
    import concourse.bacc as bacc
    from concourse.bass_utils import run_bass_kernel_spmd

    arrays = {k: np.ascontiguousarray(v) for k, v in lay_out(inputs).items()}
    nc = bacc.Bacc("TRN2", target_bir_lowering=False, num_devices=1)
    io = {}
    for name, shape in INPUTS:
        assert arrays[name].shape == shape and arrays[name].dtype == np.float32
        io[name] = nc.dram_tensor(name, shape, F32, kind="ExternalInput").ap()
    for name, shape in OUTPUTS:
        io[name] = nc.dram_tensor(name, shape, F32, kind="ExternalOutput").ap()
    build_program(nc, io)
    out = run_bass_kernel_spmd(nc, [arrays], core_ids=[0]).results[0]["out_t"]
    return np.ascontiguousarray(out.transpose(2, 1, 0).reshape(1, S, D))
```

```python
import math
from contextlib import ExitStack

import numpy as np

import concourse.bass as bass
from concourse import mybir

F32 = mybir.dt.float32
F32R = mybir.dt.float32r
BF16 = mybir.dt.bfloat16
U32 = mybir.dt.uint32
ALU = mybir.AluOpType
ACT = mybir.ActivationFunctionType
AX_X = mybir.AxisListType.X

P = 128
S = 512
QT = S // P
D = 1024
KD = D // P
EPS = 1e-6

HEADS = 8
HD = 64
AW = HEADS * HD
CW = D - AW
CT = CW // P
TAPS = 31
FF = 2816
FT = FF // P
FTAPS = 3
FHALF = (12, 10)

DA_H = 4
NSA_H, NSA_G, NSA_R = 8, 2, 4
CMP = 32
NCMP = S // CMP
CMP_HID = 256
MEM = 256
CA_H = 4
PH, PK = 8, 16
NK = 128
LAMBDA_INIT = 0.8 - 0.6 * math.exp(-0.3 * 0)
NEG = -1e30

BLK = 2048

LAYERS = [
    ("in_fm", 8, KD, 2, 256, 2),
    ("in_v", 2, KD, QT, 256, 2),
    ("out1", 4, KD, 2, 256, 2),
    ("up0", FHALF[0], KD, 2, 256, 2),
    ("down0", 8, FHALF[0], 1, 128, 4),
    ("up1", FHALF[1], KD, 2, 256, 2),
    ("down1", 8, FHALF[1], 1, 128, 4),
    ("mix_fm", 8, KD, 2, 256, 2),
    ("mix_tm", 4, KD, QT, 256, 2),
    ("gates", 8, KD, 2, 256, 2),
    ("branch", 4, KD, 4, 256, 2),
    ("out2", 4, KD, 2, 256, 2),
    ("cross_q", 2, KD, 2, 256, 2),
    ("cross_k", 2, KD, 2, 256, 2),
    ("cross_v", 2, KD, MEM // P, 256, 2),
    ("cross_o", 2, AW // P, 4, 512, 2),
    ("peer_q", 8, KD, 2, 256, 2),
]


def layer_table():
    table, ends, block, tile = {}, [], 0, 0
    for name, nb, kt, tiles, cols, unroll in LAYERS:
        table[name] = dict(nb=nb, kt=kt, tiles=tiles, cols=cols, unroll=unroll, block=block, tile=tile)
        for _ in range(nb):
            tile += tiles
            ends.append(tile)
        block += nb
    return table, ends


LAYER, TILES_AFTER = layer_table()

PARAMS = [("norm1", KD), ("norm2", KD), ("norm_mix", KD), ("norm_cross", KD), ("norm_mem", KD), ("norm_ffn", KD),
          ("norm_final", KD), ("q_norm", 1), ("k_norm", 1), ("conv_w", CT * TAPS), ("conv_b", CT), ("ln_g", CT),
          ("ln_b", CT), ("ffn_w", FT * FTAPS), ("ffn_b", FT), ("subln", 1), ("cmp_pos", CMP), ("lam", 4)]
PCOL, NPAR = {}, 0
for _n, _w in PARAMS:
    PCOL[_n] = NPAR
    NPAR += _w

INPUTS = [
    ("x_t", (P, KD, S)), ("mem_t", (P, KD, MEM)), ("params", (P, NPAR)),
    ("w_small", (len(TILES_AFTER), P, BLK)),
    ("cmp_w1", (2, P, CMP // 2, CMP_HID)), ("cmp_w2", (2, P, CMP_HID // P, HD)),
    ("subkeys_t", (P, 2 * PH, NK)),
    ("expert_u", (NK, P, KD, P)), ("expert_v", (NK, P, D)),
]

OUTPUTS = [("out_t", (P, KD, S))]

KB = 1024
BASE = 16512
RES, XH, XL = BASE, BASE + 16 * KB, BASE + 32 * KB
RAW, WH, WL = BASE + 48 * KB, BASE + 64 * KB, BASE + 80 * KB
CONST = BASE + 96 * KB
SCR = CONST + 13 * KB


def build_program(nc, io):
    with ExitStack() as ctx:
        sems = {}

        def sem(name):
            if name not in sems:
                sems[name] = ctx.enter_context(nc.semaphore(name))
            return sems[name]

        def at(name, shape, offset, dt=F32):
            return nc.alloc_sbuf_tensor_at(name, list(shape), dt, offset=offset)

        cursor = [CONST]

        def const(name, shape, dt=F32):
            size = int(np.prod(shape[1:])) * (2 if dt == BF16 else 4)
            t = at(name, shape, cursor[0], dt)
            cursor[0] += (size + 31) // 32 * 32
            assert cursor[0] <= SCR
            return t

        psum = [ctx.enter_context(nc.psum_tensor(f"bank{i}", [P, S], F32)) for i in range(8)]
        lin_bank, att_bank = psum[:4], psum[4:]

        resid = at("resid", [P, KD, S], RES)
        xh = at("xh", [P, KD, S], XH, F32R)
        xl = at("xl", [P, KD, S], XL, F32R)
        raw = [at(f"w_raw{i}", [P, BLK], RAW + i * 8 * KB) for i in range(2)]
        wh = [at(f"w_hi{i}", [P, BLK], WH + i * 8 * KB, F32R) for i in range(2)]
        wl = [at(f"w_lo{i}", [P, BLK], WL + i * 8 * KB, F32R) for i in range(2)]

        params = const("params_sb", [P, NPAR])
        ident = const("ident", [P, P])
        ones = const("ones", [P, P])
        later_key = const("later_key", [P, P])
        causal = const("causal", [P, P])
        dist = const("dist", [P, S])
        cmp_dist = const("cmp_dist", [P, QT, NCMP])
        cmp_valid = const("cmp_valid", [P, QT, NCMP])
        head_sum = const("head_sum", [P, 8, 16])
        iota16 = const("iota16", [P, PK])
        iota_key = const("iota_key", [P, NK])
        eps = const("eps", [P, 1])
        qg = const("qg", [P, 1])
        subln_g = const("subln_g", [P, 1])
        lam_prod = const("lam_prod", [P, 2])
        lam_exp = const("lam_exp", [P, 2])
        lam = const("lam_col", [P, 1])
        gates24 = const("gates24", [P, QT, NSA_H * 3])

        def col(name, i=0):
            return params[:, PCOL[name] + i:PCOL[name] + i + 1]

        qk = at("qk", [P, 8, S], SCR)
        vtok = at("vtok", [P, QT, AW], SCR + 16 * KB)
        PADW = S + TAPS - 1
        cpad = at("cpad", [P, CT, PADW], SCR + 24 * KB)
        cacc = at("cacc", [P, CT, S], SCR + 33 * KB)
        attn = at("attn", [P, CT, S], SCR + 41 * KB)
        NW = 1280
        KOFF = [0, 512, 1024, 896]
        STK = SCR + 49 * KB
        ln1 = at("ln1", [P, NW], STK)
        soft = [at(f"soft{i}", [P, NW], STK + (5 + 5 * i) * KB) for i in range(2)]
        lbeta = [at(f"lbeta{i}", [P, NW], STK + (15 + 5 * i) * KB) for i in range(2)]
        wgt = [at(f"wgt{i}", [P, NW], STK + (25 + 5 * i) * KB) for i in range(2)]
        qk_sq = at("qk_sq", [P, 8, S], STK)
        std16 = at("std16", [16, S], STK + 16 * KB)
        rstd16 = at("rstd16", [16, S], STK + 18 * KB)
        glu_sig = [at(f"glu_sig{i}", [P, S], STK + (20 + 2 * i) * KB) for i in range(2)]
        head_spread = at("head_spread", [16, 8 * P], STK + 35 * KB)
        conv_prod = [at(f"conv_prod{i}", [P, S], STK + (39 + 2 * i) * KB) for i in range(2)]
        ln_sq = at("ln_sq", [P, CT, S], STK)
        ln_std = at("ln_std", [P, S], STK + 8 * KB)
        ln_rstd = at("ln_rstd", [P, S], STK + 10 * KB)

        fh = at("fh", [P, FHALF[0], S], SCR, F32R)
        fl = at("fl", [P, FHALF[0], S], SCR + 24 * KB, F32R)
        f_conv = [at(f"f_conv{i}", [P, S], SCR + (48 + 2 * i) * KB) for i in range(2)]
        f_silu = [at(f"f_silu{i}", [P, S], SCR + (52 + 2 * i) * KB) for i in range(2)]
        f_out = [at(f"f_out{i}", [P, S], SCR + (56 + 2 * i) * KB) for i in range(2)]

        class Chain:

            def __init__(self, eng, name):
                self.eng, self.sem, self.n = eng, sem(name), 0

            def link(self, ins):
                self.n += 1
                ins.then_inc(self.sem, 1)
                self.eng.wait_ge(self.sem, self.n)

        def wait(eng, *needs):
            for name, value in needs:
                if value > 0:
                    eng.wait_ge(sem(name), value)

        NB = len(TILES_AFTER)

        def load_blocks(sp, first, last):
            for g in range(first, last):
                sp.wait_ge(sem("lo_done"), g + 1)
                n = size_of(g)
                sp.dma_start(raw[g % 2][:, :n], io["w_small"][g, :, :n]).then_inc(sem(f"raw_loaded{g % 2}"), 16)

        def size_of(g):
            for t in LAYER.values():
                if t["block"] <= g < t["block"] + t["nb"]:
                    return t["kt"] * t["cols"]

        def split_hi(act, g):
            if g >= NB:
                return
            wait(act, (f"raw_loaded{g % 2}", 16 * (g // 2 + 1)))
            if g >= 2:
                wait(act, ("lin_done", TILES_AFTER[g - 2]))
            n = size_of(g)
            act.activation(wh[g % 2][:, :n], raw[g % 2][:, :n], ACT.Copy).then_inc(sem("hi_done"), 1)

        def split_lo(pool, g):
            n = size_of(g)
            pool.wait_ge(sem("hi_done"), g + 1)
            pool.tensor_tensor(wl[g % 2][:, :n], raw[g % 2][:, :n], wh[g % 2][:, :n].bitcast(F32),
                               ALU.subtract).then_inc(sem("lo_done"), 1)

        def products(pe, out, pairs, ready=None):
            for k, (ah, al, bh, bl) in enumerate(pairs):
                if ready:
                    ready(k)
                pe.matmul(out, al, bh, start=(k == 0), stop=False)
                pe.matmul(out, ah, bl, start=False, stop=False)
                last = pe.matmul(out, ah, bh, start=False, stop=(k == len(pairs) - 1))
            return last

        def linear_pe(pe, name, pairs_of, ncols, ready=None):
            t = LAYER[name]
            u, tiles = t["unroll"], t["tiles"]

            def step(i):
                for s in range(u):
                    pe.wait_ge(sem("lo_done"), i * u + (t["block"] + s + 3))
                    for m in range(tiles):
                        n = s * tiles + m
                        pe.wait_ge(sem("bank_free"), i * (u * tiles) + (t["tile"] + n + 1))
                        out = lin_bank[n % 4][:, :ncols]
                        first = isinstance(i, int) and i == 0 and n == 0
                        products(pe, out, pairs_of(s % 2, m), ready if first else None).then_inc(sem("lin_done"), 1)

            assert t["tile"] % 4 == 0 and t["block"] % 2 == 0 and u * tiles % 4 == 0 and t["nb"] % u == 0
            start = 1 if ready or t["nb"] == u else 0
            if start:
                step(0)
            if t["nb"] // u > start:
                with pe.Fori(start, t["nb"] // u) as i:
                    step(i)

        def weights_first(name, hi, lo, n=S):
            t = LAYER[name]
            kt, cols = t["kt"], t["cols"]

            def pairs(slot, m):
                def w(x, k):
                    return x[slot][:, k * cols + m * P:k * cols + m * P + P]
                return [(w(wh, k), w(wl, k), hi[:, k, :n], lo[:, k, :n]) for k in range(kt)]
            return pairs

        def tokens_first(name, hi, lo):
            t = LAYER[name]
            kt, cols = t["kt"], t["cols"]

            def pairs(slot, m):
                def w(x, k):
                    return x[slot][:, k * cols:(k + 1) * cols]
                return [(hi[:, k, m * P:m * P + P], lo[:, k, m * P:m * P + P], w(wh, k), w(wl, k)) for k in range(kt)]
            return pairs

        def tile_ready(eng, name, n):
            eng.wait_ge(sem("lin_done"), LAYER[name]["tile"] + n + 1)
            return lin_bank[n % 4]

        NORMS = ["n1", "n2", "n3", "n4", "nm", "n5"]

        def before(st, per_norm):
            return NORMS.index(st) * per_norm

        def norm_tile_done(eng, st, k):
            eng.wait_ge(sem("norm_lo_odd" if k % 2 else "norm_lo"), before(st, KD // 2) + k // 2 + 1)

        def follow_norm(pe, st):
            return lambda k: norm_tile_done(pe, st, k)

        def follow(pe, name):
            return lambda k: pe.wait_ge(sem(name), k + 1)

        def norm_done(eng, st):
            norm_tile_done(eng, st, KD - 2)
            norm_tile_done(eng, st, KD - 1)

        def splits_and_squares(act, name):
            t = LAYER[name]
            for b in range(t["nb"]):
                split_hi(act, t["block"] + b + 2)
                for k in range(b * t["tiles"], (b + 1) * t["tiles"]):
                    act.wait_ge(sem("bank_free"), 4 + t["tile"] + k + 1)
                    act.activation(nrm2[:, k, :], resid[:, k, :], ACT.Square).then_inc(sem("norm_sq"), 1)

        def squares(act, src, sq, n, first=0, last=KD):
            for k in range(first, last):
                act.activation(sq[:, k, :n], src[:, k, :n], ACT.Square).then_inc(sem("norm_sq"), 1)

        def norm_act(act, st, sq, stat, hi, n):
            act.wait_ge(sem("norm_sum"), before(st, 1) + 1)
            tts = n // P
            act.activation(stat[:, 0:tts], att_bank[0][:, 0:tts], ACT.Sqrt, bias=eps[:, 0:1], scale=1.0 / D)\
               .then_inc(sem("norm_std"), 1)
            for k in range(KD):
                act.wait_ge(sem("norm_h"), before(st, KD) + k + 1)
                act.activation(hi[:, k, :n], sq[:, k, :n], ACT.Copy).then_inc(sem("norm_hi"), 1)

        def norm_pe(pe, st, sq, diag, n):
            pe.wait_ge(sem("norm_part"), before(st, KD - 1) + KD - 1)
            for tt in range(n // P):
                last = pe.matmul(att_bank[0][:, tt:tt + 1], sq[:, 0, tt * P:(tt + 1) * P], ones[:, 0:1], start=True, stop=True)
            last.then_inc(sem("norm_sum"), 1)
            pe.wait_ge(sem("norm_diag"), before(st, 1) + 1)
            pe.matmul(att_bank[1][:, :n], ones[:, :], diag[:, :n], start=True, stop=True).then_inc(sem("norm_rstd"), 1)

        def add_squares(dve, st, sq, n, k):
            if k == 1:
                dve.wait_ge(sem("norm_sq"), before(st, KD) + 1)
            else:
                dve.wait_ge(sem("norm_part"), before(st, KD - 1) + k - 1)
            dve.wait_ge(sem("norm_sq"), before(st, KD) + k + 1)
            dve.tensor_tensor(sq[:, 0, :n], sq[:, 0, :n], sq[:, k, :n], ALU.add).then_inc(sem("norm_part"), 1)

        def norm_dve(dve, chain, st, src, sq, stat, diag, hi, lo, gain, n):
            dve.wait_ge(sem("norm_std"), before(st, 1) + 1)
            tts = n // P
            chain.link(dve.reciprocal(stat[:, QT:QT + tts], stat[:, 0:tts]))
            shape = [P, tts, P]
            dve.tensor_tensor(diag[:, :n].rearrange("p (i t) -> p i t", t=P), ident[:, :].unsqueeze(1).to_broadcast(shape),
                              stat[:, QT:QT + tts].unsqueeze(2).to_broadcast(shape), ALU.mult).then_inc(sem("norm_diag"), 1)
            dve.wait_ge(sem("norm_rstd"), before(st, 1) + 1)
            for k in range(KD + 1):
                if k < KD:
                    dve.scalar_tensor_tensor(out=sq[:, k, :n], in0=src[:, k, :n], scalar=col(gain, k),
                                             in1=att_bank[1][:, :n], op0=ALU.mult, op1=ALU.mult).then_inc(sem("norm_h"), 1)
                if k % 2:
                    norm_low(dve, st, sq, hi, lo, n, k - 1)

        def norm_low(eng, st, sq, hi, lo, n, k):
            eng.wait_ge(sem("norm_hi"), before(st, KD) + k + 1)
            eng.tensor_tensor(lo[:, k, :n], sq[:, k, :n], hi[:, k, :n].bitcast(F32), ALU.subtract)\
               .then_inc(sem("norm_lo_odd" if k % 2 else "norm_lo"), 1)

        def norm_pool(pool, st, sq, hi, lo, n):
            for k in range(1, KD, 2):
                norm_low(pool, st, sq, hi, lo, n, k)

        NRM1, RS1 = STK, STK + 24 * KB
        nrm1 = at("nrm1", [P, KD, S], NRM1)
        norm_stat1 = at("norm_stat1", [P, 2 * QT], RS1)
        norm_diag1 = at("norm_diag1", [P, S], RS1 + 2 * KB)
        nrm2 = at("nrm2", [P, KD, S], SCR + 76 * KB)
        norm_stat2 = at("norm_stat2", [P, 2 * QT], SCR + 92 * KB)
        norm_diag2 = at("norm_diag2", [P, S], SCR + 93 * KB)

        PIECES = [(0, 512), (512, 512), (1024, 256)]

        def regions(kb):
            off = KOFF[kb]
            return off // S, off % S, S - kb * P

        CONV_DVE, CONV_POOL = (0, 1, 2), (3,)
        N_CONV = len(CONV_DVE) * TAPS

        def conv_dve(dve, first, last):
            for n in range(first, min(last, N_CONV)):
                tap, ct = n // len(CONV_DVE), CONV_DVE[n % len(CONV_DVE)]
                w = col("conv_w", ct * TAPS + tap)
                x = cpad[:, ct, tap:tap + S]
                if tap:
                    dve.wait_ge(sem("conv_dve"), n - len(CONV_DVE) + 1)
                    ins = dve.scalar_tensor_tensor(out=cacc[:, ct, :], in0=x, scalar=w, in1=cacc[:, ct, :],
                                                   op0=ALU.mult, op1=ALU.add)
                else:
                    ins = dve.tensor_scalar(cacc[:, ct, :], x, w, col("conv_b", ct), ALU.mult, ALU.add)
                ins.then_inc(sem("conv_dve"), 1)

        def conv_pool(pool):
            n_ct = len(CONV_POOL)
            for tap in range(TAPS):
                for c, ct in enumerate(CONV_POOL):
                    w = col("conv_w", ct * TAPS + tap)
                    x = cpad[:, ct, tap:tap + S]
                    if tap == 0:
                        pool.tensor_scalar(cacc[:, ct, :], x, w, col("conv_b", ct), ALU.mult, ALU.add)\
                            .then_inc(sem("conv_pool"), 1)
                    else:
                        if tap >= 2:
                            pool.wait_ge(sem("conv_pool"), (tap - 1) * n_ct + c + 1)
                        pool.tensor_scalar(conv_prod[c][:, :], x, w, None, ALU.mult).then_inc(sem("conv_prod"), 1)
                for c, ct in enumerate(CONV_POOL):
                    if tap:
                        wait(pool, ("conv_prod", (tap - 1) * n_ct + c + 1), ("conv_pool", (tap - 1) * n_ct + c + 1))
                        pool.tensor_tensor(cacc[:, ct, :], cacc[:, ct, :], conv_prod[c][:, :], ALU.add)\
                            .then_inc(sem("conv_pool"), 1)

        def conv_done(eng):
            wait(eng, ("conv_dve", N_CONV), ("conv_pool", len(CONV_POOL) * TAPS))

        def block1_act(act):
            for half in range(2):
                act.wait_ge(sem(f"x_loaded{half}"), 16)
                squares(act, resid, nrm1, S, half * KD // 2, (half + 1) * KD // 2)
            act.wait_ge(sem("consts"), N_CONST)
            split_hi(act, 0)
            split_hi(act, 1)
            norm_act(act, "n1", nrm1, norm_stat1, xh, S)
            base = LAYER["in_fm"]["block"]
            for b in range(4):
                split_hi(act, base + b + 2)
            for j in range(CT):
                bank = tile_ready(act, "in_fm", 8 + 2 * j + 1)
                if j >= 2:
                    act.wait_ge(sem("bank_free"), 4 + 8 + 2 * (j - 1))
                act.activation(glu_sig[j % 2][:, :], bank[:, :], ACT.Sigmoid).then_inc(sem("glu_sig"), 1)
                split_hi(act, base + 4 + j + 2)
            for b in range(2):
                split_hi(act, LAYER["in_v"]["block"] + b + 2)
            act.wait_ge(sem("bank_free"), 4 + 16)
            for j in range(8):
                act.activation(qk_sq[:, j, :], qk[:, j, :], ACT.Square).then_inc(sem("qk_sq"), 1)
            act.wait_ge(sem("qk_sum"), 1)
            act.activation(std16[:, :], att_bank[0][0:16, :], ACT.Sqrt, bias=eps[0:16, 0:1], scale=1.0 / HD)\
               .then_inc(sem("qk_std"), 1)

            def pre(h):
                act.wait_ge(sem("st_z"), h + 1)
                if h >= 1:
                    act.wait_ge(sem("st_zread"), h)
                for b, (off, w) in enumerate(PIECES):
                    ins = act.activation(ln1[:, off:off + w], att_bank[b][:, :w], ACT.Abs)
                ins.then_inc(sem("st_act"), 1)
                act.wait_ge(sem("st_act"), 2 * h + 1)
                act.activation(ln1[:, :], ln1[:, :], ACT.Exp, scale=-1.0).then_inc(sem("st_act"), 1)
                act.wait_ge(sem("st_act"), 2 * h + 2)
                act.activation(ln1[:, :], ln1[:, :], ACT.Ln, bias=1.0).then_inc(sem("st_ln"), 1)

            pre(0)
            for h in range(HEADS + 1):
                if h + 1 < HEADS:
                    pre(h + 1)
                if h < HEADS:
                    act.wait_ge(sem("st_logw"), h + 1)
                    act.activation(wgt[h % 2][:, :], wgt[h % 2][:, :], ACT.Exp).then_inc(sem("st_w"), 1)
                if h >= 1:
                    r = (h - 1) % 2 * HD
                    act.wait_ge(sem("st_pv"), h)
                    act.activation(attn[r:r + HD, (h - 1) // 2, :], lin_bank[3][r:r + HD, :], ACT.Copy)\
                       .then_inc(sem("st_o"), 1)
                if h == HEADS - 1:
                    for k in range(CT):
                        act.wait_ge(sem("ln_xc"), k + 1)
                        act.activation(ln_sq[:, k, :], cacc[:, k, :], ACT.Square).then_inc(sem("ln_sq"), 1)
            act.wait_ge(sem("ln_var"), 1)
            act.activation(ln_std[:, :], att_bank[3][:, :], ACT.Sqrt, bias=eps[:, 0:1], scale=1.0 / CW)\
               .then_inc(sem("ln_std"), 1)
            act.wait_ge(sem("st_o"), HEADS)
            for k in range(CT):
                act.activation(xh[:, k, :], attn[:, k, :], ACT.Copy).then_inc(sem("mix1_hi"), 1)
            for k in range(CT):
                act.wait_ge(sem("ln_y"), k + 1)
                act.activation(cacc[:, k, :], cacc[:, k, :], ACT.Silu, bias=col("ln_b", k), scale=col("ln_g", k))\
                   .then_inc(sem("ln_c"), 1)
                act.wait_ge(sem("ln_c"), k + 1)
                act.activation(xh[:, CT + k, :], cacc[:, k, :], ACT.Copy).then_inc(sem("mix1_hi"), 1)
            splits_and_squares(act, "out1")
            norm_act(act, "n2", nrm2, norm_stat2, xh, S)
            j = 0
            for half in range(2):
                up, down = LAYER[f"up{half}"], LAYER[f"down{half}"]
                for b in range(FHALF[half]):
                    act.wait_ge(sem("ff_conv"), j + 1)
                    act.activation(f_silu[j % 2][:, :], f_conv[j % 2][:, :], ACT.Silu).then_inc(sem("ff_silu"), 1)
                    act.wait_ge(sem("bank_free"), 4 + up["tile"] + 2 * (b + 1))
                    act.activation(fh[:, b, :], f_out[j % 2][:, :], ACT.Copy).then_inc(sem("ff_hi"), 1)
                    split_hi(act, up["block"] + b + 2)
                    j += 1
                if half:
                    splits_and_squares(act, "down1")
                else:
                    for b in range(8):
                        split_hi(act, down["block"] + b + 2)

        def block1_pool(pool):
            split_lo(pool, 0)
            norm_pool(pool, "n1", nrm1, xh, xl, S)
            for b in range(1, LAYER["out1"]["block"] + 2):
                split_lo(pool, b)
            wait(pool, ("bank_free", 4 + 16), ("params_loaded", 16))
            conv_pool(pool)
            for b in range(LAYER["out1"]["block"] + 2, LAYER["up0"]["block"] + 2):
                split_lo(pool, b)
            norm_pool(pool, "n2", nrm2, xh, xl, S)
            j = 0
            for half in range(2):
                up, down = LAYER[f"up{half}"], LAYER[f"down{half}"]
                for b in range(FHALF[half]):
                    pool.wait_ge(sem("ff_hi"), j + 1)
                    pool.tensor_tensor(fl[:, b, :], f_out[j % 2][:, :], fh[:, b, :].bitcast(F32), ALU.subtract)\
                        .then_inc(sem("ff_lo"), 1)
                    split_lo(pool, up["block"] + b + 2)
                    j += 1
                for b in range(8):
                    split_lo(pool, down["block"] + b + 2)

        def block1_pe(pe):
            wait(pe, ("consts", N_CONST))
            norm_pe(pe, "n1", nrm1, norm_diag1, S)
            linear_pe(pe, "in_fm", weights_first("in_fm", xh, xl), S, follow_norm(pe, "n1"))
            linear_pe(pe, "in_v", tokens_first("in_v", xh, xl), 256)
            for j in range(8):
                pe.wait_ge(sem("qk_sq"), j + 1)
                last = pe.matmul(att_bank[0][0:16, :], head_sum[:, j, :], qk_sq[:, j, :], start=(j == 0), stop=(j == 7))
            last.then_inc(sem("qk_sum"), 1)
            pe.wait_ge(sem("qk_rstd"), 1)
            for j in range(8):
                if j >= 2:
                    pe.wait_ge(sem("qk_ready"), j - 1)
                pe.matmul(att_bank[1 + j % 2][:, :], head_spread[:, j * P:(j + 1) * P], rstd16[:, :],
                          start=True, stop=True).then_inc(sem("qk_spread"), 1)

            def scores(h):
                r, t = h % 2 * HD, h // 2
                pe.wait_ge(sem("qk_ready"), 8)
                if h >= 1:
                    pe.wait_ge(sem("st_zread"), h)
                for kb in range(QT):
                    b, c, w = regions(kb)
                    last = pe.matmul(att_bank[b][:, c:c + w], qk[r:r + HD, 4 + t, kb * P:(kb + 1) * P],
                                     qk[r:r + HD, t, kb * P:S], start=True, stop=True)
                last.then_inc(sem("st_z"), 1)

            def tails(h):
                pe.wait_ge(sem("st_soft"), h + 1)
                if h >= 1:
                    pe.wait_ge(sem("st_logw"), h)
                else:
                    pe.wait_ge(sem("bank_free"), 4 + LAYER["in_v"]["tile"] + 8)
                for kb in range(QT):
                    b, c, w = regions(kb)
                    for jb in range(kb, QT):
                        wj = S - jb * P
                        last = pe.matmul(lin_bank[b][:, c + w - wj:c + w], later_key[:, :] if jb == kb else ones[:, :],
                                         soft[h % 2][:, KOFF[jb]:KOFF[jb] + wj], start=(jb == kb), stop=(jb == QT - 1))
                last.then_inc(sem("st_tail"), 1)

            def values(h):
                r = h % 2 * HD
                pe.wait_ge(sem("st_wm"), h + 1)
                if h >= 2:
                    pe.wait_ge(sem("st_o"), h - 1)
                for kb in range(QT):
                    last = pe.matmul(lin_bank[3][r:r + HD, kb * P:S], vtok[:, kb, h * HD:(h + 1) * HD],
                                     wgt[h % 2][:, KOFF[kb]:KOFF[kb] + S - kb * P], start=(kb == 0), stop=(kb == QT - 1))
                last.then_inc(sem("st_pv"), 1)

            def mean():
                conv_done(pe)
                for k in range(CT):
                    last = pe.matmul(att_bank[3][:, :], ones[:, :], cacc[:, k, :], start=(k == 0), stop=(k == CT - 1))
                last.then_inc(sem("ln_mean"), 1)

            def variance():
                pe.wait_ge(sem("ln_xc"), CT)
                for k in range(CT):
                    pe.wait_ge(sem("ln_sq"), k + 1)
                    last = pe.matmul(att_bank[3][:, :], ones[:, :], ln_sq[:, k, :], start=(k == 0), stop=(k == CT - 1))
                last.then_inc(sem("ln_var"), 1)

            scores(0)
            for h in range(HEADS + 1):
                if h + 1 < HEADS:
                    scores(h + 1)
                if h < HEADS:
                    tails(h)
                if h == HEADS:
                    variance()
                if h >= 1:
                    values(h - 1)
                if h == HEADS - 1:
                    mean()
            linear_pe(pe, "out1", weights_first("out1", xh, xl), S, follow(pe, "mix1_lo"))
            norm_pe(pe, "n2", nrm2, norm_diag2, S)
            done = 0
            for half in range(2):
                linear_pe(pe, f"up{half}", weights_first(f"up{half}", xh, xl), S,
                          None if half else follow_norm(pe, "n2"))
                done += FHALF[half]
                pe.wait_ge(sem("ff_lo"), done)
                linear_pe(pe, f"down{half}", weights_first(f"down{half}", fh, fl), S)

        def add_to_resid(dve, name, norm=None):
            for n in range(KD):
                bank = tile_ready(dve, name, n)
                dve.tensor_tensor(resid[:, n, :], bank[:, :], resid[:, n, :], ALU.add).then_inc(sem("bank_free"), 1)
                if norm and n >= 2:
                    add_squares(dve, norm, nrm2, S, n - 1)
            if norm:
                add_squares(dve, norm, nrm2, S, KD - 1)

        def block1_dve(dve, chain):
            wait(dve, ("params_loaded", 16), ("x_loaded0", 16), ("x_loaded1", 16))
            chain.link(dve.tensor_scalar(qg[:, :], col("q_norm"), HD ** -0.5, None, ALU.mult))
            for k in range(1, KD):
                add_squares(dve, "n1", nrm1, S, k)
            norm_dve(dve, chain, "n1", resid, nrm1, norm_stat1, norm_diag1, xh, xl, "norm1", S)
            for n in range(8):
                bank = tile_ready(dve, "in_fm", n)
                dve.tensor_copy(qk[:, n, :], bank[:, :]).then_inc(sem("bank_free"), 1)
            for j in range(CT):
                bank = tile_ready(dve, "in_fm", 8 + 2 * j)
                dve.wait_ge(sem("glu_sig"), j + 1)
                dve.tensor_tensor(cpad[:, j, TAPS - 1:], bank[:, :], glu_sig[j % 2][:, :], ALU.mult)\
                   .then_inc(sem("bank_free"), 2)
            for n in range(8):
                bank = tile_ready(dve, "in_v", n)
                dve.tensor_copy(vtok[:, n % QT, n // QT * 256:(n // QT + 1) * 256], bank[:, :256])\
                   .then_inc(sem("bank_free"), 1)
            dve.wait_ge(sem("qk_std"), 1)
            dve.reciprocal(rstd16[:, :], std16[:, :]).then_inc(sem("qk_rstd"), 1)
            for j in range(8):
                dve.wait_ge(sem("qk_spread"), j + 1)
                gain = qg[:, 0:1] if j < 4 else col("k_norm")
                dve.scalar_tensor_tensor(out=qk[:, j, :], in0=qk[:, j, :], scalar=gain, in1=att_bank[1 + j % 2][:, :],
                                         op0=ALU.mult, op1=ALU.mult).then_inc(sem("qk_ready"), 1)

            def mask_diagonals(x):
                for part in (x[:, :2 * S].rearrange("p (b c) -> p b c", b=2)[:, :, :P],
                             x[:, KOFF[3]:KOFF[2] + P].rearrange("p (b c) -> p b c", b=2)):
                    ins = dve.tensor_tensor(part, part, causal[:, :].unsqueeze(1).to_broadcast([P, 2, P]), ALU.mult)
                return ins

            def softplus(h):
                dve.wait_ge(sem("st_ln"), h + 1)
                if h >= 2:
                    dve.wait_ge(sem("st_tail"), h - 1)
                for b, (off, w) in enumerate(PIECES):
                    ins = dve.scalar_tensor_tensor(out=soft[h % 2][:, off:off + w], in0=att_bank[b][:, :w], scalar=0.0,
                                                   in1=ln1[:, off:off + w], op0=ALU.max, op1=ALU.add)
                for b, (off, w) in enumerate(PIECES):
                    ins = dve.scalar_tensor_tensor(out=lbeta[h % 2][:, off:off + w], in0=att_bank[b][:, :w], scalar=0.0,
                                                   in1=ln1[:, off:off + w], op0=ALU.min, op1=ALU.subtract)
                ins.then_inc(sem("st_zread"), 1)
                dve.wait_ge(sem("st_zread"), h + 1)
                mask_diagonals(soft[h % 2]).then_inc(sem("st_soft"), 1)

            def log_weights(h):
                dve.wait_ge(sem("st_tail"), h + 1)
                dve.wait_ge(sem("st_zread"), h + 1)
                if h >= 2:
                    dve.wait_ge(sem("st_pv"), h - 1)
                for b, (off, w) in enumerate(PIECES):
                    ins = dve.tensor_tensor(wgt[h % 2][:, off:off + w], lbeta[h % 2][:, off:off + w],
                                            lin_bank[b][:, :w], ALU.subtract)
                ins.then_inc(sem("st_logw"), 1)

            softplus(0)
            per_head = -(-N_CONV // (HEADS - 1))
            for h in range(HEADS + 1):
                conv_dve(dve, h * per_head, (h + 1) * per_head)
                if h >= 1:
                    dve.wait_ge(sem("st_w"), h)
                    mask_diagonals(wgt[(h - 1) % 2]).then_inc(sem("st_wm"), 1)
                if h < HEADS:
                    log_weights(h)
                if h + 1 < HEADS:
                    softplus(h + 1)
                if h == HEADS - 1:
                    conv_done(dve)
                    dve.wait_ge(sem("ln_mean"), 1)
                    for k in range(CT):
                        dve.scalar_tensor_tensor(out=cacc[:, k, :], in0=att_bank[3][:, :], scalar=-1.0 / CW, in1=cacc[:, k, :],
                                                 op0=ALU.mult, op1=ALU.add).then_inc(sem("ln_xc"), 1)
            def mixed_low(k):
                src = attn[:, k, :] if k < CT else cacc[:, k - CT, :]
                dve.wait_ge(sem("mix1_hi"), k + 1)
                dve.tensor_tensor(xl[:, k, :], src, xh[:, k, :].bitcast(F32), ALU.subtract).then_inc(sem("mix1_lo"), 1)

            dve.wait_ge(sem("ln_std"), 1)
            chain.link(dve.reciprocal(ln_rstd[:, :], ln_std[:, :]))
            for k in range(CT):
                dve.tensor_tensor(cacc[:, k, :], cacc[:, k, :], ln_rstd[:, :], ALU.mult).then_inc(sem("ln_y"), 1)
                mixed_low(k)
            for k in range(CT, KD):
                mixed_low(k)
            add_to_resid(dve, "out1", "n2")
            norm_dve(dve, chain, "n2", resid, nrm2, norm_stat2, norm_diag2, xh, xl, "norm2", S)
            j = 0
            for half in range(2):
                for b in range(FHALF[half]):
                    gate = tile_ready(dve, f"up{half}", 2 * b)
                    y = f_conv[j % 2]

                    def tap(k):
                        return col("ffn_w", j * FTAPS + k)
                    chain.link(dve.tensor_scalar(y[:, :], gate[:, :], tap(2), col("ffn_b", j), ALU.mult, ALU.add))
                    chain.link(dve.scalar_tensor_tensor(out=y[:, 1:], in0=gate[:, :S - 1], scalar=tap(1), in1=y[:, 1:],
                                                        op0=ALU.mult, op1=ALU.add))
                    dve.scalar_tensor_tensor(out=y[:, 2:], in0=gate[:, :S - 2], scalar=tap(0), in1=y[:, 2:],
                                             op0=ALU.mult, op1=ALU.add).then_inc(sem("ff_conv"), 1)
                    value = tile_ready(dve, f"up{half}", 2 * b + 1)
                    dve.wait_ge(sem("ff_silu"), j + 1)
                    if j >= 2:
                        dve.wait_ge(sem("ff_lo"), j - 1)
                    dve.tensor_tensor(f_out[j % 2][:, :], value[:, :], f_silu[j % 2][:, :], ALU.mult)\
                       .then_inc(sem("bank_free"), 2)
                    j += 1
                add_to_resid(dve, f"down{half}", "n3" if half else None)

        N_CONST = 21

        def make_consts(pool):
            done = [0]

            def step(ins):
                done[0] += 1
                ins.then_inc(sem("consts"), 1)
                pool.wait_ge(sem("consts"), done[0])

            pool.nop().then_inc(sem("bank_free"), 4)
            pool.nop().then_inc(sem("lo_done"), 2)
            peer_credits(pool)
            step(pool.memset(eps[:, :], EPS))
            step(pool.memset(ones[:, :], 1.0))
            step(pool.memset(head_sum[:, :, :], 0.0))
            step(pool.memset(head_spread[:, :], 1.0))
            step(pool.memset(cpad[:, :, 0:TAPS - 1], 0.0))
            step(pool.memset(cmp_valid[:, :, :], 1.0))
            step(pool.iota(iota16[:, :], [[1, PK]], base=0, channel_multiplier=0, allow_small_or_imprecise_dtypes=True))
            step(pool.iota(iota_key[:, :], [[1, NK]], base=0, channel_multiplier=0,
                           allow_small_or_imprecise_dtypes=True))
            step(pool.iota(dist[:, :], [[1, S]], base=P - S, channel_multiplier=-1,
                           allow_small_or_imprecise_dtypes=True))
            step(pool.iota(cmp_dist[:, :, :], [[-P, QT], [CMP, NCMP]], base=CMP - 1, channel_multiplier=-1,
                           allow_small_or_imprecise_dtypes=True))
            step(pool.memset(ident[:, :], 0.0))
            step(pool.affine_select(out=ident[:, :], in_=ident[:, :], compare_op=ALU.not_equal, fill=1.0, base=0,
                                    pattern=[[-1, P]], channel_multiplier=1))
            step(pool.affine_select(out=later_key[:, :], in_=ones[:, :], compare_op=ALU.is_gt, fill=0.0, base=0,
                                    pattern=[[-1, P]], channel_multiplier=1))
            step(pool.affine_select(out=causal[:, :], in_=ones[:, :], compare_op=ALU.is_gt, fill=0.0, base=0,
                                    pattern=[[1, P]], channel_multiplier=-1))
            step(pool.affine_select(out=dist[:, :], in_=dist[:, :], compare_op=ALU.is_ge, fill=NEG, base=S - P,
                                    pattern=[[-1, S]], channel_multiplier=1))
            step(pool.affine_select(out=cmp_dist[:, :, :], in_=cmp_dist[:, :, :], compare_op=ALU.is_ge, fill=NEG,
                                    base=1 - CMP, pattern=[[P, QT], [-CMP, NCMP]], channel_multiplier=1))
            step(pool.affine_select(out=cmp_valid[:, :, :], in_=cmp_valid[:, :, :], compare_op=ALU.is_ge, fill=0.0,
                                    base=1 - CMP, pattern=[[P, QT], [-CMP, NCMP]], channel_multiplier=1))
            sums = head_sum[:, :, :].rearrange("p j c -> p (j c)")
            step(pool.memset(sums[0:HD, 0:P:18], 1.0))
            step(pool.memset(sums[HD:P, 1:P:18], 1.0))
            step(pool.affine_select(out=head_spread[:, :], in_=head_spread[:, :], compare_op=ALU.is_ge, fill=0.0, base=0,
                                    pattern=[[1, 8 * P]], channel_multiplier=-HD))
            step(pool.affine_select(out=head_spread[:, :], in_=head_spread[:, :], compare_op=ALU.is_ge, fill=0.0,
                                    base=HD - 1, pattern=[[-1, 8 * P]], channel_multiplier=HD))
            assert done[0] == N_CONST

        def scr(kb):
            return SCR + int(kb * KB)

        qa = at("qa", [P, DA_H, S], scr(0))
        ka = at("ka", [P, DA_H, S], scr(8))
        qb = at("qb", [P, NSA_H // 2, S], scr(16))
        ks = [at(f"ks{i}", [P, S], scr(24 + 2 * i)) for i in range(2)]
        kw = [at(f"kw{i}", [P, S], scr(28 + 2 * i)) for i in range(2)]
        va = at("va", [P, QT, AW], scr(32))
        vsw = at("vsw", [P, QT, 256], scr(40))
        cmp_in = [at(f"cmp_in{i}", [P, CMP // 2, NSA_G, NCMP], scr(44 + 2 * i)) for i in range(2)]
        slope_dist = [at(f"slope_dist{i}", [P, S], scr(44 + 2 * i)) for i in range(2)]
        cmp_hid = [at(f"cmp_hid{i}", [P, 2, NSA_G * NCMP], scr(48 + 0.25 * i)) for i in range(2)]
        kc_t = at("kc_t", [P, NSA_G * NCMP], scr(48.5))
        cmp_stat = at("cmp_stat", [P, QT, NSA_H], scr(48.75))
        cmp_rec = at("cmp_rec", [P, QT, NSA_H], scr(48.875))
        vc_blk = at("vc_blk", [P, NSA_H, HD], scr(49))
        cmp_bias = at("cmp_bias", [P, QT, NSA_H, NCMP], scr(51))
        cmp_s = at("cmp_s", [P, QT, NSA_H, NCMP], scr(53))
        cmp_p = at("cmp_p", [P, QT, NSA_H, 32], scr(55))
        cmp_pt = at("cmp_pt", [P, QT, NSA_G, P], scr(51))
        cmp_w1 = [at(f"cmp_w1_{i}", [P, CMP // 2, CMP_HID], scr(60 + 16 * i)) for i in range(2)]
        cmp_w2 = [at(f"cmp_w2_{i}", [P, 2, HD], scr(92 + 0.5 * i)) for i in range(2)]
        att_e = [at(f"att_e{i}", [P, 2, S], scr(x)) for i, x in enumerate((60, 64, 68, 55))]
        att_pt = [at(f"att_pt{i}", [P, 2, S], scr(72 + 4 * i)) for i in range(2)]
        oab = at("oab", [P, KD, S], scr(80))
        stat = at("att_stat", [P, 4, 4, 2], scr(96))
        sub_sq = at("sub_sq", [P, DA_H, S], scr(60))
        sub_std = at("sub_std", [P, DA_H, S], scr(68))
        sig = at("sig", [P, 2 * KD, S], scr(0))
        oh = at("oh", [P, KD, S], scr(32), F32R)
        ol = at("ol", [P, KD, S], scr(48), F32R)
        part_a = [at(f"part_a{i}", [P, S], scr(64 + 2 * i)) for i in range(2)]
        part_b = [at(f"part_b{i}", [P, S], scr(68 + 2 * i)) for i in range(2)]
        mem = at("mem", [P, KD, MEM], scr(0))
        mem_n = at("mem_n", [P, KD, MEM], scr(8))
        mem_stat = at("mem_stat", [P, 2 * QT], scr(16))
        mem_diag = at("mem_diag", [P, MEM], scr(17))
        mem_h = at("mem_h", [P, KD, MEM], scr(18), F32R)
        mem_l = at("mem_l", [P, KD, MEM], scr(26), F32R)
        cq = at("cq", [P, CA_H, S], scr(34))
        ck = at("ck", [P, CA_H, MEM], scr(42))
        cv = at("cv", [P, MEM // P, CA_H * P], scr(46))
        ca_e = [at(f"ca_e{i}", [P, MEM], scr(50 + i)) for i in range(4)]
        ca_pt = [at(f"ca_pt{i}", [P, MEM], scr(54 + i)) for i in range(2)]
        ca_stat = at("ca_stat", [P, 4, 4], scr(56))

        CA_SCALE = (CA_H * P // CA_H) ** -0.5
        MIXED = LAYER["mix_tm"]["tile"] + 16

        UNITS = [("a", h, i) for h in range(DA_H) for i in range(QT)] + [("b", h, i) for h in range(NSA_H) for i in range(QT)]
        N_A = DA_H * QT
        NU = len(UNITS)

        def items(u):
            return [u] if u < N_A else [N_A + 2 * (u - N_A), N_A + 2 * (u - N_A) + 1]

        def head_no(u):
            return u // QT

        def unit_maps(u):
            kind, h, i = UNITS[u]
            if kind == "a":
                return [(qa[c * HD:(c + 1) * HD, h, i * P:(i + 1) * P], ka[c * HD:(c + 1) * HD, h, :]) for c in range(2)]
            r = h % 2 * HD
            swap = 0 if h // NSA_R == h % 2 else 1
            q = qb[r:r + HD, h // 2, i * P:(i + 1) * P]
            return [(q, ks[swap][r:r + HD, :]), (q, kw[swap][r:r + HD, :])]

        def slope(u):
            kind, h, _ = UNITS[u]
            return 2.0 ** (-8.0 * (h + 1) / (DA_H if kind == "a" else NSA_H))

        def block2_pool(pool):
            norm_pool(pool, "n3", nrm2, xh, xl, S)
            norm_done(pool, "n3")
            pool.memset(vc_blk[:, :, :], 0.0).then_inc(sem("cmp_zero"), 1)
            pool.memset(cmp_p[:, :, :, :], 0.0).then_inc(sem("cmp_zero"), 1)
            for b in range(LAYER["mix_fm"]["block"] + 2, LAYER["cross_q"]["block"] + 2):
                split_lo(pool, b)
            norm_pool(pool, "n4", nrm2, xh, xl, S)
            for b in range(LAYER["cross_q"]["block"] + 2, LAYER["cross_k"]["block"] + 2):
                split_lo(pool, b)
            norm_pool(pool, "nm", mem_n, mem_h, mem_l, MEM)
            for b in range(LAYER["cross_k"]["block"] + 2, LAYER["peer_q"]["block"] + 2):
                split_lo(pool, b)

        def block2_act(act):
            def splits(name, first=0, last=None):
                t = LAYER[name]
                for b in range(first, t["nb"] if last is None else last):
                    split_hi(act, t["block"] + b + 2)

            norm_act(act, "n3", nrm2, norm_stat2, xh, S)
            splits("mix_fm")
            splits("mix_tm", 0, 3)
            act.wait_ge(sem("bank_free"), 4 + LAYER["mix_tm"]["tile"] + 3 * QT)
            for n in range(QT):
                bank = tile_ready(act, "mix_tm", 3 * QT + n)
                act.activation(gates24[:, n, :], bank[:, :NSA_H * 3], ACT.Sigmoid).then_inc(sem("bank_free"), 1)
            splits("mix_tm", 3)
            act.wait_ge(sem("lam_sum"), 1)
            act.activation(lam_exp[:, :], att_bank[3][:, 0:2], ACT.Exp).then_inc(sem("lam_exp"), 1)
            for v in range(2):
                act.wait_ge(sem("cmp_h"), v + 1)
                act.activation(cmp_hid[v][:, :, :].rearrange("p m n -> p (m n)"), att_bank[v][:, 0:2 * NSA_G * NCMP],
                               ACT.Gelu).then_inc(sem("cmp_hid"), 1)
            act.wait_ge(sem("cmp_sub"), 1)
            act.activation(cmp_s[:, :, :, :], cmp_s[:, :, :, :], ACT.Exp).then_inc(sem("cmp_exp"), 1)

            def exps(u):
                w = (UNITS[u][2] + 1) * P
                act.wait_ge(sem("at_nm"), u + 1)
                for c in range(2):
                    e = att_e[u % 4][:, c, :w]
                    act.activation(e, e, ACT.Exp, bias=stat[:, u % 4, 1, c:c + 1],
                                   accum_out=stat[:, u % 4, 2, c:c + 1]).then_inc(sem("at_exp"), 1)

            def transposed(u):
                w = (UNITS[u][2] + 1) * P
                if u >= 2:
                    act.wait_ge(sem("at_pv"), u - 1)
                for c, n in enumerate(items(u)):
                    act.wait_ge(sem("at_t"), n + 1)
                    act.activation(att_pt[u % 2][:, c, :w], lin_bank[n % 2][:, :w], ACT.Copy).then_inc(sem("at_pt"), 1)

            def outputs(u):
                kind, h, i = UNITS[u]
                if i < QT - 1:
                    return
                act.wait_ge(sem("at_pv"), u + 1)
                bank = lin_bank[2 + head_no(u) % 2]
                if kind == "a":
                    ins = act.activation(oab[:, h, :], bank[:, :], ACT.Copy)
                else:
                    r = h % 2 * HD
                    ins = act.activation(oab[r:r + HD, DA_H + h // 2, :], bank[r:r + HD, :], ACT.Copy)
                ins.then_inc(sem("at_o"), 1)

            for s in range(NU + 3):
                if s < NU:
                    exps(s)
                if 2 <= s <= NU + 1:
                    transposed(s - 2)
                if s >= 3:
                    outputs(s - 3)
            for h in range(DA_H):
                act.activation(sub_sq[:, h, :], oab[:, h, :], ACT.Square).then_inc(sem("sub_sq"), 1)
            for h in range(DA_H):
                act.wait_ge(sem("sub_sum"), h + 1)
                act.activation(sub_std[:, h, :], att_bank[h][:, :], ACT.Sqrt, bias=eps[:, 0:1], scale=1.0 / P)\
                   .then_inc(sem("sub_std"), 1)
            for k in range(KD):
                if k < DA_H:
                    act.wait_ge(sem("sub_y"), k + 1)
                act.activation(oh[:, k, :], oab[:, k, :], ACT.Copy).then_inc(sem("oab_hi"), 1)
            for b in range(8):
                for n in range(2):
                    bank = tile_ready(act, "gates", 2 * b + n)
                    act.activation(sig[:, 2 * b + n, :], bank[:, :], ACT.Sigmoid).then_inc(sem("bank_free"), 1)
                split_hi(act, LAYER["gates"]["block"] + b + 2)
            for m in range(KD):
                act.wait_ge(sem("br_sum"), m + 1)
                act.activation(xh[:, m, :], part_a[m % 2][:, :], ACT.Copy).then_inc(sem("br_hi"), 1)
                if m % 2:
                    split_hi(act, LAYER["branch"]["block"] + m // 2 + 2)
            splits_and_squares(act, "out2")
            norm_act(act, "n4", nrm2, norm_stat2, xh, S)
            act.wait_ge(sem("mem_loaded"), 16)
            squares(act, mem, mem_n, MEM)
            splits("cross_q")
            norm_act(act, "nm", mem_n, mem_stat, mem_h, MEM)
            splits("cross_k")
            splits("cross_v")

            def ca_exp(u):
                act.wait_ge(sem("ca_nm"), u + 1)
                act.activation(ca_e[u % 4][:, :], att_bank[u % 4][:, :MEM], ACT.Exp, bias=ca_stat[:, u % 4, 1:2],
                               scale=CA_SCALE, accum_out=ca_stat[:, u % 4, 2:3]).then_inc(sem("ca_exp"), 1)

            def ca_transposed(u):
                if u >= 2:
                    act.wait_ge(sem("ca_pv"), u - 1)
                act.wait_ge(sem("ca_t"), u + 1)
                act.activation(ca_pt[u % 2][:, :], lin_bank[u % 2][:, :MEM], ACT.Copy).then_inc(sem("ca_pt"), 1)

            for s in range(CA_H * QT + 3):
                if s < CA_H * QT:
                    ca_exp(s)
                if 2 <= s <= CA_H * QT + 1:
                    ca_transposed(s - 2)
                u = s - 3
                if u >= 0 and u % QT == QT - 1:
                    h = u // QT
                    act.wait_ge(sem("ca_pv"), u + 1)
                    act.activation(xh[:, h, :], lin_bank[2 + h % 2][:, :], ACT.Copy).then_inc(sem("ca_hi"), 1)
            splits_and_squares(act, "cross_o")

        def block2_pe(pe):
            norm_pe(pe, "n3", nrm2, norm_diag2, S)
            pe.wait_ge(sem("lam_prod"), 1)
            pe.matmul(att_bank[3][:, 0:2], ones[0:HD, :], lam_prod[0:HD, :], start=True, stop=True)\
              .then_inc(sem("lam_sum"), 1)
            linear_pe(pe, "mix_fm", weights_first("mix_fm", xh, xl), S, follow_norm(pe, "n3"))
            linear_pe(pe, "mix_tm", tokens_first("mix_tm", xh, xl), 256)
            wait(pe, ("cmp_loaded", 64), ("cmp_in", 8))
            NC2 = NSA_G * NCMP
            for v in range(2):
                for m in range(2):
                    for lp in range(CMP // 2):
                        last = pe.matmul(att_bank[v][:, m * NC2:(m + 1) * NC2], cmp_w1[v][:, lp, m * P:(m + 1) * P],
                                         cmp_in[v][:, lp, :, :].rearrange("p g b -> p (g b)"),
                                         start=(lp == 0), stop=(lp == CMP // 2 - 1))
                last.then_inc(sem("cmp_h"), 1)
            pe.wait_ge(sem("cmp_hid"), 1)
            for m in range(2):
                last = pe.matmul(att_bank[2][0:HD, 0:NC2], cmp_w2[0][:, m, :], cmp_hid[0][:, m, :],
                                 start=(m == 0), stop=(m == 1))
            last.then_inc(sem("cmp_k"), 1)
            pe.wait_ge(sem("cmp_hid"), 2)
            pe.wait_ge(sem("lam_exp"), 1)
            for g in range(NSA_G):
                for m in range(2):
                    last = pe.matmul(att_bank[3][0:NCMP, g * HD:(g + 1) * HD], cmp_hid[1][:, m, g * NCMP:(g + 1) * NCMP],
                                     cmp_w2[1][:, m, :], start=(m == 0), stop=(m == 1))
            last.then_inc(sem("cmp_v"), 1)
            pe.wait_ge(sem("cmp_kc"), 2)
            for i in range(QT):
                for h in range(NSA_H):
                    r, g = h % 2 * HD, h // NSA_R
                    n = (i * NSA_H // 2 + h // 2) * NCMP
                    last = pe.matmul(att_bank[h % 2][:, n:n + NCMP], qb[r:r + HD, h // 2, i * P:(i + 1) * P],
                                     kc_t[r:r + HD, g * NCMP:(g + 1) * NCMP], start=True, stop=True)
            last.then_inc(sem("cmp_scores"), 1)
            pe.wait_ge(sem("cmp_p"), 1)
            for i in range(QT):
                for g in range(NSA_G):
                    n = i * NSA_G + g
                    src = cmp_p[:, i, g * NSA_R:(g + 1) * NSA_R, :].rearrange("p h c -> p (h c)")
                    last = pe.transpose(att_bank[1 + n // 4][:, n % 4 * P:(n % 4 + 1) * P], src, ident[:, :])
            last.then_inc(sem("cmp_t"), 1)

            def scores(u):
                w = (UNITS[u][2] + 1) * P
                for c, (q, k) in enumerate(unit_maps(u)):
                    if u >= 2:
                        pe.wait_ge(sem("at_max"), 2 * (u - 2) + c + 1)
                    pe.matmul(att_bank[2 * (u % 2) + c][:, :w], q, k[:, :w], start=True, stop=True)\
                      .then_inc(sem("at_s"), 1)

            def transposes(u):
                for c, n in enumerate(items(u)):
                    pe.wait_ge(sem("at_p"), n + 1)
                    if n >= 2:
                        pe.wait_ge(sem("at_pt"), n - 1)
                    for kb in range(UNITS[u][2] + 1):
                        last = pe.transpose(lin_bank[n % 2][:, kb * P:(kb + 1) * P],
                                            att_e[u % 4][:, c, kb * P:(kb + 1) * P], ident[:, :])
                    last.then_inc(sem("at_t"), 1)

            def values(u):
                kind, h, i = UNITS[u]
                pe.wait_ge(sem("at_pt"), items(u)[-1] + 1)
                if i == 0 and head_no(u) >= 2:
                    pe.wait_ge(sem("at_o"), head_no(u) - 1)
                bank = lin_bank[2 + head_no(u) % 2]
                if kind == "a":
                    out = bank[:, i * P:(i + 1) * P]
                    ops = [(va[:, kb, h * P:(h + 1) * P], att_pt[u % 2][:, 0, kb * P:(kb + 1) * P]) for kb in range(i + 1)]
                else:
                    r, g = h % 2 * HD, h // NSA_R
                    out = bank[r:r + HD, i * P:(i + 1) * P]
                    ops = [(vc_blk[:, h, :], cmp_pt[:, i, g, :])]
                    ops += [(vsw[:, kb, c * P + g * HD:c * P + (g + 1) * HD], att_pt[u % 2][:, c, kb * P:(kb + 1) * P])
                            for c in range(2) for kb in range(i + 1)]
                for n, (v, p) in enumerate(ops):
                    last = pe.matmul(out, v, p, start=(n == 0), stop=(n == len(ops) - 1))
                last.then_inc(sem("at_pv"), 1)

            wait(pe, ("bank_free", 4 + MIXED), ("cmp_pt", 2))
            for s in range(NU + 3):
                if s < NU:
                    scores(s)
                if 2 <= s <= NU + 1:
                    transposes(s - 2)
                if s >= 3:
                    values(s - 3)
            pe.wait_ge(sem("at_max"), 2 * NU)
            for h in range(DA_H):
                pe.wait_ge(sem("sub_sq"), h + 1)
                pe.matmul(att_bank[h][:, :], ones[:, :], sub_sq[:, h, :], start=True, stop=True)\
                  .then_inc(sem("sub_sum"), 1)
            pe.wait_ge(sem("at_o"), DA_H + NSA_H)
            linear_pe(pe, "gates", weights_first("gates", xh, xl), S)
            pe.wait_ge(sem("oab_lo"), KD)

            def branch_pairs(slot, m):
                half, out = m % 2, m // 2
                ks_ = range(4 * half, 4 * half + 4)
                return [(wh[slot][:, k * 256 + out * P:k * 256 + out * P + P],
                         wl[slot][:, k * 256 + out * P:k * 256 + out * P + P], oh[:, k, :], ol[:, k, :]) for k in ks_]

            linear_pe(pe, "branch", branch_pairs, S)
            linear_pe(pe, "out2", weights_first("out2", xh, xl), S, follow(pe, "br_lo"))
            norm_pe(pe, "n4", nrm2, norm_diag2, S)
            linear_pe(pe, "cross_q", weights_first("cross_q", xh, xl), S, follow_norm(pe, "n4"))
            norm_pe(pe, "nm", mem_n, mem_diag, MEM)
            linear_pe(pe, "cross_k", weights_first("cross_k", mem_h, mem_l, MEM), MEM, follow_norm(pe, "nm"))
            linear_pe(pe, "cross_v", tokens_first("cross_v", mem_h, mem_l), 256)
            pe.wait_ge(sem("bank_free"), 4 + LAYER["cross_o"]["tile"])
            n_ca = CA_H * QT
            for s in range(n_ca + 3):
                if s < n_ca:
                    h, i = s // QT, s % QT
                    if s >= 4:
                        pe.wait_ge(sem("ca_exp"), s - 3)
                    pe.matmul(att_bank[s % 4][:, :MEM], cq[:, h, i * P:(i + 1) * P], ck[:, h, :], start=True, stop=True)\
                      .then_inc(sem("ca_s"), 1)
                u = s - 2
                if 0 <= u < n_ca:
                    pe.wait_ge(sem("ca_p"), u + 1)
                    if u >= 2:
                        pe.wait_ge(sem("ca_pt"), u - 1)
                    for mt in range(MEM // P):
                        last = pe.transpose(lin_bank[u % 2][:, mt * P:(mt + 1) * P], ca_e[u % 4][:, mt * P:(mt + 1) * P],
                                            ident[:, :])
                    last.then_inc(sem("ca_t"), 1)
                u = s - 3
                if u >= 0:
                    h, i = u // QT, u % QT
                    pe.wait_ge(sem("ca_pt"), u + 1)
                    if i == 0 and h >= 2:
                        pe.wait_ge(sem("ca_lo"), h - 1)
                    for mt in range(MEM // P):
                        last = pe.matmul(lin_bank[2 + h % 2][:, i * P:(i + 1) * P], cv[:, mt, h * P:(h + 1) * P],
                                         ca_pt[u % 2][:, mt * P:(mt + 1) * P], start=(mt == 0), stop=(mt == 1))
                    last.then_inc(sem("ca_pv"), 1)
            linear_pe(pe, "cross_o", weights_first("cross_o", xh, xl), S, follow(pe, "ca_lo"))

        def block2_dve(dve, chain):
            p0 = PCOL["lam"]
            dve.tensor_tensor(lam_prod[:, :], params[:, p0:p0 + 4:2], params[:, p0 + 1:p0 + 4:2], ALU.mult)\
               .then_inc(sem("lam_prod"), 1)
            chain.link(dve.tensor_scalar(subln_g[:, :], col("subln"), 1.0 - LAMBDA_INIT, None, ALU.mult))
            norm_dve(dve, chain, "n3", resid, nrm2, norm_stat2, norm_diag2, xh, xl, "norm_mix", S)
            scale = HD ** -0.5
            for n in range(12):
                bank = tile_ready(dve, "mix_fm", n)
                out = (qa, ka, qb)[n // 4][:, n % 4, :]
                if n // 4 == 1:
                    ins = dve.tensor_copy(out, bank[:, :])
                else:
                    ins = dve.tensor_scalar(out, bank[:, :], scale, None, ALU.mult)
                ins.then_inc(sem("bank_free"), 1)
            for v in range(2):
                bank = tile_ready(dve, "mix_fm", 12 + v)
                for g in range(NSA_G):
                    rows = slice(g * HD, (g + 1) * HD)
                    tokens = bank[rows, :].rearrange("p (b l) -> p l b", l=CMP)
                    pos = params[rows, PCOL["cmp_pos"]:PCOL["cmp_pos"] + CMP]
                    for par in range(2):
                        dve.tensor_tensor(
                            cmp_in[v][par * HD:(par + 1) * HD, :, g, :], tokens[:, par::2, :],
                            pos[:, par::2].unsqueeze(2).to_broadcast([HD, CMP // 2, NCMP]), ALU.add)\
                           .then_inc(sem("cmp_in"), 1)
                dve.wait_ge(sem("cmp_in"), 4 * (v + 1))
                dve.sem_inc(sem("bank_free"), 1)
            for n, x in ((14, ks), (15, kw)):
                bank = tile_ready(dve, "mix_fm", n)
                dve.tensor_copy(x[0][:, :], bank[:, :])
                dve.tensor_copy(x[1][0:HD, :], bank[HD:P, :])
                dve.tensor_copy(x[1][HD:P, :], bank[0:HD, :]).then_inc(sem("bank_free"), 1)
            for n in range(3 * QT):
                bank = tile_ready(dve, "mix_tm", n)
                b, tt = n // QT, n % QT
                out = va[:, tt, b * 256:(b + 1) * 256] if b < 2 else vsw[:, tt, :]
                dve.tensor_copy(out, bank[:, :256]).then_inc(sem("bank_free"), 1)
            for h in range(NSA_H):
                dve.tensor_scalar(cmp_bias[:, :, h, :], cmp_dist[:, :, :], 2.0 ** -(h + 1), None, ALU.mult)
            dve.wait_ge(sem("lam_exp"), 1)
            chain.link(dve.tensor_scalar(lam[:, :], lam_exp[:, 0:1], lam_exp[:, 1:2], LAMBDA_INIT, ALU.subtract, ALU.add))
            dve.wait_ge(sem("cmp_k"), 1)
            for half in range(2):
                dve.tensor_copy(kc_t[half * HD:(half + 1) * HD, :], att_bank[2][0:HD, 0:NSA_G * NCMP])\
                   .then_inc(sem("cmp_kc"), 1)
            wait(dve, ("cmp_v", 1), ("cmp_zero", 2))
            for h in range(NSA_H):
                g, r = h // NSA_R, h % NSA_R
                ins = dve.tensor_copy(vc_blk[32 * r:32 * r + NCMP, h, :], att_bank[3][0:NCMP, g * HD:(g + 1) * HD])
            chain.link(ins)
            dve.wait_ge(sem("cmp_scores"), 1)
            flat = "p i h c -> p (i h) c"
            s3, b3 = cmp_s[:, :, :, :].rearrange(flat), cmp_bias[:, :, :, :].rearrange(flat)
            stat2, rec2 = cmp_stat[:, :, :].rearrange("p i h -> p (i h)"), cmp_rec[:, :, :].rearrange("p i h -> p (i h)")
            NIH = QT * NSA_H

            def spread(x):
                return x.unsqueeze(2).to_broadcast([P, NIH, NCMP])

            for odd in range(2):
                by_parity = "p i (h o) c -> p o (i h) c"
                ins = dve.tensor_tensor(cmp_s[:, :, :, :].rearrange(by_parity, o=2)[:, odd],
                                        att_bank[odd][:, :S // 2].rearrange("p (n c) -> p n c", c=NCMP),
                                        cmp_bias[:, :, :, :].rearrange(by_parity, o=2)[:, odd], ALU.add)
            chain.link(ins)
            chain.link(dve.tensor_reduce(stat2, s3, AX_X, ALU.max))
            dve.tensor_tensor(s3, s3, spread(stat2), ALU.subtract).then_inc(sem("cmp_sub"), 1)
            dve.wait_ge(sem("cmp_exp"), 1)
            chain.link(dve.tensor_reduce(stat2, s3, AX_X, ALU.add))
            chain.link(dve.reciprocal(rec2, stat2))
            chain.link(dve.tensor_tensor(cmp_rec[:, :, :], cmp_rec[:, :, :], gates24[:, :, 0::3], ALU.mult))
            for i in range(QT):
                ins = dve.tensor_tensor(cmp_s[:, i, :, :], cmp_s[:, i, :, :],
                                        cmp_valid[:, i, :].unsqueeze(1).to_broadcast([P, NSA_H, NCMP]), ALU.mult)
            chain.link(ins)
            padded = cmp_p[:, :, :, :].rearrange(flat)
            dve.tensor_tensor(padded[:, :, 0:NCMP], s3, spread(rec2), ALU.mult).then_inc(sem("cmp_p"), 1)
            dve.wait_ge(sem("cmp_t"), 1)
            turned = cmp_pt[:, :, :, :].rearrange("p i g t -> p (i g t)")
            for b in range(2):
                dve.tensor_copy(turned[:, b * S:(b + 1) * S], att_bank[1 + b][:, :]).then_inc(sem("cmp_pt"), 1)

            def maxima(u):
                kind, h, i = UNITS[u]
                w = (i + 1) * P
                sd = slope_dist[head_no(u) % 2]
                if i == 0:
                    chain.link(dve.tensor_scalar(sd[:, :], dist[:, :], slope(u), None, ALU.mult))
                if u >= 4:
                    dve.wait_ge(sem("at_t"), items(u - 4)[-1] + 1)
                for c in range(2):
                    dve.wait_ge(sem("at_s"), 2 * u + c + 1)
                    dve.tensor_tensor_reduce(out=att_e[u % 4][:, c, :w], in0=att_bank[2 * (u % 2) + c][:, :w],
                                             in1=sd[:, S - w:], scale=1.0, scalar=-3.0e38, op0=ALU.add, op1=ALU.max,
                                             accum_out=stat[:, u % 4, 0, c:c + 1]).then_inc(sem("at_max"), 1)
                dve.wait_ge(sem("at_max"), 2 * u + 2)
                dve.tensor_scalar(stat[:, u % 4, 1, :], stat[:, u % 4, 0, :], -1.0, None, ALU.mult).then_inc(sem("at_nm"), 1)

            def weights(u):
                kind, h, i = UNITS[u]
                w = (i + 1) * P
                e, factor = att_e[u % 4], stat[:, u % 4, 3, :]
                dve.wait_ge(sem("at_exp"), 2 * u + 2)
                chain.link(dve.reciprocal(factor, stat[:, u % 4, 2, :]))
                if kind == "a":
                    chain.link(dve.tensor_scalar(factor[:, 1:2], factor[:, 1:2], lam[:, 0:1], None, ALU.mult))
                    chain.link(dve.tensor_scalar(e[:, 1, :w], e[:, 1, :w], factor[:, 1:2], None, ALU.mult))
                    dve.scalar_tensor_tensor(out=e[:, 0, :w], in0=e[:, 0, :w], scalar=factor[:, 0:1], in1=e[:, 1, :w],
                                             op0=ALU.mult, op1=ALU.subtract).then_inc(sem("at_p"), 1)
                else:
                    chain.link(dve.tensor_tensor(factor, factor, gates24[:, i, 3 * h + 1:3 * h + 3], ALU.mult))
                    for c in range(2):
                        dve.tensor_scalar(e[:, c, :w], e[:, c, :w], factor[:, c:c + 1], None, ALU.mult)\
                           .then_inc(sem("at_p"), 1)

            for s in range(NU + 1):
                if s < NU:
                    maxima(s)
                if s >= 1:
                    weights(s - 1)
            for h in range(DA_H):
                dve.wait_ge(sem("sub_std"), h + 1)
                chain.link(dve.reciprocal(sub_std[:, h, :], sub_std[:, h, :]))
                dve.scalar_tensor_tensor(out=oab[:, h, :], in0=oab[:, h, :], scalar=subln_g[:, 0:1],
                                         in1=sub_std[:, h, :], op0=ALU.mult, op1=ALU.mult).then_inc(sem("sub_y"), 1)
            for k in range(KD):
                dve.wait_ge(sem("oab_hi"), k + 1)
                dve.tensor_tensor(ol[:, k, :], oab[:, k, :], oh[:, k, :].bitcast(F32), ALU.subtract)\
                   .then_inc(sem("oab_lo"), 1)
            dve.wait_ge(sem("bank_free"), 4 + LAYER["branch"]["tile"])
            for m in range(KD):
                a = tile_ready(dve, "branch", 2 * m)
                b = tile_ready(dve, "branch", 2 * m + 1)
                if m >= 2:
                    dve.wait_ge(sem("br_hi"), m - 1)
                dve.tensor_tensor(part_a[m % 2][:, :], a[:, :], sig[:, 2 * m, :], ALU.mult)
                dve.tensor_tensor(part_b[m % 2][:, :], b[:, :], sig[:, 2 * m + 1, :], ALU.mult)\
                   .then_inc(sem("bank_free"), 2)
                dve.wait_ge(sem("bank_free"), 4 + LAYER["branch"]["tile"] + 2 * (m + 1))
                dve.tensor_tensor(part_a[m % 2][:, :], part_a[m % 2][:, :], part_b[m % 2][:, :], ALU.add)\
                   .then_inc(sem("br_sum"), 1)
                dve.wait_ge(sem("br_hi"), m + 1)
                dve.tensor_tensor(xl[:, m, :], part_a[m % 2][:, :], xh[:, m, :].bitcast(F32), ALU.subtract)\
                   .then_inc(sem("br_lo"), 1)
            add_to_resid(dve, "out2", "n4")
            norm_dve(dve, chain, "n4", resid, nrm2, norm_stat2, norm_diag2, xh, xl, "norm_cross", S)
            for k in range(1, KD):
                add_squares(dve, "nm", mem_n, MEM, k)
            for n in range(CA_H):
                bank = tile_ready(dve, "cross_q", n)
                dve.tensor_copy(cq[:, n, :], bank[:, :]).then_inc(sem("bank_free"), 1)
            norm_dve(dve, chain, "nm", mem, mem_n, mem_stat, mem_diag, mem_h, mem_l, "norm_mem", MEM)
            for n in range(CA_H):
                bank = tile_ready(dve, "cross_k", n)
                dve.tensor_copy(ck[:, n, :], bank[:, :MEM]).then_inc(sem("bank_free"), 1)
            for n in range(4):
                bank = tile_ready(dve, "cross_v", n)
                dve.tensor_copy(cv[:, n % 2, n // 2 * 256:(n // 2 + 1) * 256], bank[:, :256]).then_inc(sem("bank_free"), 1)
            n_ca = CA_H * QT
            for s in range(n_ca + 4):
                if s < n_ca:
                    dve.wait_ge(sem("ca_s"), s + 1)
                    chain.link(dve.tensor_reduce(ca_stat[:, s % 4, 0:1], att_bank[s % 4][:, :MEM], AX_X, ALU.max))
                    if s >= 4:
                        dve.wait_ge(sem("ca_t"), s - 3)
                    dve.tensor_scalar(ca_stat[:, s % 4, 1:2], ca_stat[:, s % 4, 0:1], -CA_SCALE, None, ALU.mult)\
                       .then_inc(sem("ca_nm"), 1)
                u = s - 1
                if 0 <= u < n_ca:
                    dve.wait_ge(sem("ca_exp"), u + 1)
                    chain.link(dve.reciprocal(ca_stat[:, u % 4, 3:4], ca_stat[:, u % 4, 2:3]))
                    dve.tensor_scalar(ca_e[u % 4][:, :], ca_e[u % 4][:, :], ca_stat[:, u % 4, 3:4], None, ALU.mult)\
                       .then_inc(sem("ca_p"), 1)
                u = s - 4
                if u >= 0 and u % QT == QT - 1:
                    h = u // QT
                    dve.wait_ge(sem("ca_hi"), h + 1)
                    dve.tensor_tensor(xl[:, h, :], lin_bank[2 + h % 2][:, :], xh[:, h, :].bitcast(F32), ALU.subtract)\
                       .then_inc(sem("ca_lo"), 1)
            add_to_resid(dve, "cross_o", "n5")

        def block12_loads(sp, last=NB):
            first = LAYER["mix_fm"]["block"] + 2
            load_blocks(sp, 1, first)
            norm_done(sp, "n3")
            for v in range(2):
                sp.dma_start(cmp_w1[v][:, :, :], io["cmp_w1"][v]).then_inc(sem("cmp_loaded"), 16)
                sp.dma_start(cmp_w2[v][:, :, :], io["cmp_w2"][v]).then_inc(sem("cmp_loaded"), 16)
            load_blocks(sp, first, LAYER["out2"]["block"] + 2)
            sp.wait_ge(sem("br_lo"), KD)
            sp.dma_start(mem[:, :, :], io["mem_t"]).then_inc(sem("mem_loaded"), 16)
            load_blocks(sp, LAYER["out2"]["block"] + 2, last)

        HC = 2 * PH
        TG = 64
        NPAIR = NK // 2
        g_dram = nc.dram_tensor("g_scratch", (S // TG, NPAIR, P + 8, 2, TG), F32).ap()

        qp = [at(f"qp{i}", [P, S], scr(2 * i)) for i in range(4)]
        subkeys = at("subkeys", [P, HC * NK], scr(8))
        s_all = at("s_all", [P, HC * QT * NK], scr(64))
        ROWS, COLS = 4, 4
        WIDE = ROWS * PK
        NCAND = WIDE + (PK - ROWS) * COLS
        one_hot = [at(f"one_hot{i}", [P, PH, PK, PK], scr(4 * i), BF16) for i in range(2)]
        top_s = at("top_s", [P, QT, PH, 2, PK], scr(16))
        top_i = at("top_i", [P, QT, PH, 2, PK], scr(20), U32)
        top_f = at("top_f", [P, PH, 2, PK], scr(24), BF16)
        cand = at("cand", [P, QT, NCAND], scr(25))
        place_f = at("place_f", [P, PH, PK], scr(28.5))
        wide_row = at("wide_row", [P, PH, PK], scr(29))
        tall_row = at("tall_row", [P, PH, PK], scr(29.5))
        is_tall = at("is_tall", [P, PH, PK], scr(30))
        tall_col = at("tall_col", [P, PH, PK], scr(30.5))
        j_half = at("j_half", [P, 2, PH, PK], scr(31))
        dec = at("dec", [P, 3, PH * PK], scr(96))
        g_stat = at("g_stat", [P, 2, PH], scr(97.5))
        best_s = at("best_s", [P, QT, PH, 2, PK], scr(16))[:, :, :, 0, :]
        best_j = at("best_j", [P, QT, PH, 2, PK], scr(16), U32)[:, :, :, 1, :]
        best_e = at("best_e", [P, PH, PK], WL + 14 * KB)
        wide_u = at("wide_u", [P, PH, PK], WL + 15 * KB, U32)
        tall_u = at("tall_u", [P, PH, PK], WL + 15 * KB + 512, U32)
        stage = [at("stage0", [P, NK, TG], scr(32)), at("stage1", [P, NK, TG], RAW)]
        turned3 = at("turned3", [P, 3, S], WL)
        ab = [at(f"ab{i}", [P, 2, 4, NK], scr(80 + 4 * i)) for i in range(4)]
        u_raw = [at(f"u_raw{i}", [P, KD, P], scr(64 + 4 * i)) for i in range(4)]
        v_raw = [at(f"v_raw{i}", [P, D], scr(80 + 4 * i)) for i in range(4)]
        u_hi = [at(f"u_hi{i}", [P, KD, P], scr(4 * i), F32R) for i in range(4)]
        u_lo = [at(f"u_lo{i}", [P, KD, P], scr(16 + 4 * i), F32R) for i in range(4)]
        v_hi = [at(f"v_hi{i}", [P, D], scr(32 + 4 * i), F32R) for i in range(4)]
        v_lo = [at(f"v_lo{i}", [P, D], scr(48 + 4 * i), F32R) for i in range(4)]
        g_in = [at(f"g_in{i}", [P, S // TG, 2, TG], RAW + 4 * i * KB) for i in range(2)]
        h_raw = [at(f"h_raw{i}", [P, S], WL + (6 + 2 * i) * KB) for i in range(4)]
        h_hi = [at(f"h_hi{i}", [P, S], RAW + (8 + 2 * i) * KB, F32R) for i in range(4)]
        h_lo = [at(f"h_lo{i}", [P, S], WH + 2 * i * KB, F32R) for i in range(4)]
        out_sq = at("out_sq", [P, KD, S], scr(0))
        out_std = at("out_std", [P, S], scr(16))
        out_rstd = at("out_rstd", [P, S], scr(18))

        BG = P // 4
        QUADS = NK // 4
        LOWEST = -3.0e38

        def peer_credits(pool):
            for name, n in (("pk_s", 4), ("pk_sc", 4), ("g_done", 4), ("g_free", 4), ("pk_t", 1), ("pk_idx", 1), ("g_stored0", 16), ("g_stored1", 16),
                            ("u_lo", 4), ("v_lo", 4), ("ge", 4), ("out_done", 16), ("out_free", 4), ("h_f", 4), ("h_lo", 4)):
                pool.nop().then_inc(sem(name), n)

        def peer_loads(sp):
            sp.wait_ge(sem("ca_lo"), CA_H)
            sp.dma_start(subkeys[:, :], io["subkeys_t"].rearrange("p h n -> p (h n)")).then_inc(sem("subkeys_loaded"), 16)
            load_blocks(sp, LAYER["peer_q"]["block"] + 2, NB)
            sp.wait_ge(sem("pk_dec"), 1)
            for n in range(4):
                load_u(sp, 0, n)
            with sp.Fori(0, QT) as i:
                for q in range(2):
                    sp.wait_ge(sem("g_free"), i * BG + (16 * (q + 1) + 4))
                    sp.dma_start(g_dram[bass.ds(i * 2 + q, 1), :, 0:P].rearrange("o n p c t -> p (o n) c t"),
                                 stage[q][:, :, :].rearrange("p (n c) t -> p n c t", c=2)).then_inc(sem(f"g_stored{q}"), 16)
            sp.wait_ge(sem("g_done"), 4 + QT * BG)

            for s in range(4):
                load_v(sp, 0, s)
            wait(sp, ("g_stored0", 16 + 16 * QT), ("g_stored1", 16 + 16 * QT))
            load_g(sp, 0, 0)
            load_g(sp, 0, 1)
            with sp.Fori(1, QUADS) as i:
                for s in range(4):
                    load_u(sp, i, s)
                    load_v(sp, i, s)
                    if s % 2 == 0:
                        load_g(sp, i, s // 2)

        def load_u(sp, i, n):
            sp.wait_ge(sem("u_lo"), i * 4 + (n + 1))
            sp.dma_start(u_raw[n % 4][:, :, :], io["expert_u"][at_chunk(i, n)]).then_inc(sem(f"u_loaded{n % 4}"), 16)

        def load_v(sp, i, n):
            sp.wait_ge(sem("v_lo"), i * 4 + (n + 1))
            sp.dma_start(v_raw[n % 4][:, :], io["expert_v"][at_chunk(i, n)]).then_inc(sem(f"v_loaded{n % 4}"), 16)

        def load_g(sp, i, b):
            sp.wait_ge(sem("h_f"), i * 4 + (2 * b + 2))
            n = i * 2 + b
            src = g_dram[:, bass.ds(n, 1), 0:P].rearrange("g o p c t -> g (o p) c t")
            sp.dma_start(g_in[b][:, :, :, :], src.rearrange("g p c t -> p g c t")).then_inc(sem(f"g_loaded{b}"), 16)

        def at_chunk(i, n):
            return i * 4 + n

        def split_u_hi(act, i, n):
            act.wait_ge(sem(f"u_loaded{n % 4}"), i * 16 + 16 * (n // 4 + 1))
            act.activation(u_hi[n % 4][:, :, :], u_raw[n % 4][:, :, :], ACT.Copy).then_inc(sem("u_hi"), 1)

        def split_u_lo(pool, i, n):
            pool.wait_ge(sem("u_hi"), i * 4 + (n + 1))
            pool.tensor_tensor(u_lo[n % 4][:, :, :], u_raw[n % 4][:, :, :], u_hi[n % 4][:, :, :].bitcast(F32), ALU.subtract)\
                .then_inc(sem("u_lo"), 1)

        def block3_pool(pool):
            norm_pool(pool, "n5", nrm2, xh, xl, S)
            for b in range(LAYER["peer_q"]["block"] + 2, NB):
                split_lo(pool, b)
            with pool.Fori(0, QT) as i:
                for n in range(BG):
                    pool.wait_ge(sem("ab_done"), i * BG + (n + 1))
                    b = ab[n % 4][:, 1, :, :]
                    pool.tensor_tensor(b, b, turned3[:, 2, bass.ds(i * P + 4 * n, 4)].unsqueeze(2).to_broadcast([P, 4, NK]),
                                       ALU.mult).then_inc(sem("g_rows"), 1)

            for n in range(2):
                split_u_lo(pool, 0, n)

            def quad(i, last):
                for s in range(4):
                    pool.wait_ge(sem("v_hi"), i * 4 + (s + 1))
                    pool.tensor_tensor(v_lo[s][:, :], v_raw[s][:, :], v_hi[s][:, :].bitcast(F32), ALU.subtract)\
                        .then_inc(sem("v_lo"), 1)
                    if not last or s < 2:
                        split_u_lo(pool, i, s + 2)

            with pool.Fori(0, QUADS - 1) as i:
                quad(i, False)
            quad(QUADS - 1, True)

        def block3_act(act):
            norm_act(act, "n5", nrm2, norm_stat2, xh, S)

            def scores_out(n):
                act.wait_ge(sem("pk_s"), n + 5)
                act.activation(s_all[:, n * S:(n + 1) * S], att_bank[n % 4][:, :], ACT.Copy).then_inc(sem("pk_sc"), 1)

            for n in range(HC):
                bank = tile_ready(act, "peer_q", n)
                act.wait_ge(sem("pk_s"), n + 1)
                act.activation(qp[n % 4][:, :], bank[:, :], ACT.Copy).then_inc(sem("bank_free"), 1)
                if n % 2:
                    split_hi(act, LAYER["peer_q"]["block"] + n // 2 + 2)
                if n >= 1:
                    scores_out(n - 1)
            scores_out(HC - 1)
            with act.Fori(0, QT) as i:
                act.wait_ge(sem("pk_gsub"), i + 1)
                act.activation(best_e[:, :, :], best_e[:, :, :], ACT.Exp).then_inc(sem("pk_gexp"), 1)
                act.wait_ge(sem("pk_t"), i + 2)
                act.activation(turned3[:, :, bass.ds(i * P, P)], att_bank[0][:, :3 * P].rearrange("p (j t) -> p j t", j=3),
                               ACT.Copy).then_inc(sem("pk_idx"), 1)
                for n in range(BG):
                    q = n // 16
                    if n % 16 == 0:
                        act.wait_ge(sem(f"g_stored{q}"), i * 16 + 16)
                    act.wait_ge(sem("g_done"), i * BG + (n + 5))
                    t = n % 16 * 4
                    act.activation(stage[q][:, :, t:t + 4], lin_bank[n % 4][:, :].rearrange("p (t c) -> p c t", t=4),
                                   ACT.Copy).then_inc(sem("g_free"), 1)
            for n in range(2):
                split_u_hi(act, 0, n)
            act.wait_ge(sem("g_stored0"), 16 + 16 * QT)

            def quad(i, last):
                for s in range(4):
                    act.wait_ge(sem(f"v_loaded{s}"), i * 16 + 16)
                    act.wait_ge(sem("out_done"), i * 16 + 8 * (s // 2 + 1))
                    act.activation(v_hi[s][:, :], v_raw[s][:, :], ACT.Copy).then_inc(sem("v_hi"), 1)
                    if not last or s < 2:
                        split_u_hi(act, i, s + 2)
                    act.wait_ge(sem("act_done"), i * 4 + (s + 1))
                    act.wait_ge(sem("h_lo"), i * 4 + (s + 1))
                    act.activation(h_raw[s][:, :], lin_bank[s][:, :], ACT.Gelu).then_inc(sem("ge"), 1)
                    act.wait_ge(sem("h_f"), i * 4 + (s + 5))
                    act.activation(h_hi[s][:, :], h_raw[s][:, :], ACT.Copy).then_inc(sem("h_hi"), 1)

            with act.Fori(0, QUADS - 1) as i:
                quad(i, False)
            quad(QUADS - 1, True)
            act.wait_ge(sem("out_free"), 4 + 8 * NPAIR)
            for k in range(KD):
                act.activation(out_sq[:, k, :], resid[:, k, :], ACT.Square).then_inc(sem("n6_sq"), 1)
            act.wait_ge(sem("n6_sum"), 1)
            act.activation(out_std[:, :], lin_bank[0][:, :], ACT.Sqrt, bias=eps[:, 0:1], scale=1.0 / D)\
               .then_inc(sem("n6_std"), 1)

        def block3_pe(pe):
            norm_pe(pe, "n5", nrm2, norm_diag2, S)
            pe.wait_ge(sem("subkeys_loaded"), 16)
            t = LAYER["peer_q"]
            pairs_of = weights_first("peer_q", xh, xl)
            def step(i):
                def scores(n):
                    pe.wait_ge(sem("bank_free"), i * 4 + (t["tile"] + n + 5))
                    pe.wait_ge(sem("pk_sc"), i * 4 + (n + 1))
                    for tt in range(QT):
                        last = pe.matmul(att_bank[n][:, tt * NK:(tt + 1) * NK], qp[n][:, tt * P:(tt + 1) * P],
                                         subkeys[:, bass.ds(i * (4 * NK) + n * NK, NK)], start=True, stop=True)
                    last.then_inc(sem("pk_s"), 1)

                for n in range(4):
                    if n % 2 == 0:
                        pe.wait_ge(sem("lo_done"), i * 2 + (t["block"] + n // 2 + 3))
                    pe.wait_ge(sem("bank_free"), i * 4 + (t["tile"] + n + 1))
                    ready = follow_norm(pe, "n5") if isinstance(i, int) and n == 0 else None
                    products(pe, lin_bank[n][:, :], pairs_of(n // 2, n % 2), ready).then_inc(sem("lin_done"), 1)
                    if n >= 1:
                        scores(n - 1)
                scores(3)

            step(0)
            with pe.Fori(1, HC // 4) as i:
                step(i)
            pe.wait_ge(sem("pk_sc"), 4 + HC)
            with pe.Fori(0, QT) as i:
                pe.wait_ge(sem("pk_dec"), i + 1)
                pe.wait_ge(sem("pk_idx"), i + 1)
                for j in range(3):
                    last = pe.transpose(att_bank[0][:, j * P:(j + 1) * P], dec[:, j, :], ident[:, :])
                last.then_inc(sem("pk_t"), 1)
                for n in range(BG):
                    pe.wait_ge(sem("g_rows"), i * BG + (n + 1))
                    pe.wait_ge(sem("g_free"), i * BG + (n + 1))
                    for t in range(4):
                        last = pe.matmul(lin_bank[n % 4][:, t * P:(t + 1) * P], ab[n % 4][:, 0, t, :], ab[n % 4][:, 1, t, :],
                                         start=True, stop=True)
                    last.then_inc(sem("g_done"), 1)
            pe.wait_ge(sem("g_free"), 4 + QT * BG)

            def activations(i, n):
                pe.wait_ge(sem("u_lo"), i * 4 + (n + 5))
                pe.wait_ge(sem("ge"), i * 4 + (n + 1))
                s = n % 4
                pairs = [(u_hi[s][:, k, :], u_lo[s][:, k, :], xh[:, k, :], xl[:, k, :]) for k in range(KD)]
                products(pe, lin_bank[s][:, :], pairs).then_inc(sem("act_done"), 1)

            def outputs(i, b):
                pe.wait_ge(sem("v_lo"), i * 4 + (2 * b + 6))
                pe.wait_ge(sem("h_lo"), i * 4 + (2 * b + 6))
                for m in range(KD):
                    pe.wait_ge(sem("out_free"), i * 16 + (8 * b + m + 1))
                    cols = slice(m * P, (m + 1) * P)
                    pairs = [(v_hi[s][:, cols], v_lo[s][:, cols], h_hi[s][:, :], h_lo[s][:, :]) for s in (2 * b, 2 * b + 1)]
                    products(pe, att_bank[m % 4][:, :], pairs).then_inc(sem("out_done"), 1)

            def quad(i, last):
                activations(i, 2)
                activations(i, 3)
                outputs(i, 0)
                if not last:
                    activations(i, 4)
                    activations(i, 5)
                outputs(i, 1)

            activations(0, 0)
            activations(0, 1)
            with pe.Fori(0, QUADS - 1) as i:
                quad(i, False)
            quad(QUADS - 1, True)
            for k in range(KD):
                pe.wait_ge(sem("n6_sq"), k + 1)
                last = pe.matmul(lin_bank[0][:, :], ones[:, :], out_sq[:, k, :], start=(k == 0), stop=(k == KD - 1))
            last.then_inc(sem("n6_sum"), 1)

        def block3_dve(dve, chain):
            norm_dve(dve, chain, "n5", resid, nrm2, norm_stat2, norm_diag2, xh, xl, "norm_ffn", S)
            link = chain.link

            def best16(n, values, best, index):
                for j in range(n):
                    ins = dve.max(best(j)[:, 0:8], values(j))
                link(ins)
                for j in range(n):
                    dve.max_index(index(j)[:, 0:8], best(j)[:, 0:8], values(j))
                for j in range(n):
                    ins = dve.match_replace(values(j), best(j)[:, 0:8], values(j), LOWEST)
                link(ins)
                for j in range(n):
                    ins = dve.max(best(j)[:, 8:16], values(j))
                link(ins)
                for j in range(n):
                    ins = dve.max_index(index(j)[:, 8:16], best(j)[:, 8:16], values(j))
                link(ins)

            for n in range(HC):
                dve.wait_ge(sem("pk_sc"), n + 5)
                best16(QT, lambda tt: s_all[:, (n * QT + tt) * NK:(n * QT + tt + 1) * NK],
                       lambda tt: top_s[:, tt, n // 2, n % 2, :], lambda tt: top_i[:, tt, n // 2, n % 2, :])

                if n % 2:
                    h = n // 2
                    for first, rows, cols, out in ((0, ROWS, PK, cand[:, :, 0:WIDE]), (ROWS, PK - ROWS, COLS, cand[:, :, WIDE:])):
                        grid = [P, QT, rows, cols]
                        ins = dve.tensor_tensor(out.rearrange("p i (a b) -> p i a b", b=cols),
                                                top_s[:, :, h, 0, first:first + rows].unsqueeze(3).to_broadcast(grid),
                                                top_s[:, :, h, 1, 0:cols].unsqueeze(2).to_broadcast(grid), ALU.add)
                    link(ins)
                    best16(QT, lambda tt: cand[:, tt, :], lambda tt: best_s[:, tt, h, :], lambda tt: best_j[:, tt, h, :])

            def choose(tt):
                link(dve.tensor_copy(top_f[:, :, :, :], top_i[:, tt, :, :, :]))
                best, place = best_s[:, tt], best_j[:, tt]
                dve.tensor_tensor(best_e[:, :, :], best, best[:, :, 0].unsqueeze(2).to_broadcast([P, PH, PK]),
                                  ALU.subtract).then_inc(sem("pk_gsub"), 1)
                dve.tensor_scalar(wide_u[:, :, :], place, 4, None, ALU.logical_shift_right)
                dve.tensor_scalar(tall_u[:, :, :], place, 2, None, ALU.logical_shift_right)
                link(dve.tensor_copy(place_f[:, :, :], place))
                dve.tensor_copy(wide_row[:, :, :], wide_u[:, :, :])
                dve.tensor_copy(tall_row[:, :, :], tall_u[:, :, :])
                link(dve.tensor_scalar(is_tall[:, :, :], place_f[:, :, :], WIDE - 0.5, None, ALU.is_gt))
                wide_col = j_half[:, 1, :, :]
                dve.scalar_tensor_tensor(out=tall_col[:, :, :], in0=tall_row[:, :, :], scalar=-float(COLS), in1=place_f[:, :, :],
                                         op0=ALU.mult, op1=ALU.add)
                dve.scalar_tensor_tensor(out=wide_col, in0=wide_row[:, :, :], scalar=-float(PK), in1=place_f[:, :, :],
                                         op0=ALU.mult, op1=ALU.add)
                link(dve.scalar_tensor_tensor(out=tall_row[:, :, :], in0=tall_row[:, :, :], scalar=float(ROWS - WIDE // COLS),
                                              in1=wide_row[:, :, :], op0=ALU.add, op1=ALU.subtract))
                dve.tensor_tensor(tall_row[:, :, :], tall_row[:, :, :], is_tall[:, :, :], ALU.mult)
                link(dve.tensor_tensor(tall_col[:, :, :], tall_col[:, :, :], wide_col, ALU.subtract))
                dve.tensor_tensor(j_half[:, 0, :, :], wide_row[:, :, :], tall_row[:, :, :], ALU.add)
                link(dve.tensor_tensor(tall_col[:, :, :], tall_col[:, :, :], is_tall[:, :, :], ALU.mult))
                link(dve.tensor_tensor(wide_col, wide_col, tall_col[:, :, :], ALU.add))
                grid = [P, PH, PK, PK]
                for half in range(2):
                    spread = j_half[:, half, :, :].unsqueeze(3).to_broadcast(grid)
                    ins = dve.tensor_tensor(one_hot[half][:, :, :, :], iota16[:, :].unsqueeze(1).unsqueeze(1).to_broadcast(grid),
                                            spread, ALU.is_equal)
                link(ins)
                for half in range(2):
                    ins = dve.tensor_tensor(one_hot[half][:, :, :, :], one_hot[half][:, :, :, :],
                                            top_f[:, :, half, :].unsqueeze(2).to_broadcast(grid), ALU.mult)
                link(ins)
                dve.wait_ge(sem("pk_t"), tt + 1)
                for half in range(2):
                    ins = dve.tensor_reduce(dec[:, half, :].rearrange("p (h k) -> p h k", h=PH), one_hot[half][:, :, :, :],
                                            AX_X, ALU.add)
                link(ins)
                dve.wait_ge(sem("pk_gexp"), tt + 1)
                link(dve.tensor_reduce(g_stat[:, 0, :], best_e[:, :, :], AX_X, ALU.add))
                link(dve.reciprocal(g_stat[:, 1, :], g_stat[:, 0, :]))
                dve.tensor_tensor(dec[:, 2, :].rearrange("p (h k) -> p h k", h=PH), best_e[:, :, :],
                                  g_stat[:, 1, :].unsqueeze(2).to_broadcast([P, PH, PK]), ALU.mult).then_inc(sem("pk_dec"), 1)

            for tt in range(QT):
                choose(tt)
                dve.wait_ge(sem("pk_idx"), tt + 2)
                with dve.Fori(0, BG // 4) as quad_no:
                    for n in range(4):
                        dve.wait_ge(sem("g_done"), quad_no * 4 + (tt * BG + n + 1))
                        shape = [P, 2, 4, NK]
                        dve.tensor_tensor(ab[n][:, :, :, :], iota_key[:, :].unsqueeze(1).unsqueeze(1).to_broadcast(shape),
                                          turned3[:, 0:2, bass.ds(quad_no * 16 + (tt * P + 4 * n), 4)].unsqueeze(3).to_broadcast(shape),
                                          ALU.is_equal).then_inc(sem("ab_done"), 1)

            def weighted(i, n):
                s = n % 4
                dve.wait_ge(sem("ge"), i * 4 + (n + 5))
                if s % 2 == 0:
                    dve.wait_ge(sem(f"g_loaded{s // 2}"), i * 16 + 16 * (n // 4 + 1))
                h = h_raw[s][:, :].rearrange("p (g t) -> p g t", t=TG)
                dve.tensor_tensor(h, h, g_in[s // 2][:, :, s % 2, :], ALU.mult).then_inc(sem("h_f"), 1)
                dve.wait_ge(sem("h_hi"), i * 4 + (n + 1))
                dve.tensor_tensor(h_lo[s][:, :], h_raw[s][:, :], h_hi[s][:, :].bitcast(F32), ALU.subtract)\
                   .then_inc(sem("h_lo"), 1)

            def add_outputs(i, b):
                for m in range(KD):
                    dve.wait_ge(sem("out_done"), i * 16 + (16 + 8 * b + m + 1))
                    dve.tensor_tensor(resid[:, m, :], att_bank[m % 4][:, :], resid[:, m, :], ALU.add)\
                       .then_inc(sem("out_free"), 1)

            def quad(i, last):
                weighted(i, 2)
                weighted(i, 3)
                add_outputs(i, 0)
                if not last:
                    weighted(i, 4)
                    weighted(i, 5)
                add_outputs(i, 1)

            weighted(0, 0)
            weighted(0, 1)
            with dve.Fori(0, QUADS - 1) as i:
                quad(i, False)
            quad(QUADS - 1, True)
            dve.wait_ge(sem("n6_std"), 1)
            chain.link(dve.reciprocal(out_rstd[:, :], out_std[:, :]))
            for k in range(KD):
                dve.scalar_tensor_tensor(out=out_sq[:, k, :], in0=resid[:, k, :], scalar=col("norm_final", k),
                                         in1=out_rstd[:, :], op0=ALU.mult, op1=ALU.mult).then_inc(sem("n6_out"), 1)

        def store_output(sp):
            for k in range(KD):
                sp.wait_ge(sem("n6_out"), k + 1)
                sp.dma_start(io["out_t"][:, k, :], out_sq[:, k, :]).then_inc(sem("out_stored"), 16)
            sp.wait_ge(sem("out_stored"), 16 * KD)
        block = ctx.enter_context(nc.Block())
        @block.sync
        def _(sp):
            for half in range(2):
                ks_ = slice(half * KD // 2, (half + 1) * KD // 2)
                sp.dma_start(resid[:, ks_, :], io["x_t"][:, ks_, :]).then_inc(sem(f"x_loaded{half}"), 16)
            load_blocks(sp, 0, 1)
            sp.dma_start(params[:, :], io["params"]).then_inc(sem("params_loaded"), 16)
            block12_loads(sp, LAYER["peer_q"]["block"] + 2)
            peer_loads(sp)
            store_output(sp)

        @block.gpsimd
        def _(pool):
            make_consts(pool)
            block1_pool(pool)
            block2_pool(pool)
            block3_pool(pool)

        @block.scalar
        def _(act):
            block1_act(act)
            block2_act(act)
            block3_act(act)

        @block.vector
        def _(dve):
            chain = Chain(dve, "dve_step")
            block1_dve(dve, chain)
            block2_dve(dve, chain)
            block3_dve(dve, chain)

        @block.tensor
        def _(pe):
            block1_pe(pe)
            block2_pe(pe)
            block3_pe(pe)


def blocks_of(w, kt, columns):
    w = np.asarray(w).reshape(kt, P, -1)
    return [np.concatenate([w[:, :, a:b] for a, b in part], axis=2).transpose(1, 0, 2).reshape(P, -1) for part in columns]


def lay_out(i):
    f = {k: np.asarray(v) for k, v in i.items()}
    w_in, w_mix, w_up, w_down = f["w_in"][0], f["w_in_2"][0], f["w_up"][0], f["w_down"][0]

    def runs(first, n, width):
        return [[(first + width * b, first + width * (b + 1))] for b in range(n)]

    def side_by_side(a, b, n):
        return [[(a + P * j, a + P * (j + 1)), (b + P * j, b + P * (j + 1))] for j in range(n)]

    A = AW
    kv = 4 * A
    gb = kv + 6 * P
    ga = gb + NSA_H * 3
    branches = np.concatenate([f["w_branch_a_2"][0], f["w_branch_b_2"][0]])
    split = FHALF[0] * P
    parts = {
        "in_fm": blocks_of(w_in, KD, runs(0, 4, 256) + side_by_side(3 * A, 3 * A + CW, CT)),
        "in_v": blocks_of(w_in, KD, runs(2 * A, 2, 256)),
        "out1": blocks_of(f["w_out"][0], KD, runs(0, 4, 256)),
        "up0": blocks_of(w_up, KD, side_by_side(0, FF, FT)[:FHALF[0]]),
        "down0": blocks_of(w_down[:split], FHALF[0], runs(0, 8, P)),
        "up1": blocks_of(w_up, KD, side_by_side(0, FF, FT)[FHALF[0]:]),
        "down1": blocks_of(w_down[split:], FHALF[1], runs(0, 8, P)),
        "mix_fm": blocks_of(w_mix, KD, runs(0, 4, 256) + runs(3 * A, 2, 256) + [
            [(kv, kv + 2 * P)], [(kv + 2 * P, kv + 3 * P), (kv + 4 * P, kv + 5 * P)]]),
        "mix_tm": blocks_of(w_mix, KD, runs(2 * A, 2, 256) + [
            [(kv + 3 * P, kv + 4 * P), (kv + 5 * P, kv + 6 * P)], [(gb, gb + 256)]]),
        "gates": blocks_of(w_mix, KD, side_by_side(ga, ga + D, KD)),
        "branch": blocks_of(branches, KD, runs(0, 4, 256)),
        "out2": blocks_of(f["w_out_2"][0], KD, runs(0, 4, 256)),
        "cross_q": blocks_of(f["w_cross_q_2"][0], KD, runs(0, 2, 256)),
        "cross_k": blocks_of(f["w_cross_kv_2"][0], KD, runs(0, 2, 256)),
        "cross_v": blocks_of(f["w_cross_kv_2"][0], KD, runs(AW, 2, 256)),
        "cross_o": blocks_of(f["w_cross_o_2"][0], AW // P, runs(0, 2, 512)),
        "peer_q": blocks_of(f["peer_wq_2"][0], KD, runs(0, 8, 256)),
    }
    w_small = np.zeros((len(TILES_AFTER), P, BLK), np.float32)
    for name, blocks in parts.items():
        for b, w in enumerate(blocks):
            w_small[LAYER[name]["block"] + b, :, :w.shape[1]] = w

    def tiles(v):
        return v.reshape(-1, P).T

    def channel_taps(v):
        return v.reshape(v.shape[0], -1, P).transpose(2, 1, 0).reshape(P, -1)

    def twice(v):
        return np.concatenate([v, v])

    params = np.concatenate([
        tiles(f["norm1_g"]), tiles(f["norm2_g"]), tiles(f["norm_mix_2"]), tiles(f["norm_cross_2"]),
        tiles(f["norm_mem_2"]), tiles(f["norm_ffn_2"]), tiles(f["norm_final_2"]),
        twice(f["q_norm_g"].T), twice(f["k_norm_g"].T), channel_taps(f["conv_dw_w"][0]), tiles(f["conv_dw_b"]),
        tiles(f["conv_ln_g"]), tiles(f["conv_ln_b"]), channel_taps(f["ffn_dw_w"][0]), tiles(f["ffn_dw_b"]),
        tiles(f["diff_subln_2"]), twice(f["nsa_cmp_pos_2"][0].T), twice(f["diff_lambda_2"][0].T)], axis=1)

    def feature_major(x):
        return x.T.reshape(KD, P, -1).transpose(1, 0, 2)

    def both(k, v, shape):
        return np.stack([f[k][0].reshape(shape).transpose(1, 0, 2), f[v][0].reshape(shape).transpose(1, 0, 2)])

    return {
        "x_t": feature_major(f["x"][0]), "mem_t": feature_major(f["mem_2"][0]), "params": params, "w_small": w_small,
        "cmp_w1": both("nsa_ck_w1_2", "nsa_cv_w1_2", (CMP // 2, P, CMP_HID)),
        "cmp_w2": both("nsa_ck_w2_2", "nsa_cv_w2_2", (CMP_HID // P, P, HD)),
        "subkeys_t": f["peer_subkeys_2"][0].reshape(2 * PH, NK, P).transpose(2, 0, 1),
        "expert_u": f["peer_u_2"][0].reshape(NK, NK, KD, P).transpose(1, 3, 2, 0),
        "expert_v": f["peer_v_2"][0].reshape(NK, NK, D).transpose(1, 0, 2),
    }


def kernel(**inputs):
    import concourse.bacc as bacc
    from concourse.bass_utils import run_bass_kernel_spmd

    arrays = {k: np.ascontiguousarray(v) for k, v in lay_out(inputs).items()}
    nc = bacc.Bacc("TRN2", target_bir_lowering=False, num_devices=1)
    io = {}
    for name, shape in INPUTS:
        assert arrays[name].shape == shape and arrays[name].dtype == np.float32
        io[name] = nc.dram_tensor(name, shape, F32, kind="ExternalInput").ap()
    for name, shape in OUTPUTS:
        io[name] = nc.dram_tensor(name, shape, F32, kind="ExternalOutput").ap()
    build_program(nc, io)
    out = run_bass_kernel_spmd(nc, [arrays], core_ids=[0]).results[0]["out_t"]
    return np.ascontiguousarray(out.transpose(2, 1, 0).reshape(1, S, D))
```

```python
import math
from contextlib import ExitStack

import numpy as np

import concourse.bass as bass
from concourse import mybir

F32 = mybir.dt.float32
F32R = mybir.dt.float32r
BF16 = mybir.dt.bfloat16
U32 = mybir.dt.uint32
ALU = mybir.AluOpType
ACT = mybir.ActivationFunctionType
AX_X = mybir.AxisListType.X

P = 128
S = 512
QT = S // P
D = 1024
KD = D // P
EPS = 1e-6

HEADS = 8
HD = 64
AW = HEADS * HD
CW = D - AW
CT = CW // P
TAPS = 31
FF = 2816
FT = FF // P
FTAPS = 3
FHALF = (12, 10)

DA_H = 4
NSA_H, NSA_G, NSA_R = 8, 2, 4
CMP = 32
NCMP = S // CMP
CMP_HID = 256
MEM = 256
CA_H = 4
PH, PK = 8, 16
NK = 128
LAMBDA_INIT = 0.8 - 0.6 * math.exp(-0.3 * 0)
NEG = -1e30

BLK = 2048

LAYERS = [
    ("in_fm", 8, KD, 2, 256, 2),
    ("in_v", 2, KD, QT, 256, 2),
    ("out1", 4, KD, 2, 256, 2),
    ("up0", FHALF[0], KD, 2, 256, 2),
    ("down0", 8, FHALF[0], 1, 128, 4),
    ("up1", FHALF[1], KD, 2, 256, 2),
    ("down1", 8, FHALF[1], 1, 128, 4),
    ("mix_fm", 8, KD, 2, 256, 2),
    ("mix_tm", 4, KD, QT, 256, 2),
    ("gates", 8, KD, 2, 256, 2),
    ("branch", 4, KD, 4, 256, 2),
    ("out2", 4, KD, 2, 256, 2),
    ("cross_q", 2, KD, 2, 256, 2),
    ("cross_k", 2, KD, 2, 256, 2),
    ("cross_v", 2, KD, MEM // P, 256, 2),
    ("cross_o", 2, AW // P, 4, 512, 2),
    ("peer_q", 8, KD, 2, 256, 2),
]


def layer_table():
    table, ends, block, tile = {}, [], 0, 0
    for name, nb, kt, tiles, cols, unroll in LAYERS:
        table[name] = dict(nb=nb, kt=kt, tiles=tiles, cols=cols, unroll=unroll, block=block, tile=tile)
        for _ in range(nb):
            tile += tiles
            ends.append(tile)
        block += nb
    return table, ends


LAYER, TILES_AFTER = layer_table()

PARAMS = [("norm1", KD), ("norm2", KD), ("norm_mix", KD), ("norm_cross", KD), ("norm_mem", KD), ("norm_ffn", KD),
          ("norm_final", KD), ("q_norm", 1), ("k_norm", 1), ("conv_w", CT * TAPS), ("conv_b", CT), ("ln_g", CT),
          ("ln_b", CT), ("ffn_w", FT * FTAPS), ("ffn_b", FT), ("subln", 1), ("cmp_pos", CMP), ("lam", 4)]
PCOL, NPAR = {}, 0
for _n, _w in PARAMS:
    PCOL[_n] = NPAR
    NPAR += _w

INPUTS = [
    ("x_t", (P, KD, S)), ("mem_t", (P, KD, MEM)), ("params", (P, NPAR)),
    ("w_small", (len(TILES_AFTER), P, BLK)),
    ("cmp_w1", (2, P, CMP // 2, CMP_HID)), ("cmp_w2", (2, P, CMP_HID // P, HD)),
    ("subkeys_t", (P, 2 * PH, NK)),
    ("expert_u", (NK, P, KD, P)), ("expert_v", (NK, P, D)),
]

OUTPUTS = [("out_t", (P, KD, S))]

KB = 1024
BASE = 16512
RES, XH, XL = BASE, BASE + 16 * KB, BASE + 32 * KB
RAW, WH, WL = BASE + 48 * KB, BASE + 64 * KB, BASE + 80 * KB
CONST = BASE + 96 * KB
SCR = CONST + 13 * KB


def build_program(nc, io):
    with ExitStack() as ctx:
        sems = {}

        def sem(name):
            if name not in sems:
                sems[name] = ctx.enter_context(nc.semaphore(name))
            return sems[name]

        def at(name, shape, offset, dt=F32):
            return nc.alloc_sbuf_tensor_at(name, list(shape), dt, offset=offset)

        cursor = [CONST]

        def const(name, shape, dt=F32):
            size = int(np.prod(shape[1:])) * (2 if dt == BF16 else 4)
            t = at(name, shape, cursor[0], dt)
            cursor[0] += (size + 31) // 32 * 32
            assert cursor[0] <= SCR
            return t

        psum = [ctx.enter_context(nc.psum_tensor(f"bank{i}", [P, S], F32)) for i in range(8)]
        lin_bank, att_bank = psum[:4], psum[4:]

        resid = at("resid", [P, KD, S], RES)
        xh = at("xh", [P, KD, S], XH, F32R)
        xl = at("xl", [P, KD, S], XL, F32R)
        raw = [at(f"w_raw{i}", [P, BLK], RAW + i * 8 * KB) for i in range(2)]
        wh = [at(f"w_hi{i}", [P, BLK], WH + i * 8 * KB, F32R) for i in range(2)]
        wl = [at(f"w_lo{i}", [P, BLK], WL + i * 8 * KB, F32R) for i in range(2)]

        params = const("params_sb", [P, NPAR])
        ident = const("ident", [P, P])
        ones = const("ones", [P, P])
        later_key = const("later_key", [P, P])
        causal = const("causal", [P, P])
        dist = const("dist", [P, S])
        cmp_dist = const("cmp_dist", [P, QT, NCMP])
        cmp_valid = const("cmp_valid", [P, QT, NCMP])
        head_sum = const("head_sum", [P, 8, 16])
        iota16 = const("iota16", [P, PK])
        iota_key = const("iota_key", [P, NK])
        eps = const("eps", [P, 1])
        qg = const("qg", [P, 1])
        subln_g = const("subln_g", [P, 1])
        lam_prod = const("lam_prod", [P, 2])
        lam_exp = const("lam_exp", [P, 2])
        lam = const("lam_col", [P, 1])
        gates24 = const("gates24", [P, QT, NSA_H * 3])

        def col(name, i=0):
            return params[:, PCOL[name] + i:PCOL[name] + i + 1]

        qk = at("qk", [P, 8, S], SCR)
        vtok = at("vtok", [P, QT, AW], SCR + 16 * KB)
        PADW = S + TAPS - 1
        cpad = at("cpad", [P, CT, PADW], SCR + 24 * KB)
        cacc = at("cacc", [P, CT, S], SCR + 33 * KB)
        attn = at("attn", [P, CT, S], SCR + 41 * KB)
        NW = 1280
        KOFF = [0, 512, 1024, 896]
        STK = SCR + 49 * KB
        ln1 = at("ln1", [P, NW], STK)
        soft = [at(f"soft{i}", [P, NW], STK + (5 + 5 * i) * KB) for i in range(2)]
        lbeta = [at(f"lbeta{i}", [P, NW], STK + (15 + 5 * i) * KB) for i in range(2)]
        wgt = [at(f"wgt{i}", [P, NW], STK + (25 + 5 * i) * KB) for i in range(2)]
        qk_sq = at("qk_sq", [P, 8, S], STK)
        std16 = at("std16", [16, S], STK + 16 * KB)
        rstd16 = at("rstd16", [16, S], STK + 18 * KB)
        glu_sig = [at(f"glu_sig{i}", [P, S], STK + (20 + 2 * i) * KB) for i in range(2)]
        head_spread = at("head_spread", [16, 8 * P], STK + 35 * KB)
        conv_prod = [at(f"conv_prod{i}", [P, S], STK + (39 + 2 * i) * KB) for i in range(2)]
        ln_sq = at("ln_sq", [P, CT, S], STK)
        ln_std = at("ln_std", [P, S], STK + 8 * KB)
        ln_rstd = at("ln_rstd", [P, S], STK + 10 * KB)

        fh = at("fh", [P, FHALF[0], S], SCR, F32R)
        fl = at("fl", [P, FHALF[0], S], SCR + 24 * KB, F32R)
        f_conv = [at(f"f_conv{i}", [P, S], SCR + (48 + 2 * i) * KB) for i in range(2)]
        f_silu = [at(f"f_silu{i}", [P, S], SCR + (52 + 2 * i) * KB) for i in range(2)]
        f_out = [at(f"f_out{i}", [P, S], SCR + (56 + 2 * i) * KB) for i in range(2)]

        class Chain:

            def __init__(self, eng, name):
                self.eng, self.sem, self.n = eng, sem(name), 0

            def link(self, ins):
                self.n += 1
                ins.then_inc(self.sem, 1)
                self.eng.wait_ge(self.sem, self.n)

        def wait(eng, *needs):
            for name, value in needs:
                if value > 0:
                    eng.wait_ge(sem(name), value)

        NB = len(TILES_AFTER)

        def load_blocks(sp, first, last):
            for g in range(first, last):
                sp.wait_ge(sem("lo_done"), g + 1)
                n = size_of(g)
                sp.dma_start(raw[g % 2][:, :n], io["w_small"][g, :, :n]).then_inc(sem(f"raw_loaded{g % 2}"), 16)

        def size_of(g):
            for t in LAYER.values():
                if t["block"] <= g < t["block"] + t["nb"]:
                    return t["kt"] * t["cols"]

        def split_hi(act, g):
            if g >= NB:
                return
            wait(act, (f"raw_loaded{g % 2}", 16 * (g // 2 + 1)))
            if g >= 2:
                wait(act, ("lin_done", TILES_AFTER[g - 2]))
            n = size_of(g)
            act.activation(wh[g % 2][:, :n], raw[g % 2][:, :n], ACT.Copy).then_inc(sem("hi_done"), 1)

        def split_lo(pool, g):
            n = size_of(g)
            pool.wait_ge(sem("hi_done"), g + 1)
            pool.tensor_tensor(wl[g % 2][:, :n], raw[g % 2][:, :n], wh[g % 2][:, :n].bitcast(F32),
                               ALU.subtract).then_inc(sem("lo_done"), 1)

        def products(pe, out, pairs, ready=None):
            for k, (ah, al, bh, bl) in enumerate(pairs):
                if ready:
                    ready(k)
                pe.matmul(out, al, bh, start=(k == 0), stop=False)
                pe.matmul(out, ah, bl, start=False, stop=False)
                last = pe.matmul(out, ah, bh, start=False, stop=(k == len(pairs) - 1))
            return last

        def linear_pe(pe, name, pairs_of, ncols, ready=None, between=None):
            t = LAYER[name]
            u, tiles = t["unroll"], t["tiles"]

            def step(i):
                for s in range(u):
                    pe.wait_ge(sem("lo_done"), i * u + (t["block"] + s + 3))
                    for m in range(tiles):
                        n = s * tiles + m
                        pe.wait_ge(sem("bank_free"), i * (u * tiles) + (t["tile"] + n + 1))
                        out = lin_bank[n % 4][:, :ncols]
                        first = isinstance(i, int) and i == 0 and n == 0
                        products(pe, out, pairs_of(s % 2, m), ready if first else None).then_inc(sem("lin_done"), 1)
                        if between:
                            between(i * (u * tiles) + n)

            assert t["tile"] % 4 == 0 and t["block"] % 2 == 0 and u * tiles % 4 == 0 and t["nb"] % u == 0
            start = t["nb"] // u if between else 1 if ready or t["nb"] == u else 0
            for i in range(start):
                step(i)
            if t["nb"] // u > start:
                with pe.Fori(start, t["nb"] // u) as i:
                    step(i)

        def weights_first(name, hi, lo, n=S):
            t = LAYER[name]
            kt, cols = t["kt"], t["cols"]

            def pairs(slot, m):
                def w(x, k):
                    return x[slot][:, k * cols + m * P:k * cols + m * P + P]
                return [(w(wh, k), w(wl, k), hi[:, k, :n], lo[:, k, :n]) for k in range(kt)]
            return pairs

        def tokens_first(name, hi, lo):
            t = LAYER[name]
            kt, cols = t["kt"], t["cols"]

            def pairs(slot, m):
                def w(x, k):
                    return x[slot][:, k * cols:(k + 1) * cols]
                return [(hi[:, k, m * P:m * P + P], lo[:, k, m * P:m * P + P], w(wh, k), w(wl, k)) for k in range(kt)]
            return pairs

        def tile_ready(eng, name, n):
            eng.wait_ge(sem("lin_done"), LAYER[name]["tile"] + n + 1)
            return lin_bank[n % 4]

        NORMS = ["n1", "n2", "n3", "n4", "nm", "n5"]

        def before(st, per_norm):
            return NORMS.index(st) * per_norm

        def norm_tile_done(eng, st, k):
            eng.wait_ge(sem("norm_lo_odd" if k % 2 else "norm_lo"), before(st, KD // 2) + k // 2 + 1)

        def follow_norm(pe, st):
            return lambda k: norm_tile_done(pe, st, k)

        def follow(pe, name):
            return lambda k: pe.wait_ge(sem(name), k + 1)

        def norm_done(eng, st):
            norm_tile_done(eng, st, KD - 2)
            norm_tile_done(eng, st, KD - 1)

        def splits_and_squares(act, name):
            t = LAYER[name]
            for b in range(t["nb"]):
                if b < t["nb"] - 1:
                    split_hi(act, t["block"] + b + 2)
                for k in range(b * t["tiles"], (b + 1) * t["tiles"]):
                    act.wait_ge(sem("bank_free"), 4 + t["tile"] + k + 1)
                    act.activation(nrm2[:, k, :], resid[:, k, :], ACT.Square).then_inc(sem("norm_sq"), 1)

        def squares(act, src, sq, n, first=0, last=KD):
            for k in range(first, last):
                act.activation(sq[:, k, :n], src[:, k, :n], ACT.Square).then_inc(sem("norm_sq"), 1)

        def norm_act(act, st, sq, stat, hi, n, layer_before=None):
            act.wait_ge(sem("norm_sum"), before(st, 1) + 1)
            tts = n // P
            act.activation(stat[:, 0:tts], att_bank[0][:, 0:tts], ACT.Sqrt, bias=eps[:, 0:1], scale=1.0 / D)\
               .then_inc(sem("norm_std"), 1)
            if layer_before:
                split_hi(act, LAYER[layer_before]["block"] + LAYER[layer_before]["nb"] + 1)
            for k in range(KD):
                act.wait_ge(sem("norm_h"), before(st, KD) + k + 1)
                act.activation(hi[:, k, :n], sq[:, k, :n], ACT.Copy).then_inc(sem("norm_hi"), 1)

        def norm_pe(pe, st, sq, diag, n):
            pe.wait_ge(sem("norm_part"), before(st, KD - 1) + KD - 1)
            for tt in range(n // P):
                last = pe.matmul(att_bank[0][:, tt:tt + 1], sq[:, 0, tt * P:(tt + 1) * P], ones[:, 0:1], start=True, stop=True)
            last.then_inc(sem("norm_sum"), 1)
            pe.wait_ge(sem("norm_diag"), before(st, 1) + 1)
            pe.matmul(att_bank[1][:, :n], ones[:, :], diag[:, :n], start=True, stop=True).then_inc(sem("norm_rstd"), 1)

        def add_squares(dve, st, sq, n, k):
            if k == 1:
                dve.wait_ge(sem("norm_sq"), before(st, KD) + 1)
            else:
                dve.wait_ge(sem("norm_part"), before(st, KD - 1) + k - 1)
            dve.wait_ge(sem("norm_sq"), before(st, KD) + k + 1)
            dve.tensor_tensor(sq[:, 0, :n], sq[:, 0, :n], sq[:, k, :n], ALU.add).then_inc(sem("norm_part"), 1)

        def norm_dve(dve, chain, st, src, sq, stat, diag, hi, lo, gain, n):
            dve.wait_ge(sem("norm_std"), before(st, 1) + 1)
            tts = n // P
            chain.link(dve.reciprocal(stat[:, QT:QT + tts], stat[:, 0:tts]))
            shape = [P, tts, P]
            dve.tensor_tensor(diag[:, :n].rearrange("p (i t) -> p i t", t=P), ident[:, :].unsqueeze(1).to_broadcast(shape),
                              stat[:, QT:QT + tts].unsqueeze(2).to_broadcast(shape), ALU.mult).then_inc(sem("norm_diag"), 1)
            dve.wait_ge(sem("norm_rstd"), before(st, 1) + 1)
            for k in range(KD + 1):
                if k < KD:
                    dve.scalar_tensor_tensor(out=sq[:, k, :n], in0=src[:, k, :n], scalar=col(gain, k),
                                             in1=att_bank[1][:, :n], op0=ALU.mult, op1=ALU.mult).then_inc(sem("norm_h"), 1)
                if k % 2:
                    norm_low(dve, st, sq, hi, lo, n, k - 1)

        def norm_low(eng, st, sq, hi, lo, n, k):
            eng.wait_ge(sem("norm_hi"), before(st, KD) + k + 1)
            eng.tensor_tensor(lo[:, k, :n], sq[:, k, :n], hi[:, k, :n].bitcast(F32), ALU.subtract)\
               .then_inc(sem("norm_lo_odd" if k % 2 else "norm_lo"), 1)

        def norm_pool(pool, st, sq, hi, lo, n):
            for k in range(1, KD, 2):
                norm_low(pool, st, sq, hi, lo, n, k)

        NRM1, RS1 = STK, STK + 24 * KB
        nrm1 = at("nrm1", [P, KD, S], NRM1)
        norm_stat1 = at("norm_stat1", [P, 2 * QT], RS1)
        norm_diag1 = at("norm_diag1", [P, S], RS1 + 2 * KB)
        nrm2 = at("nrm2", [P, KD, S], SCR + 76 * KB)
        norm_stat2 = at("norm_stat2", [P, 2 * QT], SCR + 92 * KB)
        norm_diag2 = at("norm_diag2", [P, S], SCR + 93 * KB)

        PIECES = [(0, 512), (512, 512), (1024, 256)]

        def regions(kb):
            off = KOFF[kb]
            return off // S, off % S, S - kb * P

        CONV_DVE, CONV_POOL = (0, 1, 2), (3,)
        N_CONV = len(CONV_DVE) * TAPS

        def conv_dve(dve, first, last):
            for n in range(first, min(last, N_CONV)):
                tap, ct = n // len(CONV_DVE), CONV_DVE[n % len(CONV_DVE)]
                w = col("conv_w", ct * TAPS + tap)
                x = cpad[:, ct, tap:tap + S]
                if tap:
                    dve.wait_ge(sem("conv_dve"), n - len(CONV_DVE) + 1)
                    ins = dve.scalar_tensor_tensor(out=cacc[:, ct, :], in0=x, scalar=w, in1=cacc[:, ct, :],
                                                   op0=ALU.mult, op1=ALU.add)
                else:
                    ins = dve.tensor_scalar(cacc[:, ct, :], x, w, col("conv_b", ct), ALU.mult, ALU.add)
                ins.then_inc(sem("conv_dve"), 1)

        def conv_pool(pool):
            n_ct = len(CONV_POOL)
            for tap in range(TAPS):
                for c, ct in enumerate(CONV_POOL):
                    w = col("conv_w", ct * TAPS + tap)
                    x = cpad[:, ct, tap:tap + S]
                    if tap == 0:
                        pool.tensor_scalar(cacc[:, ct, :], x, w, col("conv_b", ct), ALU.mult, ALU.add)\
                            .then_inc(sem("conv_pool"), 1)
                    else:
                        if tap >= 2:
                            pool.wait_ge(sem("conv_pool"), (tap - 1) * n_ct + c + 1)
                        pool.tensor_scalar(conv_prod[c][:, :], x, w, None, ALU.mult).then_inc(sem("conv_prod"), 1)
                for c, ct in enumerate(CONV_POOL):
                    if tap:
                        wait(pool, ("conv_prod", (tap - 1) * n_ct + c + 1), ("conv_pool", (tap - 1) * n_ct + c + 1))
                        pool.tensor_tensor(cacc[:, ct, :], cacc[:, ct, :], conv_prod[c][:, :], ALU.add)\
                            .then_inc(sem("conv_pool"), 1)

        def conv_done(eng):
            wait(eng, ("conv_dve", N_CONV), ("conv_pool", len(CONV_POOL) * TAPS))

        def block1_act(act):
            for half in range(2):
                act.wait_ge(sem(f"x_loaded{half}"), 16)
                squares(act, resid, nrm1, S, half * KD // 2, (half + 1) * KD // 2)
            act.wait_ge(sem("consts"), N_CONST)
            split_hi(act, 0)
            norm_act(act, "n1", nrm1, norm_stat1, xh, S)
            split_hi(act, 1)
            base = LAYER["in_fm"]["block"]
            for b in range(4):
                split_hi(act, base + b + 2)
            for j in range(CT):
                bank = tile_ready(act, "in_fm", 8 + 2 * j + 1)
                if j >= 2:
                    act.wait_ge(sem("bank_free"), 4 + 8 + 2 * (j - 1))
                act.activation(glu_sig[j % 2][:, :], bank[:, :], ACT.Sigmoid).then_inc(sem("glu_sig"), 1)
                split_hi(act, base + 4 + j + 2)
                if j < 2:
                    act.wait_ge(sem("bank_free"), 4 + 8)
                    for k in range(4 * j, 4 * j + 4):
                        act.activation(qk_sq[:, k, :], qk[:, k, :], ACT.Square).then_inc(sem("qk_sq"), 1)
            act.wait_ge(sem("qk_sum"), 1)
            act.activation(std16[:, :], att_bank[0][0:16, :], ACT.Sqrt, bias=eps[0:16, 0:1], scale=1.0 / HD)\
               .then_inc(sem("qk_std"), 1)
            for b in range(2):
                split_hi(act, LAYER["in_v"]["block"] + b + 2)

            def pre(h):
                act.wait_ge(sem("st_z"), h + 1)
                if h >= 1:
                    act.wait_ge(sem("st_zread"), h)
                for b, (off, w) in enumerate(PIECES):
                    ins = act.activation(ln1[:, off:off + w], att_bank[b][:, :w], ACT.Abs)
                ins.then_inc(sem("st_act"), 1)
                act.wait_ge(sem("st_act"), 2 * h + 1)
                act.activation(ln1[:, :], ln1[:, :], ACT.Exp, scale=-1.0).then_inc(sem("st_act"), 1)
                act.wait_ge(sem("st_act"), 2 * h + 2)
                act.activation(ln1[:, :], ln1[:, :], ACT.Ln, bias=1.0).then_inc(sem("st_ln"), 1)

            pre(0)
            for h in range(HEADS + 1):
                if h + 1 < HEADS:
                    pre(h + 1)
                if h < HEADS:
                    act.wait_ge(sem("st_logw"), h + 1)
                    act.activation(wgt[h % 2][:, :], wgt[h % 2][:, :], ACT.Exp).then_inc(sem("st_w"), 1)
                if h >= 1:
                    r = (h - 1) % 2 * HD
                    act.wait_ge(sem("st_pv"), h)
                    act.activation(attn[r:r + HD, (h - 1) // 2, :], lin_bank[3][r:r + HD, :], ACT.Copy)\
                       .then_inc(sem("st_o"), 1)
                if h == HEADS - 1:
                    for k in range(CT):
                        act.wait_ge(sem("ln_xc"), k + 1)
                        act.activation(ln_sq[:, k, :], cacc[:, k, :], ACT.Square).then_inc(sem("ln_sq"), 1)
            act.wait_ge(sem("ln_var"), 1)
            act.activation(ln_std[:, :], att_bank[3][:, :], ACT.Sqrt, bias=eps[:, 0:1], scale=1.0 / CW)\
               .then_inc(sem("ln_std"), 1)
            act.wait_ge(sem("st_o"), HEADS)
            for k in range(CT):
                act.activation(xh[:, k, :], attn[:, k, :], ACT.Copy).then_inc(sem("mix1_hi"), 1)
            for k in range(CT):
                act.wait_ge(sem("ln_y"), k + 1)
                act.activation(cacc[:, k, :], cacc[:, k, :], ACT.Silu, bias=col("ln_b", k), scale=col("ln_g", k))\
                   .then_inc(sem("ln_c"), 1)
                act.wait_ge(sem("ln_c"), k + 1)
                act.activation(xh[:, CT + k, :], cacc[:, k, :], ACT.Copy).then_inc(sem("mix1_hi"), 1)
            splits_and_squares(act, "out1")
            norm_act(act, "n2", nrm2, norm_stat2, xh, S, "out1")
            j = 0
            for half in range(2):
                up, down = LAYER[f"up{half}"], LAYER[f"down{half}"]
                for b in range(FHALF[half]):
                    act.wait_ge(sem("ff_conv"), j + 1)
                    act.activation(f_silu[j % 2][:, :], f_conv[j % 2][:, :], ACT.Silu).then_inc(sem("ff_silu"), 1)
                    act.wait_ge(sem("bank_free"), 4 + up["tile"] + 2 * (b + 1))
                    act.activation(fh[:, b, :], f_out[j % 2][:, :], ACT.Copy).then_inc(sem("ff_hi"), 1)
                    split_hi(act, up["block"] + b + 2)
                    j += 1
                if half:
                    splits_and_squares(act, "down1")
                else:
                    for b in range(8):
                        split_hi(act, down["block"] + b + 2)

        def block1_pool(pool):
            split_lo(pool, 0)
            norm_pool(pool, "n1", nrm1, xh, xl, S)
            for b in range(1, LAYER["out1"]["block"] + 2):
                split_lo(pool, b)
            wait(pool, ("bank_free", 4 + 16), ("params_loaded", 16))
            conv_pool(pool)
            for b in range(LAYER["out1"]["block"] + 2, LAYER["up0"]["block"] + 2):
                split_lo(pool, b)
            norm_pool(pool, "n2", nrm2, xh, xl, S)
            j = 0
            for half in range(2):
                up, down = LAYER[f"up{half}"], LAYER[f"down{half}"]
                for b in range(FHALF[half]):
                    pool.wait_ge(sem("ff_hi"), j + 1)
                    pool.tensor_tensor(fl[:, b, :], f_out[j % 2][:, :], fh[:, b, :].bitcast(F32), ALU.subtract)\
                        .then_inc(sem("ff_lo"), 1)
                    split_lo(pool, up["block"] + b + 2)
                    j += 1
                for b in range(8):
                    split_lo(pool, down["block"] + b + 2)

        def block1_pe(pe):
            wait(pe, ("consts", N_CONST))
            norm_pe(pe, "n1", nrm1, norm_diag1, S)
            linear_pe(pe, "in_fm", weights_first("in_fm", xh, xl), S, follow_norm(pe, "n1"))
            for j in range(8):
                pe.wait_ge(sem("qk_sq"), j + 1)
                last = pe.matmul(att_bank[0][0:16, :], head_sum[:, j, :], qk_sq[:, j, :], start=(j == 0), stop=(j == 7))
            last.then_inc(sem("qk_sum"), 1)
            linear_pe(pe, "in_v", tokens_first("in_v", xh, xl), 256)
            pe.wait_ge(sem("qk_rstd"), 1)
            for j in range(8):
                if j >= 2:
                    pe.wait_ge(sem("qk_ready"), j - 1)
                pe.matmul(att_bank[1 + j % 2][:, :], head_spread[:, j * P:(j + 1) * P], rstd16[:, :],
                          start=True, stop=True).then_inc(sem("qk_spread"), 1)

            def scores(h):
                r, t = h % 2 * HD, h // 2
                pe.wait_ge(sem("qk_ready"), 8)
                if h >= 1:
                    pe.wait_ge(sem("st_zread"), h)
                for kb in range(QT):
                    b, c, w = regions(kb)
                    last = pe.matmul(att_bank[b][:, c:c + w], qk[r:r + HD, 4 + t, kb * P:(kb + 1) * P],
                                     qk[r:r + HD, t, kb * P:S], start=True, stop=True)
                last.then_inc(sem("st_z"), 1)

            def tails(h):
                pe.wait_ge(sem("st_soft"), h + 1)
                if h >= 1:
                    pe.wait_ge(sem("st_logw"), h)
                else:
                    pe.wait_ge(sem("bank_free"), 4 + LAYER["in_v"]["tile"] + 8)
                for kb in range(QT):
                    b, c, w = regions(kb)
                    for jb in range(kb, QT):
                        wj = S - jb * P
                        last = pe.matmul(lin_bank[b][:, c + w - wj:c + w], later_key[:, :] if jb == kb else ones[:, :],
                                         soft[h % 2][:, KOFF[jb]:KOFF[jb] + wj], start=(jb == kb), stop=(jb == QT - 1))
                last.then_inc(sem("st_tail"), 1)

            def values(h):
                r = h % 2 * HD
                pe.wait_ge(sem("st_wm"), h + 1)
                if h >= 2:
                    pe.wait_ge(sem("st_o"), h - 1)
                for kb in range(QT):
                    last = pe.matmul(lin_bank[3][r:r + HD, kb * P:S], vtok[:, kb, h * HD:(h + 1) * HD],
                                     wgt[h % 2][:, KOFF[kb]:KOFF[kb] + S - kb * P], start=(kb == 0), stop=(kb == QT - 1))
                last.then_inc(sem("st_pv"), 1)

            def mean():
                conv_done(pe)
                for k in range(CT):
                    last = pe.matmul(att_bank[3][:, :], ones[:, :], cacc[:, k, :], start=(k == 0), stop=(k == CT - 1))
                last.then_inc(sem("ln_mean"), 1)

            def variance():
                pe.wait_ge(sem("ln_xc"), CT)
                for k in range(CT):
                    pe.wait_ge(sem("ln_sq"), k + 1)
                    last = pe.matmul(att_bank[3][:, :], ones[:, :], ln_sq[:, k, :], start=(k == 0), stop=(k == CT - 1))
                last.then_inc(sem("ln_var"), 1)

            scores(0)
            for h in range(HEADS + 1):
                if h + 1 < HEADS:
                    scores(h + 1)
                if h < HEADS:
                    tails(h)
                if h == HEADS:
                    variance()
                if h >= 1:
                    values(h - 1)
                if h == HEADS - 1:
                    mean()
            linear_pe(pe, "out1", weights_first("out1", xh, xl), S, follow(pe, "mix1_lo"))
            norm_pe(pe, "n2", nrm2, norm_diag2, S)
            done = 0
            for half in range(2):
                linear_pe(pe, f"up{half}", weights_first(f"up{half}", xh, xl), S,
                          None if half else follow_norm(pe, "n2"))
                done += FHALF[half]
                pe.wait_ge(sem("ff_lo"), done)
                linear_pe(pe, f"down{half}", weights_first(f"down{half}", fh, fl), S)

        def add_to_resid(dve, name, norm=None):
            for n in range(KD):
                bank = tile_ready(dve, name, n)
                dve.tensor_tensor(resid[:, n, :], bank[:, :], resid[:, n, :], ALU.add).then_inc(sem("bank_free"), 1)
                if norm and n >= 2:
                    add_squares(dve, norm, nrm2, S, n - 1)
            if norm:
                add_squares(dve, norm, nrm2, S, KD - 1)

        def block1_dve(dve, chain):
            for k in range(1, KD):
                add_squares(dve, "n1", nrm1, S, k)
            wait(dve, ("params_loaded", 16), ("x_loaded0", 16), ("x_loaded1", 16))
            chain.link(dve.tensor_scalar(qg[:, :], col("q_norm"), HD ** -0.5, None, ALU.mult))
            norm_dve(dve, chain, "n1", resid, nrm1, norm_stat1, norm_diag1, xh, xl, "norm1", S)
            for n in range(8):
                bank = tile_ready(dve, "in_fm", n)
                dve.tensor_copy(qk[:, n, :], bank[:, :]).then_inc(sem("bank_free"), 1)
            for j in range(CT):
                bank = tile_ready(dve, "in_fm", 8 + 2 * j)
                dve.wait_ge(sem("glu_sig"), j + 1)
                dve.tensor_tensor(cpad[:, j, TAPS - 1:], bank[:, :], glu_sig[j % 2][:, :], ALU.mult)\
                   .then_inc(sem("bank_free"), 2)
            for n in range(8):
                bank = tile_ready(dve, "in_v", n)
                dve.tensor_copy(vtok[:, n % QT, n // QT * 256:(n // QT + 1) * 256], bank[:, :256])\
                   .then_inc(sem("bank_free"), 1)
                if n == 2:
                    dve.wait_ge(sem("qk_std"), 1)
                    dve.reciprocal(rstd16[:, :], std16[:, :]).then_inc(sem("qk_rstd"), 1)
            for j in range(8):
                dve.wait_ge(sem("qk_spread"), j + 1)
                gain = qg[:, 0:1] if j < 4 else col("k_norm")
                dve.scalar_tensor_tensor(out=qk[:, j, :], in0=qk[:, j, :], scalar=gain, in1=att_bank[1 + j % 2][:, :],
                                         op0=ALU.mult, op1=ALU.mult).then_inc(sem("qk_ready"), 1)

            def mask_diagonals(x):
                for part in (x[:, :2 * S].rearrange("p (b c) -> p b c", b=2)[:, :, :P],
                             x[:, KOFF[3]:KOFF[2] + P].rearrange("p (b c) -> p b c", b=2)):
                    ins = dve.tensor_tensor(part, part, causal[:, :].unsqueeze(1).to_broadcast([P, 2, P]), ALU.mult)
                return ins

            def softplus(h):
                dve.wait_ge(sem("st_ln"), h + 1)
                if h >= 2:
                    dve.wait_ge(sem("st_tail"), h - 1)
                for b, (off, w) in enumerate(PIECES):
                    ins = dve.scalar_tensor_tensor(out=soft[h % 2][:, off:off + w], in0=att_bank[b][:, :w], scalar=0.0,
                                                   in1=ln1[:, off:off + w], op0=ALU.max, op1=ALU.add)
                for b, (off, w) in enumerate(PIECES):
                    ins = dve.scalar_tensor_tensor(out=lbeta[h % 2][:, off:off + w], in0=att_bank[b][:, :w], scalar=0.0,
                                                   in1=ln1[:, off:off + w], op0=ALU.min, op1=ALU.subtract)
                ins.then_inc(sem("st_zread"), 1)
                dve.wait_ge(sem("st_zread"), h + 1)
                mask_diagonals(soft[h % 2]).then_inc(sem("st_soft"), 1)

            def log_weights(h):
                dve.wait_ge(sem("st_tail"), h + 1)
                dve.wait_ge(sem("st_zread"), h + 1)
                if h >= 2:
                    dve.wait_ge(sem("st_pv"), h - 1)
                for b, (off, w) in enumerate(PIECES):
                    ins = dve.tensor_tensor(wgt[h % 2][:, off:off + w], lbeta[h % 2][:, off:off + w],
                                            lin_bank[b][:, :w], ALU.subtract)
                ins.then_inc(sem("st_logw"), 1)

            softplus(0)
            per_head = -(-N_CONV // (HEADS - 1))
            for h in range(HEADS + 1):
                conv_dve(dve, h * per_head, (h + 1) * per_head)
                if h >= 1:
                    dve.wait_ge(sem("st_w"), h)
                    mask_diagonals(wgt[(h - 1) % 2]).then_inc(sem("st_wm"), 1)
                if h < HEADS:
                    log_weights(h)
                if h + 1 < HEADS:
                    softplus(h + 1)
                if h == HEADS - 1:
                    conv_done(dve)
                    dve.wait_ge(sem("ln_mean"), 1)
                    for k in range(CT):
                        dve.scalar_tensor_tensor(out=cacc[:, k, :], in0=att_bank[3][:, :], scalar=-1.0 / CW, in1=cacc[:, k, :],
                                                 op0=ALU.mult, op1=ALU.add).then_inc(sem("ln_xc"), 1)
            def mixed_low(k):
                src = attn[:, k, :] if k < CT else cacc[:, k - CT, :]
                dve.wait_ge(sem("mix1_hi"), k + 1)
                dve.tensor_tensor(xl[:, k, :], src, xh[:, k, :].bitcast(F32), ALU.subtract).then_inc(sem("mix1_lo"), 1)

            dve.wait_ge(sem("ln_std"), 1)
            chain.link(dve.reciprocal(ln_rstd[:, :], ln_std[:, :]))
            for k in range(CT):
                dve.tensor_tensor(cacc[:, k, :], cacc[:, k, :], ln_rstd[:, :], ALU.mult).then_inc(sem("ln_y"), 1)
                mixed_low(k)
            for k in range(CT, KD):
                mixed_low(k)
            add_to_resid(dve, "out1", "n2")
            norm_dve(dve, chain, "n2", resid, nrm2, norm_stat2, norm_diag2, xh, xl, "norm2", S)
            j = 0
            for half in range(2):
                for b in range(FHALF[half]):
                    gate = tile_ready(dve, f"up{half}", 2 * b)
                    y = f_conv[j % 2]

                    def tap(k):
                        return col("ffn_w", j * FTAPS + k)
                    chain.link(dve.tensor_scalar(y[:, :], gate[:, :], tap(2), col("ffn_b", j), ALU.mult, ALU.add))
                    chain.link(dve.scalar_tensor_tensor(out=y[:, 1:], in0=gate[:, :S - 1], scalar=tap(1), in1=y[:, 1:],
                                                        op0=ALU.mult, op1=ALU.add))
                    dve.scalar_tensor_tensor(out=y[:, 2:], in0=gate[:, :S - 2], scalar=tap(0), in1=y[:, 2:],
                                             op0=ALU.mult, op1=ALU.add).then_inc(sem("ff_conv"), 1)
                    value = tile_ready(dve, f"up{half}", 2 * b + 1)
                    dve.wait_ge(sem("ff_silu"), j + 1)
                    if j >= 2:
                        dve.wait_ge(sem("ff_lo"), j - 1)
                    dve.tensor_tensor(f_out[j % 2][:, :], value[:, :], f_silu[j % 2][:, :], ALU.mult)\
                       .then_inc(sem("bank_free"), 2)
                    j += 1
                add_to_resid(dve, f"down{half}", "n3" if half else None)

        N_CONST = 21

        def make_consts(pool):
            done = [0]

            def step(ins):
                done[0] += 1
                ins.then_inc(sem("consts"), 1)
                pool.wait_ge(sem("consts"), done[0])

            pool.nop().then_inc(sem("bank_free"), 4)
            pool.nop().then_inc(sem("lo_done"), 2)
            peer_credits(pool)
            step(pool.memset(eps[:, :], EPS))
            step(pool.memset(ones[:, :], 1.0))
            step(pool.memset(head_sum[:, :, :], 0.0))
            step(pool.memset(head_spread[:, :], 1.0))
            step(pool.memset(cpad[:, :, 0:TAPS - 1], 0.0))
            step(pool.memset(cmp_valid[:, :, :], 1.0))
            step(pool.iota(iota16[:, :], [[1, PK]], base=0, channel_multiplier=0, allow_small_or_imprecise_dtypes=True))
            step(pool.iota(iota_key[:, :], [[1, NK]], base=0, channel_multiplier=0,
                           allow_small_or_imprecise_dtypes=True))
            step(pool.iota(dist[:, :], [[1, S]], base=P - S, channel_multiplier=-1,
                           allow_small_or_imprecise_dtypes=True))
            step(pool.iota(cmp_dist[:, :, :], [[-P, QT], [CMP, NCMP]], base=CMP - 1, channel_multiplier=-1,
                           allow_small_or_imprecise_dtypes=True))
            step(pool.memset(ident[:, :], 0.0))
            step(pool.affine_select(out=ident[:, :], in_=ident[:, :], compare_op=ALU.not_equal, fill=1.0, base=0,
                                    pattern=[[-1, P]], channel_multiplier=1))
            step(pool.affine_select(out=later_key[:, :], in_=ones[:, :], compare_op=ALU.is_gt, fill=0.0, base=0,
                                    pattern=[[-1, P]], channel_multiplier=1))
            step(pool.affine_select(out=causal[:, :], in_=ones[:, :], compare_op=ALU.is_gt, fill=0.0, base=0,
                                    pattern=[[1, P]], channel_multiplier=-1))
            step(pool.affine_select(out=dist[:, :], in_=dist[:, :], compare_op=ALU.is_ge, fill=NEG, base=S - P,
                                    pattern=[[-1, S]], channel_multiplier=1))
            step(pool.affine_select(out=cmp_dist[:, :, :], in_=cmp_dist[:, :, :], compare_op=ALU.is_ge, fill=NEG,
                                    base=1 - CMP, pattern=[[P, QT], [-CMP, NCMP]], channel_multiplier=1))
            step(pool.affine_select(out=cmp_valid[:, :, :], in_=cmp_valid[:, :, :], compare_op=ALU.is_ge, fill=0.0,
                                    base=1 - CMP, pattern=[[P, QT], [-CMP, NCMP]], channel_multiplier=1))
            sums = head_sum[:, :, :].rearrange("p j c -> p (j c)")
            step(pool.memset(sums[0:HD, 0:P:18], 1.0))
            step(pool.memset(sums[HD:P, 1:P:18], 1.0))
            step(pool.affine_select(out=head_spread[:, :], in_=head_spread[:, :], compare_op=ALU.is_ge, fill=0.0, base=0,
                                    pattern=[[1, 8 * P]], channel_multiplier=-HD))
            step(pool.affine_select(out=head_spread[:, :], in_=head_spread[:, :], compare_op=ALU.is_ge, fill=0.0,
                                    base=HD - 1, pattern=[[-1, 8 * P]], channel_multiplier=HD))
            assert done[0] == N_CONST

        def scr(kb):
            return SCR + int(kb * KB)

        qa = at("qa", [P, DA_H, S], scr(0))
        ka = at("ka", [P, DA_H, S], scr(8))
        qb = at("qb", [P, NSA_H // 2, S], scr(16))
        ks = [at(f"ks{i}", [P, S], scr(24 + 2 * i)) for i in range(2)]
        kw = [at(f"kw{i}", [P, S], scr(28 + 2 * i)) for i in range(2)]
        va = at("va", [P, QT, AW], scr(32))
        vsw = at("vsw", [P, QT, 256], scr(40))
        cmp_in = [at(f"cmp_in{i}", [P, CMP // 2, NSA_G, NCMP], scr(44 + 2 * i)) for i in range(2)]
        slope_dist = [at(f"slope_dist{i}", [P, S], scr(44 + 2 * i)) for i in range(2)]
        cmp_hid = [at(f"cmp_hid{i}", [P, 2, NSA_G * NCMP], scr(48 + 0.25 * i)) for i in range(2)]
        kc_t = at("kc_t", [P, NSA_G * NCMP], scr(48.5))
        cmp_stat = at("cmp_stat", [P, QT, NSA_H], scr(48.75))
        cmp_rec = at("cmp_rec", [P, QT, NSA_H], scr(48.875))
        vc_blk = at("vc_blk", [P, NSA_H, HD], scr(49))
        cmp_bias = at("cmp_bias", [P, QT, NSA_H, NCMP], scr(51))
        cmp_s = at("cmp_s", [P, QT, NSA_H, NCMP], scr(53))
        cmp_p = at("cmp_p", [P, QT, NSA_H, 32], scr(55))
        cmp_pt = at("cmp_pt", [P, QT, NSA_G, P], scr(51))
        cmp_w1 = [at(f"cmp_w1_{i}", [P, CMP // 2, CMP_HID], scr(60 + 16 * i)) for i in range(2)]
        cmp_w2 = [at(f"cmp_w2_{i}", [P, 2, HD], scr(92 + 0.5 * i)) for i in range(2)]
        att_e = [at(f"att_e{i}", [P, 2, S], scr(x)) for i, x in enumerate((60, 64, 68, 55))]
        att_pt = [at(f"att_pt{i}", [P, 2, S], scr(72 + 4 * i)) for i in range(2)]
        oab = at("oab", [P, KD, S], scr(80))
        stat = at("att_stat", [P, 4, 4, 2], scr(96))
        sub_sq = at("sub_sq", [P, DA_H, S], scr(60))
        sub_std = at("sub_std", [P, DA_H, S], scr(68))
        sig = at("sig", [P, 2 * KD, S], scr(0))
        oh = at("oh", [P, KD, S], scr(32), F32R)
        ol = at("ol", [P, KD, S], scr(48), F32R)
        part_a = [at(f"part_a{i}", [P, S], scr(64 + 2 * i)) for i in range(2)]
        part_b = [at(f"part_b{i}", [P, S], scr(68 + 2 * i)) for i in range(2)]
        mem = at("mem", [P, KD, MEM], scr(0))
        mem_n = at("mem_n", [P, KD, MEM], scr(8))
        mem_stat = at("mem_stat", [P, 2 * QT], scr(16))
        mem_diag = at("mem_diag", [P, MEM], scr(17))
        mem_h = at("mem_h", [P, KD, MEM], scr(18), F32R)
        mem_l = at("mem_l", [P, KD, MEM], scr(26), F32R)
        cq = at("cq", [P, CA_H, S], scr(34))
        ck = at("ck", [P, CA_H, MEM], scr(42))
        cv = at("cv", [P, MEM // P, CA_H * P], scr(46))
        ca_e = [at(f"ca_e{i}", [P, MEM], scr(50 + i)) for i in range(4)]
        ca_pt = [at(f"ca_pt{i}", [P, MEM], scr(54 + i)) for i in range(2)]
        ca_stat = at("ca_stat", [P, 4, 4], scr(56))

        CA_SCALE = (CA_H * P // CA_H) ** -0.5
        MIXED = LAYER["mix_tm"]["tile"] + 16

        UNITS = [("a", h, i) for h in range(DA_H) for i in range(QT)] + [("b", h, i) for h in range(NSA_H) for i in range(QT)]
        N_A = DA_H * QT
        NU = len(UNITS)

        def items(u):
            return [u] if u < N_A else [N_A + 2 * (u - N_A), N_A + 2 * (u - N_A) + 1]

        def head_no(u):
            return u // QT

        def unit_maps(u):
            kind, h, i = UNITS[u]
            if kind == "a":
                return [(qa[c * HD:(c + 1) * HD, h, i * P:(i + 1) * P], ka[c * HD:(c + 1) * HD, h, :]) for c in range(2)]
            r = h % 2 * HD
            swap = 0 if h // NSA_R == h % 2 else 1
            q = qb[r:r + HD, h // 2, i * P:(i + 1) * P]
            return [(q, ks[swap][r:r + HD, :]), (q, kw[swap][r:r + HD, :])]

        def slope(u):
            kind, h, _ = UNITS[u]
            return 2.0 ** (-8.0 * (h + 1) / (DA_H if kind == "a" else NSA_H))

        def block2_pool(pool):
            norm_pool(pool, "n3", nrm2, xh, xl, S)
            norm_done(pool, "n3")
            pool.memset(vc_blk[:, :, :], 0.0).then_inc(sem("cmp_zero"), 1)
            pool.memset(cmp_p[:, :, :, :], 0.0).then_inc(sem("cmp_zero"), 1)
            for b in range(LAYER["mix_fm"]["block"] + 2, LAYER["cross_q"]["block"] + 2):
                split_lo(pool, b)
            norm_pool(pool, "n4", nrm2, xh, xl, S)
            for b in range(LAYER["cross_q"]["block"] + 2, LAYER["cross_k"]["block"] + 2):
                split_lo(pool, b)
            norm_pool(pool, "nm", mem_n, mem_h, mem_l, MEM)
            for b in range(LAYER["cross_k"]["block"] + 2, LAYER["peer_q"]["block"] + 2):
                split_lo(pool, b)

        def block2_act(act):
            def splits(name, first=0, last=None):
                t = LAYER[name]
                for b in range(first, t["nb"] if last is None else last):
                    split_hi(act, t["block"] + b + 2)

            norm_act(act, "n3", nrm2, norm_stat2, xh, S, "down1")
            splits("mix_fm")
            splits("mix_tm", 0, 2)

            def hidden(v):
                act.wait_ge(sem("cmp_h"), v + 1)
                act.activation(cmp_hid[v][:, :, :].rearrange("p m n -> p (m n)"), att_bank[2 * v][:, 0:2 * NSA_G * NCMP],
                               ACT.Gelu).then_inc(sem("cmp_hid"), 1)

            hidden(0)
            splits("mix_tm", 2, 3)
            act.wait_ge(sem("bank_free"), 4 + LAYER["mix_tm"]["tile"] + 3 * QT)
            for n in range(QT):
                bank = tile_ready(act, "mix_tm", 3 * QT + n)
                act.activation(gates24[:, n, :], bank[:, :NSA_H * 3], ACT.Sigmoid).then_inc(sem("bank_free"), 1)
            act.wait_ge(sem("lam_sum"), 1)
            act.activation(lam_exp[:, :], att_bank[3][:, 0:2], ACT.Exp).then_inc(sem("lam_exp"), 1)
            act.wait_ge(sem("cmp_sub"), 1)
            act.activation(cmp_s[:, :, :, :], cmp_s[:, :, :, :], ACT.Exp).then_inc(sem("cmp_exp"), 1)
            hidden(1)
            splits("mix_tm", 3)

            def exps(u):
                w = (UNITS[u][2] + 1) * P
                act.wait_ge(sem("at_nm"), u + 1)
                for c in range(2):
                    e = att_e[u % 4][:, c, :w]
                    act.activation(e, e, ACT.Exp, bias=stat[:, u % 4, 1, c:c + 1],
                                   accum_out=stat[:, u % 4, 2, c:c + 1]).then_inc(sem("at_exp"), 1)

            def transposed(u):
                w = (UNITS[u][2] + 1) * P
                if u >= 2:
                    act.wait_ge(sem("at_pv"), u - 1)
                for c, n in enumerate(items(u)):
                    act.wait_ge(sem("at_t"), n + 1)
                    act.activation(att_pt[u % 2][:, c, :w], lin_bank[n % 2][:, :w], ACT.Copy).then_inc(sem("at_pt"), 1)

            def outputs(u):
                kind, h, i = UNITS[u]
                if i < QT - 1:
                    return
                act.wait_ge(sem("at_pv"), u + 1)
                bank = lin_bank[2 + head_no(u) % 2]
                if kind == "a":
                    ins = act.activation(oab[:, h, :], bank[:, :], ACT.Copy)
                else:
                    r = h % 2 * HD
                    ins = act.activation(oab[r:r + HD, DA_H + h // 2, :], bank[r:r + HD, :], ACT.Copy)
                ins.then_inc(sem("at_o"), 1)

            for s in range(NU + 3):
                if s < NU:
                    exps(s)
                if 2 <= s <= NU + 1:
                    transposed(s - 2)
                if s >= 3:
                    outputs(s - 3)
            for h in range(DA_H):
                act.activation(sub_sq[:, h, :], oab[:, h, :], ACT.Square).then_inc(sem("sub_sq"), 1)
            for h in range(DA_H):
                act.wait_ge(sem("sub_sum"), h + 1)
                act.activation(sub_std[:, h, :], att_bank[h][:, :], ACT.Sqrt, bias=eps[:, 0:1], scale=1.0 / P)\
                   .then_inc(sem("sub_std"), 1)
            for k in range(KD):
                if k < DA_H:
                    act.wait_ge(sem("sub_y"), k + 1)
                act.activation(oh[:, k, :], oab[:, k, :], ACT.Copy).then_inc(sem("oab_hi"), 1)
            for b in range(8):
                for n in range(2):
                    bank = tile_ready(act, "gates", 2 * b + n)
                    act.activation(sig[:, 2 * b + n, :], bank[:, :], ACT.Sigmoid).then_inc(sem("bank_free"), 1)
                split_hi(act, LAYER["gates"]["block"] + b + 2)
            for m in range(KD):
                act.wait_ge(sem("br_sum"), m + 1)
                act.activation(xh[:, m, :], part_a[m % 2][:, :], ACT.Copy).then_inc(sem("br_hi"), 1)
                if m % 2:
                    split_hi(act, LAYER["branch"]["block"] + m // 2 + 2)
            splits_and_squares(act, "out2")
            norm_act(act, "n4", nrm2, norm_stat2, xh, S, "out2")
            act.wait_ge(sem("mem_loaded"), 16)
            squares(act, mem, mem_n, MEM)
            splits("cross_q")
            norm_act(act, "nm", mem_n, mem_stat, mem_h, MEM)
            splits("cross_k")
            splits("cross_v")

            def ca_exp(u):
                act.wait_ge(sem("ca_nm"), u + 1)
                act.activation(ca_e[u % 4][:, :], att_bank[u % 4][:, :MEM], ACT.Exp, bias=ca_stat[:, u % 4, 1:2],
                               scale=CA_SCALE, accum_out=ca_stat[:, u % 4, 2:3]).then_inc(sem("ca_exp"), 1)

            def ca_transposed(u):
                if u >= 2:
                    act.wait_ge(sem("ca_pv"), u - 1)
                act.wait_ge(sem("ca_t"), u + 1)
                act.activation(ca_pt[u % 2][:, :], lin_bank[u % 2][:, :MEM], ACT.Copy).then_inc(sem("ca_pt"), 1)

            for s in range(CA_H * QT + 3):
                if s < CA_H * QT:
                    ca_exp(s)
                if 2 <= s <= CA_H * QT + 1:
                    ca_transposed(s - 2)
                u = s - 3
                if u >= 0 and u % QT == QT - 1:
                    h = u // QT
                    act.wait_ge(sem("ca_pv"), u + 1)
                    act.activation(xh[:, h, :], lin_bank[2 + h % 2][:, :], ACT.Copy).then_inc(sem("ca_hi"), 1)
            splits_and_squares(act, "cross_o")

        def block2_pe(pe):
            norm_pe(pe, "n3", nrm2, norm_diag2, S)
            pe.wait_ge(sem("lam_prod"), 1)
            pe.matmul(att_bank[3][:, 0:2], ones[0:HD, :], lam_prod[0:HD, :], start=True, stop=True)\
              .then_inc(sem("lam_sum"), 1)
            linear_pe(pe, "mix_fm", weights_first("mix_fm", xh, xl), S, follow_norm(pe, "n3"))
            NC2 = NSA_G * NCMP
            HALF = LAYER["mix_tm"]["unroll"] * QT
            PER_TILE = CMP // HALF

            def first_layer(v, part):
                if part == 0:
                    wait(pe, ("cmp_loaded", 64), ("cmp_in", 4 * (v + 1)))
                m, first = part * PER_TILE // (CMP // 2), part * PER_TILE % (CMP // 2)
                for lp in range(first, first + PER_TILE):
                    last = pe.matmul(att_bank[2 * v][:, m * NC2:(m + 1) * NC2], cmp_w1[v][:, lp, m * P:(m + 1) * P],
                                     cmp_in[v][:, lp, :, :].rearrange("p g b -> p (g b)"),
                                     start=(lp == 0), stop=(lp == CMP // 2 - 1))
                if part == HALF - 1:
                    last.then_inc(sem("cmp_h"), 1)

            def compressed_keys():
                pe.wait_ge(sem("cmp_hid"), 1)
                for m in range(2):
                    last = pe.matmul(att_bank[0][0:HD, 0:NC2], cmp_w2[0][:, m, :], cmp_hid[0][:, m, :],
                                     start=(m == 0), stop=(m == 1))
                last.then_inc(sem("cmp_k"), 1)

            def compressed_scores(i):
                pe.wait_ge(sem("cmp_kc"), 2)
                for h in range(NSA_H):
                    r, g = h % 2 * HD, h // NSA_R
                    n = (i * NSA_H // 2 + h // 2) * NCMP
                    last = pe.matmul(att_bank[h % 2][:, n:n + NCMP], qb[r:r + HD, h // 2, i * P:(i + 1) * P],
                                     kc_t[r:r + HD, g * NCMP:(g + 1) * NCMP], start=True, stop=True)
                if i == QT - 1:
                    last.then_inc(sem("cmp_scores"), 1)

            def compression(n):
                first_layer(n // HALF, n % HALF)
                if n == HALF:
                    compressed_keys()
                if HALF + 2 <= n < HALF + 2 + QT:
                    compressed_scores(n - HALF - 2)

            linear_pe(pe, "mix_tm", tokens_first("mix_tm", xh, xl), 256, between=compression)
            pe.wait_ge(sem("cmp_hid"), 2)
            pe.wait_ge(sem("lam_exp"), 1)
            for g in range(NSA_G):
                for m in range(2):
                    last = pe.matmul(att_bank[3][0:NCMP, g * HD:(g + 1) * HD], cmp_hid[1][:, m, g * NCMP:(g + 1) * NCMP],
                                     cmp_w2[1][:, m, :], start=(m == 0), stop=(m == 1))
            last.then_inc(sem("cmp_v"), 1)
            pe.wait_ge(sem("cmp_p"), 1)
            for i in range(QT):
                for g in range(NSA_G):
                    n = i * NSA_G + g
                    src = cmp_p[:, i, g * NSA_R:(g + 1) * NSA_R, :].rearrange("p h c -> p (h c)")
                    last = pe.transpose(att_bank[1 + n // 4][:, n % 4 * P:(n % 4 + 1) * P], src, ident[:, :])
            last.then_inc(sem("cmp_t"), 1)

            def scores(u):
                w = (UNITS[u][2] + 1) * P
                for c, (q, k) in enumerate(unit_maps(u)):
                    if u >= 2:
                        pe.wait_ge(sem("at_max"), 2 * (u - 2) + c + 1)
                    pe.matmul(att_bank[2 * (u % 2) + c][:, :w], q, k[:, :w], start=True, stop=True)\
                      .then_inc(sem("at_s"), 1)

            def transposes(u):
                for c, n in enumerate(items(u)):
                    pe.wait_ge(sem("at_p"), n + 1)
                    if n >= 2:
                        pe.wait_ge(sem("at_pt"), n - 1)
                    for kb in range(UNITS[u][2] + 1):
                        last = pe.transpose(lin_bank[n % 2][:, kb * P:(kb + 1) * P],
                                            att_e[u % 4][:, c, kb * P:(kb + 1) * P], ident[:, :])
                    last.then_inc(sem("at_t"), 1)

            def values(u):
                kind, h, i = UNITS[u]
                pe.wait_ge(sem("at_pt"), items(u)[-1] + 1)
                if i == 0 and head_no(u) >= 2:
                    pe.wait_ge(sem("at_o"), head_no(u) - 1)
                bank = lin_bank[2 + head_no(u) % 2]
                if kind == "a":
                    out = bank[:, i * P:(i + 1) * P]
                    ops = [(va[:, kb, h * P:(h + 1) * P], att_pt[u % 2][:, 0, kb * P:(kb + 1) * P]) for kb in range(i + 1)]
                else:
                    r, g = h % 2 * HD, h // NSA_R
                    out = bank[r:r + HD, i * P:(i + 1) * P]
                    ops = [(vc_blk[:, h, :], cmp_pt[:, i, g, :])]
                    ops += [(vsw[:, kb, c * P + g * HD:c * P + (g + 1) * HD], att_pt[u % 2][:, c, kb * P:(kb + 1) * P])
                            for c in range(2) for kb in range(i + 1)]
                for n, (v, p) in enumerate(ops):
                    last = pe.matmul(out, v, p, start=(n == 0), stop=(n == len(ops) - 1))
                last.then_inc(sem("at_pv"), 1)

            wait(pe, ("bank_free", 4 + MIXED), ("cmp_pt", 2))
            for s in range(NU + 3):
                if s < NU:
                    scores(s)
                if 2 <= s <= NU + 1:
                    transposes(s - 2)
                if s >= 3:
                    values(s - 3)
            pe.wait_ge(sem("at_max"), 2 * NU)
            for h in range(DA_H):
                pe.wait_ge(sem("sub_sq"), h + 1)
                pe.matmul(att_bank[h][:, :], ones[:, :], sub_sq[:, h, :], start=True, stop=True)\
                  .then_inc(sem("sub_sum"), 1)
            pe.wait_ge(sem("at_o"), DA_H + NSA_H)
            linear_pe(pe, "gates", weights_first("gates", xh, xl), S)
            pe.wait_ge(sem("oab_lo"), KD)

            def branch_pairs(slot, m):
                half, out = m % 2, m // 2
                ks_ = range(4 * half, 4 * half + 4)
                return [(wh[slot][:, k * 256 + out * P:k * 256 + out * P + P],
                         wl[slot][:, k * 256 + out * P:k * 256 + out * P + P], oh[:, k, :], ol[:, k, :]) for k in ks_]

            linear_pe(pe, "branch", branch_pairs, S)
            linear_pe(pe, "out2", weights_first("out2", xh, xl), S, follow(pe, "br_lo"))
            norm_pe(pe, "n4", nrm2, norm_diag2, S)
            linear_pe(pe, "cross_q", weights_first("cross_q", xh, xl), S, follow_norm(pe, "n4"))
            norm_pe(pe, "nm", mem_n, mem_diag, MEM)
            linear_pe(pe, "cross_k", weights_first("cross_k", mem_h, mem_l, MEM), MEM, follow_norm(pe, "nm"))
            linear_pe(pe, "cross_v", tokens_first("cross_v", mem_h, mem_l), 256)
            pe.wait_ge(sem("bank_free"), 4 + LAYER["cross_o"]["tile"])
            n_ca = CA_H * QT
            for s in range(n_ca + 3):
                if s < n_ca:
                    h, i = s // QT, s % QT
                    if s >= 4:
                        pe.wait_ge(sem("ca_exp"), s - 3)
                    pe.matmul(att_bank[s % 4][:, :MEM], cq[:, h, i * P:(i + 1) * P], ck[:, h, :], start=True, stop=True)\
                      .then_inc(sem("ca_s"), 1)
                u = s - 2
                if 0 <= u < n_ca:
                    pe.wait_ge(sem("ca_p"), u + 1)
                    if u >= 2:
                        pe.wait_ge(sem("ca_pt"), u - 1)
                    for mt in range(MEM // P):
                        last = pe.transpose(lin_bank[u % 2][:, mt * P:(mt + 1) * P], ca_e[u % 4][:, mt * P:(mt + 1) * P],
                                            ident[:, :])
                    last.then_inc(sem("ca_t"), 1)
                u = s - 3
                if u >= 0:
                    h, i = u // QT, u % QT
                    pe.wait_ge(sem("ca_pt"), u + 1)
                    if i == 0 and h >= 2:
                        pe.wait_ge(sem("ca_lo"), h - 1)
                    for mt in range(MEM // P):
                        last = pe.matmul(lin_bank[2 + h % 2][:, i * P:(i + 1) * P], cv[:, mt, h * P:(h + 1) * P],
                                         ca_pt[u % 2][:, mt * P:(mt + 1) * P], start=(mt == 0), stop=(mt == 1))
                    last.then_inc(sem("ca_pv"), 1)
            linear_pe(pe, "cross_o", weights_first("cross_o", xh, xl), S, follow(pe, "ca_lo"))

        def block2_dve(dve, chain):
            p0 = PCOL["lam"]
            dve.tensor_tensor(lam_prod[:, :], params[:, p0:p0 + 4:2], params[:, p0 + 1:p0 + 4:2], ALU.mult)\
               .then_inc(sem("lam_prod"), 1)
            chain.link(dve.tensor_scalar(subln_g[:, :], col("subln"), 1.0 - LAMBDA_INIT, None, ALU.mult))
            norm_dve(dve, chain, "n3", resid, nrm2, norm_stat2, norm_diag2, xh, xl, "norm_mix", S)
            scale = HD ** -0.5
            for n in range(12):
                bank = tile_ready(dve, "mix_fm", n)
                out = (qa, ka, qb)[n // 4][:, n % 4, :]
                if n // 4 == 1:
                    ins = dve.tensor_copy(out, bank[:, :])
                else:
                    ins = dve.tensor_scalar(out, bank[:, :], scale, None, ALU.mult)
                ins.then_inc(sem("bank_free"), 1)
            for v in range(2):
                bank = tile_ready(dve, "mix_fm", 12 + v)
                for g in range(NSA_G):
                    rows = slice(g * HD, (g + 1) * HD)
                    tokens = bank[rows, :].rearrange("p (b l) -> p l b", l=CMP)
                    pos = params[rows, PCOL["cmp_pos"]:PCOL["cmp_pos"] + CMP]
                    for par in range(2):
                        dve.tensor_tensor(
                            cmp_in[v][par * HD:(par + 1) * HD, :, g, :], tokens[:, par::2, :],
                            pos[:, par::2].unsqueeze(2).to_broadcast([HD, CMP // 2, NCMP]), ALU.add)\
                           .then_inc(sem("cmp_in"), 1)
                dve.wait_ge(sem("cmp_in"), 4 * (v + 1))
                dve.sem_inc(sem("bank_free"), 1)
            for n, x in ((14, ks), (15, kw)):
                bank = tile_ready(dve, "mix_fm", n)
                dve.tensor_copy(x[0][:, :], bank[:, :])
                dve.tensor_copy(x[1][0:HD, :], bank[HD:P, :])
                dve.tensor_copy(x[1][HD:P, :], bank[0:HD, :]).then_inc(sem("bank_free"), 1)
            for n in range(3 * QT):
                bank = tile_ready(dve, "mix_tm", n)
                b, tt = n // QT, n % QT
                out = va[:, tt, b * 256:(b + 1) * 256] if b < 2 else vsw[:, tt, :]
                dve.tensor_copy(out, bank[:, :256]).then_inc(sem("bank_free"), 1)
                if n == 2 * QT:
                    dve.wait_ge(sem("cmp_k"), 1)
                    for half in range(2):
                        dve.tensor_copy(kc_t[half * HD:(half + 1) * HD, :], att_bank[0][0:HD, 0:NSA_G * NCMP])\
                           .then_inc(sem("cmp_kc"), 1)
            for h in range(NSA_H):
                ins = dve.tensor_scalar(cmp_bias[:, :, h, :], cmp_dist[:, :, :], 2.0 ** -(h + 1), None, ALU.mult)
            chain.link(ins)
            dve.wait_ge(sem("cmp_scores"), 1)
            flat = "p i h c -> p (i h) c"
            s3, b3 = cmp_s[:, :, :, :].rearrange(flat), cmp_bias[:, :, :, :].rearrange(flat)
            stat2, rec2 = cmp_stat[:, :, :].rearrange("p i h -> p (i h)"), cmp_rec[:, :, :].rearrange("p i h -> p (i h)")
            NIH = QT * NSA_H

            def spread(x):
                return x.unsqueeze(2).to_broadcast([P, NIH, NCMP])

            for odd in range(2):
                by_parity = "p i (h o) c -> p o (i h) c"
                ins = dve.tensor_tensor(cmp_s[:, :, :, :].rearrange(by_parity, o=2)[:, odd],
                                        att_bank[odd][:, :S // 2].rearrange("p (n c) -> p n c", c=NCMP),
                                        cmp_bias[:, :, :, :].rearrange(by_parity, o=2)[:, odd], ALU.add)
            chain.link(ins)
            chain.link(dve.tensor_reduce(stat2, s3, AX_X, ALU.max))
            dve.tensor_tensor(s3, s3, spread(stat2), ALU.subtract).then_inc(sem("cmp_sub"), 1)
            dve.wait_ge(sem("cmp_exp"), 1)
            chain.link(dve.tensor_reduce(stat2, s3, AX_X, ALU.add))
            chain.link(dve.reciprocal(rec2, stat2))
            chain.link(dve.tensor_tensor(cmp_rec[:, :, :], cmp_rec[:, :, :], gates24[:, :, 0::3], ALU.mult))
            for i in range(QT):
                ins = dve.tensor_tensor(cmp_s[:, i, :, :], cmp_s[:, i, :, :],
                                        cmp_valid[:, i, :].unsqueeze(1).to_broadcast([P, NSA_H, NCMP]), ALU.mult)
            chain.link(ins)
            padded = cmp_p[:, :, :, :].rearrange(flat)
            dve.wait_ge(sem("cmp_zero"), 2)
            dve.tensor_tensor(padded[:, :, 0:NCMP], s3, spread(rec2), ALU.mult).then_inc(sem("cmp_p"), 1)
            dve.wait_ge(sem("lam_exp"), 1)
            chain.link(dve.tensor_scalar(lam[:, :], lam_exp[:, 0:1], lam_exp[:, 1:2], LAMBDA_INIT, ALU.subtract, ALU.add))
            dve.wait_ge(sem("cmp_v"), 1)
            for h in range(NSA_H):
                g, r = h // NSA_R, h % NSA_R
                ins = dve.tensor_copy(vc_blk[32 * r:32 * r + NCMP, h, :], att_bank[3][0:NCMP, g * HD:(g + 1) * HD])
            chain.link(ins)
            dve.wait_ge(sem("cmp_t"), 1)
            turned = cmp_pt[:, :, :, :].rearrange("p i g t -> p (i g t)")
            for b in range(2):
                dve.tensor_copy(turned[:, b * S:(b + 1) * S], att_bank[1 + b][:, :]).then_inc(sem("cmp_pt"), 1)

            def maxima(u):
                kind, h, i = UNITS[u]
                w = (i + 1) * P
                sd = slope_dist[head_no(u) % 2]
                if i == 0:
                    chain.link(dve.tensor_scalar(sd[:, :], dist[:, :], slope(u), None, ALU.mult))
                if u >= 4:
                    dve.wait_ge(sem("at_t"), items(u - 4)[-1] + 1)
                for c in range(2):
                    dve.wait_ge(sem("at_s"), 2 * u + c + 1)
                    dve.tensor_tensor_reduce(out=att_e[u % 4][:, c, :w], in0=att_bank[2 * (u % 2) + c][:, :w],
                                             in1=sd[:, S - w:], scale=1.0, scalar=-3.0e38, op0=ALU.add, op1=ALU.max,
                                             accum_out=stat[:, u % 4, 0, c:c + 1]).then_inc(sem("at_max"), 1)
                dve.wait_ge(sem("at_max"), 2 * u + 2)
                dve.tensor_scalar(stat[:, u % 4, 1, :], stat[:, u % 4, 0, :], -1.0, None, ALU.mult).then_inc(sem("at_nm"), 1)

            def weights(u):
                kind, h, i = UNITS[u]
                w = (i + 1) * P
                e, factor = att_e[u % 4], stat[:, u % 4, 3, :]
                dve.wait_ge(sem("at_exp"), 2 * u + 2)
                chain.link(dve.reciprocal(factor, stat[:, u % 4, 2, :]))
                if kind == "a":
                    chain.link(dve.tensor_scalar(factor[:, 1:2], factor[:, 1:2], lam[:, 0:1], None, ALU.mult))
                    chain.link(dve.tensor_scalar(e[:, 1, :w], e[:, 1, :w], factor[:, 1:2], None, ALU.mult))
                    dve.scalar_tensor_tensor(out=e[:, 0, :w], in0=e[:, 0, :w], scalar=factor[:, 0:1], in1=e[:, 1, :w],
                                             op0=ALU.mult, op1=ALU.subtract).then_inc(sem("at_p"), 1)
                else:
                    chain.link(dve.tensor_tensor(factor, factor, gates24[:, i, 3 * h + 1:3 * h + 3], ALU.mult))
                    for c in range(2):
                        dve.tensor_scalar(e[:, c, :w], e[:, c, :w], factor[:, c:c + 1], None, ALU.mult)\
                           .then_inc(sem("at_p"), 1)

            for s in range(NU + 1):
                if s < NU:
                    maxima(s)
                if s >= 1:
                    weights(s - 1)
            for h in range(DA_H):
                dve.wait_ge(sem("sub_std"), h + 1)
                chain.link(dve.reciprocal(sub_std[:, h, :], sub_std[:, h, :]))
                dve.scalar_tensor_tensor(out=oab[:, h, :], in0=oab[:, h, :], scalar=subln_g[:, 0:1],
                                         in1=sub_std[:, h, :], op0=ALU.mult, op1=ALU.mult).then_inc(sem("sub_y"), 1)
            for k in range(KD):
                dve.wait_ge(sem("oab_hi"), k + 1)
                dve.tensor_tensor(ol[:, k, :], oab[:, k, :], oh[:, k, :].bitcast(F32), ALU.subtract)\
                   .then_inc(sem("oab_lo"), 1)
            dve.wait_ge(sem("bank_free"), 4 + LAYER["branch"]["tile"])
            for m in range(KD):
                a = tile_ready(dve, "branch", 2 * m)
                b = tile_ready(dve, "branch", 2 * m + 1)
                if m >= 2:
                    dve.wait_ge(sem("br_hi"), m - 1)
                dve.tensor_tensor(part_a[m % 2][:, :], a[:, :], sig[:, 2 * m, :], ALU.mult)
                dve.tensor_tensor(part_b[m % 2][:, :], b[:, :], sig[:, 2 * m + 1, :], ALU.mult)\
                   .then_inc(sem("bank_free"), 2)
                dve.wait_ge(sem("bank_free"), 4 + LAYER["branch"]["tile"] + 2 * (m + 1))
                dve.tensor_tensor(part_a[m % 2][:, :], part_a[m % 2][:, :], part_b[m % 2][:, :], ALU.add)\
                   .then_inc(sem("br_sum"), 1)
                dve.wait_ge(sem("br_hi"), m + 1)
                dve.tensor_tensor(xl[:, m, :], part_a[m % 2][:, :], xh[:, m, :].bitcast(F32), ALU.subtract)\
                   .then_inc(sem("br_lo"), 1)
            add_to_resid(dve, "out2", "n4")
            norm_dve(dve, chain, "n4", resid, nrm2, norm_stat2, norm_diag2, xh, xl, "norm_cross", S)
            for k in range(1, KD):
                add_squares(dve, "nm", mem_n, MEM, k)
            for n in range(CA_H):
                bank = tile_ready(dve, "cross_q", n)
                dve.tensor_copy(cq[:, n, :], bank[:, :]).then_inc(sem("bank_free"), 1)
            norm_dve(dve, chain, "nm", mem, mem_n, mem_stat, mem_diag, mem_h, mem_l, "norm_mem", MEM)
            for n in range(CA_H):
                bank = tile_ready(dve, "cross_k", n)
                dve.tensor_copy(ck[:, n, :], bank[:, :MEM]).then_inc(sem("bank_free"), 1)
            for n in range(4):
                bank = tile_ready(dve, "cross_v", n)
                dve.tensor_copy(cv[:, n % 2, n // 2 * 256:(n // 2 + 1) * 256], bank[:, :256]).then_inc(sem("bank_free"), 1)
            n_ca = CA_H * QT
            for s in range(n_ca + 4):
                if s < n_ca:
                    dve.wait_ge(sem("ca_s"), s + 1)
                    chain.link(dve.tensor_reduce(ca_stat[:, s % 4, 0:1], att_bank[s % 4][:, :MEM], AX_X, ALU.max))
                    if s >= 4:
                        dve.wait_ge(sem("ca_t"), s - 3)
                    dve.tensor_scalar(ca_stat[:, s % 4, 1:2], ca_stat[:, s % 4, 0:1], -CA_SCALE, None, ALU.mult)\
                       .then_inc(sem("ca_nm"), 1)
                u = s - 1
                if 0 <= u < n_ca:
                    dve.wait_ge(sem("ca_exp"), u + 1)
                    chain.link(dve.reciprocal(ca_stat[:, u % 4, 3:4], ca_stat[:, u % 4, 2:3]))
                    dve.tensor_scalar(ca_e[u % 4][:, :], ca_e[u % 4][:, :], ca_stat[:, u % 4, 3:4], None, ALU.mult)\
                       .then_inc(sem("ca_p"), 1)
                u = s - 4
                if u >= 0 and u % QT == QT - 1:
                    h = u // QT
                    dve.wait_ge(sem("ca_hi"), h + 1)
                    dve.tensor_tensor(xl[:, h, :], lin_bank[2 + h % 2][:, :], xh[:, h, :].bitcast(F32), ALU.subtract)\
                       .then_inc(sem("ca_lo"), 1)
            add_to_resid(dve, "cross_o", "n5")

        def block12_loads(sp, last=NB):
            first = LAYER["mix_fm"]["block"] + 2
            load_blocks(sp, 1, first)
            norm_done(sp, "n3")
            for v in range(2):
                sp.dma_start(cmp_w1[v][:, :, :], io["cmp_w1"][v]).then_inc(sem("cmp_loaded"), 16)
                sp.dma_start(cmp_w2[v][:, :, :], io["cmp_w2"][v]).then_inc(sem("cmp_loaded"), 16)
            load_blocks(sp, first, LAYER["out2"]["block"] + 2)
            sp.wait_ge(sem("br_lo"), KD)
            sp.dma_start(mem[:, :, :], io["mem_t"]).then_inc(sem("mem_loaded"), 16)
            load_blocks(sp, LAYER["out2"]["block"] + 2, last)

        HC = 2 * PH
        TG = 64
        NPAIR = NK // 2
        g_dram = nc.dram_tensor("g_scratch", (S // TG, NPAIR, P + 8, 2, TG), F32).ap()

        qp = [at(f"qp{i}", [P, S], scr(2 * i)) for i in range(4)]
        subkeys = at("subkeys", [P, HC * NK], scr(8))
        s_all = at("s_all", [P, HC * QT * NK], scr(64))
        ROWS, COLS = 4, 4
        WIDE = ROWS * PK
        NCAND = WIDE + (PK - ROWS) * COLS
        one_hot = at("one_hot", [P, 2 * PH, PK, PK], scr(0), BF16)
        top_s = at("top_s", [P, QT, PH, 2, PK], scr(16))
        top_i = at("top_i", [P, QT, PH, 2, PK], scr(20), U32)
        top_f = at("top_f", [P, 2, PH, PK], scr(24), BF16)
        cand = at("cand", [P, QT, NCAND], scr(25))
        place_f = at("place_f", [P, PH, PK], scr(28.5))
        wide_row = at("wide_row", [P, PH, PK], scr(29))
        tall_row = at("tall_row", [P, PH, PK], scr(29.5))
        is_tall = at("is_tall", [P, PH, PK], scr(30))
        tall_col = at("tall_col", [P, PH, PK], scr(30.5))
        j_half = at("j_half", [P, 2, PH, PK], scr(31))
        chosen = at("chosen", [P, 3, PH * PK], scr(96))
        g_stat = at("g_stat", [P, 2, QT, PH], scr(97.5))
        best_s = at("best_s", [P, QT, PH, 2, PK], scr(16))[:, :, :, 0, :]
        best_j = at("best_j", [P, QT, PH, 2, PK], scr(16), U32)[:, :, :, 1, :]
        best_e = at("best_e", [P, QT, PH, PK], WL + 4 * KB)
        wide_u = at("wide_u", [P, PH, PK], WL + 15 * KB, U32)
        tall_u = at("tall_u", [P, PH, PK], WL + 15 * KB + 512, U32)
        stage = [at("stage0", [P, NK, TG], scr(32)), at("stage1", [P, NK, TG], RAW)]
        turned_keys = at("turned_keys", [P, 2, S], WL, BF16)
        turned_weight = at("turned_weight", [P, S], WL + 2 * KB)
        BT = 8
        key_rows = at("key_rows", [P, NK, BT], scr(25), BF16)
        hits = [at(f"hits{i}", [P, 2, NK, BT], o, BF16) for i, o in enumerate((scr(8), scr(12), scr(72), scr(76)))]
        ab = [at(f"ab{i}", [P, 2, BT, NK], scr(80 + 8 * i)) for i in range(2)]
        u_raw = [at(f"u_raw{i}", [P, KD, P], scr(64 + 4 * i)) for i in range(4)]
        v_raw = [at(f"v_raw{i}", [P, D], scr(80 + 4 * i)) for i in range(4)]
        def four(name, shape, first, last):
            return [at(f"{name}{i}", shape, (first, first, last, last)[i] + i % 2 * 4 * KB, F32R) for i in range(4)]

        u_hi, u_lo = four("u_hi", [P, KD, P], scr(0), RAW), four("u_lo", [P, KD, P], scr(8), RAW + 8 * KB)
        v_hi, v_lo = four("v_hi", [P, D], scr(16), WH), four("v_lo", [P, D], scr(24), WH + 8 * KB)
        u_hi_first = at("u_hi_first", [P, KD, P], scr(8), F32R)
        u_lo_first = at("u_lo_first", [P, KD, P], scr(12), F32R)
        g_in = [at(f"g_in{i}", [P, S // TG, 2, TG], scr(32 + 4 * i)) for i in range(2)]
        h_raw = [at(f"h_raw{i}", [P, S], WL + (6 + 2 * i) * KB) for i in range(4)]
        h_hi = [at(f"h_hi{i}", [P, S], scr(40 + 2 * i), F32R) for i in range(4)]
        h_lo = [at(f"h_lo{i}", [P, S], scr(48 + 2 * i), F32R) for i in range(4)]
        out_sq = at("out_sq", [P, KD, S], scr(0))
        out_std = at("out_std", [P, S], scr(16))
        out_rstd = at("out_rstd", [P, S], scr(18))

        TURN_AT = P // BT - 4
        NB8 = P // BT
        BG = P // 4
        QUADS = NK // 4
        LOWEST = -3.0e38

        def peer_credits(pool):
            for name, n in (("pk_s", 4), ("pk_sc", 4), ("g_done", 4), ("g_free", 4), ("pk_t", 1), ("pk_idx", 1), ("g_stored0", 16), ("g_stored1", 16), ("a_rows", 4), ("b_rows", 4),
                            ("u_lo", 4), ("v_lo", 4), ("ge", 4), ("out_done", 16), ("out_free", 4), ("h_f", 4), ("h_lo", 4)):
                pool.nop().then_inc(sem(name), n)

        def peer_loads(sp):
            sp.wait_ge(sem("ca_lo"), CA_H)
            sp.dma_start(subkeys[:, :], io["subkeys_t"].rearrange("p h n -> p (h n)")).then_inc(sem("subkeys_loaded"), 16)
            load_blocks(sp, LAYER["peer_q"]["block"] + 2, NB)
            sp.wait_ge(sem("first_lists"), 1)
            for n in range(6):
                load_u(sp, 0, n)

            def store_g(i, q, pairs, name):
                sp.wait_ge(sem("g_free"), i * BG + (16 * (q + 1) + 4))
                sp.dma_start(g_dram[bass.ds(i * 2 + q, 1), pairs, 0:P].rearrange("o n p c t -> p (o n) c t"),
                             stage[q][:, 2 * pairs.start:2 * pairs.stop, :].rearrange("p (n c) t -> p n c t", c=2))\
                  .then_inc(sem(name), 16)

            everything = slice(0, NPAIR)
            with sp.Fori(0, QT - 1) as i:
                for q in range(2):
                    store_g(i, q, everything, f"g_stored{q}")
            store_g(QT - 1, 0, everything, "g_stored0")
            store_g(QT - 1, 1, slice(0, 4), "g_first")
            sp.wait_ge(sem("g_done"), 4 + QT * BG)
            load_v(sp, 0, 0)
            load_v(sp, 0, 1)
            wait(sp, ("g_stored0", 16 + 16 * QT), ("g_stored1", 16 * QT), ("g_first", 16))
            load_g(sp, 0, 0)
            load_g(sp, 0, 1)
            load_u(sp, 0, 6)
            load_u(sp, 0, 7)
            store_g(QT - 1, 1, slice(4, NPAIR), "g_stored1")
            load_v(sp, 0, 2)
            load_v(sp, 0, 3)
            sp.wait_ge(sem("g_stored1"), 16 + 16 * QT)

            def quad(i, last):
                for s in range(4):
                    load_v(sp, i, s)
                    if not last:
                        load_u(sp, i, s + 4)
                    if s % 2 == 0:
                        load_g(sp, i, s // 2)

            with sp.Fori(1, QUADS - 1) as i:
                quad(i, False)
            quad(QUADS - 1, True)

        def load_u(sp, i, n):
            sp.wait_ge(sem("u_lo"), i * 4 + (n + 1))
            sp.dma_start(u_raw[n % 4][:, :, :], io["expert_u"][at_chunk(i, n)]).then_inc(sem(f"u_loaded{n % 4}"), 16)

        def load_v(sp, i, n):
            sp.wait_ge(sem("v_lo"), i * 4 + (n + 1))
            sp.dma_start(v_raw[n % 4][:, :], io["expert_v"][at_chunk(i, n)]).then_inc(sem(f"v_loaded{n % 4}"), 16)

        def load_g(sp, i, b):
            sp.wait_ge(sem("h_f"), i * 4 + (2 * b + 2))
            n = i * 2 + b
            src = g_dram[:, bass.ds(n, 1), 0:P].rearrange("g o p c t -> g (o p) c t")
            sp.dma_start(g_in[b][:, :, :, :], src.rearrange("g p c t -> p g c t")).then_inc(sem(f"g_loaded{b}"), 16)

        def at_chunk(i, n):
            return i * 4 + n

        def split_u_hi(act, i, n, hi):
            act.wait_ge(sem(f"u_loaded{n % 4}"), i * 16 + 16 * (n // 4 + 1))
            act.activation(hi[:, :, :], u_raw[n % 4][:, :, :], ACT.Copy).then_inc(sem("u_hi"), 1)

        def split_u_lo(pool, i, n, hi, lo):
            pool.wait_ge(sem("u_hi"), i * 4 + (n + 1))
            pool.tensor_tensor(lo[:, :, :], u_raw[n % 4][:, :, :], hi[:, :, :].bitcast(F32), ALU.subtract)\
                .then_inc(sem("u_lo"), 1)

        def rows_needed(eng, i, n):
            eng.wait_ge(sem("hits_done"), i * NB8 + (n + 1))
            eng.wait_ge(sem("g_done"), i * BG + (2 * n + 2))

        def block3_pool(pool):
            norm_pool(pool, "n5", nrm2, xh, xl, S)
            for b in range(LAYER["peer_q"]["block"] + 2, NB):
                split_lo(pool, b)
            for n in range(4):
                split_u_lo(pool, 0, n, u_hi_first, u_lo_first)
            with pool.Fori(0, QT) as i:
                for n in range(NB8):
                    rows_needed(pool, i, n)
                    b = ab[n % 2][:, 1, :, :].rearrange("p t c -> p c t")
                    weight = turned_weight[:, bass.ds(i * P + BT * n, BT)].unsqueeze(1).to_broadcast([P, NK, BT])
                    pool.tensor_tensor(b, hits[n % 4][:, 1, :, :], weight, ALU.mult).then_inc(sem("b_rows"), 1)

            def quad(i, last):
                for n in (0, 2):
                    if not last:
                        for c in (n + 4, n + 5):
                            split_u_lo(pool, i, c, u_hi[c % 4], u_lo[c % 4])
                    for s in (n, n + 1):
                        pool.wait_ge(sem("v_hi"), i * 4 + (s + 1))
                        pool.tensor_tensor(v_lo[s][:, :], v_raw[s][:, :], v_hi[s][:, :].bitcast(F32), ALU.subtract)\
                            .then_inc(sem("v_lo"), 1)

            with pool.Fori(0, QUADS - 1) as i:
                quad(i, False)
            quad(QUADS - 1, True)

        def block3_act(act):
            norm_act(act, "n5", nrm2, norm_stat2, xh, S, "cross_o")

            def scores_out(n):
                act.wait_ge(sem("pk_s"), n + 5)
                act.activation(s_all[:, n * S:(n + 1) * S], att_bank[n % 4][:, :], ACT.Copy).then_inc(sem("pk_sc"), 1)

            for n in range(HC):
                bank = tile_ready(act, "peer_q", n)
                act.wait_ge(sem("pk_s"), n + 1)
                act.activation(qp[n % 4][:, :], bank[:, :], ACT.Copy).then_inc(sem("bank_free"), 1)
                if n % 2:
                    split_hi(act, LAYER["peer_q"]["block"] + n // 2 + 2)
                if n >= 1:
                    scores_out(n - 1)
            scores_out(HC - 1)

            def gelu(i, n):
                act.wait_ge(sem("act_done"), i * 4 + (n + 1))
                act.wait_ge(sem("h_lo"), i * 4 + (n + 1))
                act.activation(h_raw[n % 4][:, :], lin_bank[n % 4][:, :], ACT.Gelu).then_inc(sem("ge"), 1)

            for n in range(4):
                if n:
                    act.wait_ge(sem("act_done"), n)
                split_u_hi(act, 0, n, u_hi_first)
                if n:
                    gelu(0, n - 1)
            gelu(0, 3)
            act.wait_ge(sem("pk_gsub"), 1)
            act.activation(best_e[:, :, :, :], best_e[:, :, :, :], ACT.Exp).then_inc(sem("pk_gexp"), 1)

            def turn(i):
                act.wait_ge(sem("pk_t"), i + 2)
                act.activation(turned_weight[:, bass.ds(i * P, P)], att_bank[0][:, 2 * P:3 * P], ACT.Copy)
                act.activation(turned_keys[:, :, bass.ds(i * P, P)], att_bank[0][:, :2 * P].rearrange("p (j t) -> p j t", j=2),
                               ACT.Copy).then_inc(sem("pk_idx"), 1)

            def first_rows(i, n):
                rows_needed(act, i, n)
                act.activation(ab[n % 2][:, 0, :, :].rearrange("p t c -> p c t"), hits[n % 4][:, 0, :, :], ACT.Copy)\
                   .then_inc(sem("a_rows"), 1)

            def store_rows(i, last):
                for n in range(BG):
                    if n % 2 == 0 and not (last and n == BG - 2):
                        first_rows(i, n // 2 + 1)
                    if n == TURN_AT * 2 and not last:
                        turn(i + 1)
                    q = n // 16
                    if n % 16 == 0:
                        act.wait_ge(sem(f"g_stored{q}"), i * 16 + 16)
                    act.wait_ge(sem("g_done"), i * BG + (n + 5))
                    t = n % 16 * 4
                    act.activation(stage[q][:, :, t:t + 4], lin_bank[n % 4][:, :].rearrange("p (t c) -> p c t", t=4),
                                   ACT.Copy).then_inc(sem("g_free"), 1)

            turn(0)
            first_rows(0, 0)
            with act.Fori(0, QT - 1) as i:
                store_rows(i, False)
            store_rows(QT - 1, True)

            def quad(i, last):
                for n in (0, 2):
                    if n:
                        act.wait_ge(sem("g_stored1"), 16 + 16 * QT)
                    if not last:
                        for c in (n + 4, n + 5):
                            split_u_hi(act, i, c, u_hi[c % 4])
                    for s in (n, n + 1):
                        act.wait_ge(sem(f"v_loaded{s}"), i * 16 + 16)
                        act.wait_ge(sem("out_done"), i * 16 + 8 * (s // 2 + 1))
                        act.activation(v_hi[s][:, :], v_raw[s][:, :], ACT.Copy).then_inc(sem("v_hi"), 1)
                    for s in (n, n + 1):
                        act.wait_ge(sem("h_f"), i * 4 + (s + 5))
                        act.activation(h_hi[s][:, :], h_raw[s][:, :], ACT.Copy).then_inc(sem("h_hi"), 1)
                    if not last:
                        gelu(i, n + 4)
                        gelu(i, n + 5)

            with act.Fori(0, QUADS - 1) as i:
                quad(i, False)
            quad(QUADS - 1, True)
            act.wait_ge(sem("out_free"), 4 + 8 * NPAIR)
            for k in range(KD):
                act.activation(out_sq[:, k, :], resid[:, k, :], ACT.Square).then_inc(sem("n6_sq"), 1)
            act.wait_ge(sem("n6_sum"), 1)
            act.activation(out_std[:, :], lin_bank[0][:, :], ACT.Sqrt, bias=eps[:, 0:1], scale=1.0 / D)\
               .then_inc(sem("n6_std"), 1)

        def block3_pe(pe):
            norm_pe(pe, "n5", nrm2, norm_diag2, S)
            pe.wait_ge(sem("subkeys_loaded"), 16)
            t = LAYER["peer_q"]
            pairs_of = weights_first("peer_q", xh, xl)
            def step(i):
                def scores(n):
                    pe.wait_ge(sem("bank_free"), i * 4 + (t["tile"] + n + 5))
                    pe.wait_ge(sem("pk_sc"), i * 4 + (n + 1))
                    for tt in range(QT):
                        last = pe.matmul(att_bank[n][:, tt * NK:(tt + 1) * NK], qp[n][:, tt * P:(tt + 1) * P],
                                         subkeys[:, bass.ds(i * (4 * NK) + n * NK, NK)], start=True, stop=True)
                    last.then_inc(sem("pk_s"), 1)

                for n in range(4):
                    if n % 2 == 0:
                        pe.wait_ge(sem("lo_done"), i * 2 + (t["block"] + n // 2 + 3))
                    pe.wait_ge(sem("bank_free"), i * 4 + (t["tile"] + n + 1))
                    ready = follow_norm(pe, "n5") if isinstance(i, int) and n == 0 else None
                    products(pe, lin_bank[n][:, :], pairs_of(n // 2, n % 2), ready).then_inc(sem("lin_done"), 1)
                    if n >= 1:
                        scores(n - 1)
                scores(3)

            step(0)
            with pe.Fori(1, HC // 4) as i:
                step(i)
            pe.wait_ge(sem("pk_sc"), 4 + HC)

            def activations(i, n, hi, lo):
                pe.wait_ge(sem("u_lo"), i * 4 + (n + 5))
                pe.wait_ge(sem("ge"), i * 4 + (n + 1))
                pairs = [(hi[:, k, :], lo[:, k, :], xh[:, k, :], xl[:, k, :]) for k in range(KD)]
                products(pe, lin_bank[n % 4][:, :], pairs).then_inc(sem("act_done"), 1)

            pe.wait_ge(sem("bank_free"), 4 + TILES_AFTER[-1])
            for n in range(4):
                activations(0, n, u_hi_first, u_lo_first)
            pe.wait_ge(sem("ge"), 8)

            def turn(i):
                pe.wait_ge(sem("pk_keys"), i + 1)
                pe.wait_ge(sem("pk_idx"), i + 1)
                for j in range(3):
                    last = pe.transpose(att_bank[0][:, j * P:(j + 1) * P], chosen[:, j, :], ident[:, :])
                last.then_inc(sem("pk_t"), 1)

            def token_rows(i, last):
                for n in range(NB8):
                    if n == TURN_AT and not last:
                        turn(i + 1)
                    pe.wait_ge(sem("a_rows"), i * NB8 + (n + 5))
                    pe.wait_ge(sem("b_rows"), i * NB8 + (n + 5))
                    for g in (2 * n, 2 * n + 1):
                        pe.wait_ge(sem("g_free"), i * BG + (g + 1))
                        for t in range(4):
                            a, b = [ab[n % 2][:, half, g % 2 * 4 + t, :] for half in range(2)]
                            done = pe.matmul(lin_bank[g % 4][:, t * P:(t + 1) * P], a, b, start=True, stop=True)
                        done.then_inc(sem("g_done"), 1)

            turn(0)
            with pe.Fori(0, QT - 1) as i:
                token_rows(i, False)
            token_rows(QT - 1, True)
            pe.wait_ge(sem("g_free"), 4 + QT * BG)

            def outputs(i, b):
                pe.wait_ge(sem("v_lo"), i * 4 + (2 * b + 6))
                pe.wait_ge(sem("h_lo"), i * 4 + (2 * b + 6))
                for m in range(KD):
                    pe.wait_ge(sem("out_free"), i * 16 + (8 * b + m + 1))
                    cols = slice(m * P, (m + 1) * P)
                    pairs = [(v_hi[s][:, cols], v_lo[s][:, cols], h_hi[s][:, :], h_lo[s][:, :]) for s in (2 * b, 2 * b + 1)]
                    products(pe, att_bank[m % 4][:, :], pairs).then_inc(sem("out_done"), 1)

            def quad(i, last):
                for b in range(2):
                    if not last:
                        for n in (2 * b + 4, 2 * b + 5):
                            activations(i, n, u_hi[n % 4], u_lo[n % 4])
                    outputs(i, b)

            with pe.Fori(0, QUADS - 1) as i:
                quad(i, False)
            quad(QUADS - 1, True)
            for k in range(KD):
                pe.wait_ge(sem("n6_sq"), k + 1)
                last = pe.matmul(lin_bank[0][:, :], ones[:, :], out_sq[:, k, :], start=(k == 0), stop=(k == KD - 1))
            last.then_inc(sem("n6_sum"), 1)

        def block3_dve(dve, chain):
            norm_dve(dve, chain, "n5", resid, nrm2, norm_stat2, norm_diag2, xh, xl, "norm_ffn", S)
            link = chain.link

            def best16(n, values, best, index):
                for j in range(n):
                    ins = dve.max(best(j)[:, 0:8], values(j))
                link(ins)
                for j in range(n):
                    dve.max_index(index(j)[:, 0:8], best(j)[:, 0:8], values(j))
                for j in range(n):
                    ins = dve.match_replace(values(j), best(j)[:, 0:8], values(j), LOWEST)
                link(ins)
                for j in range(n):
                    ins = dve.max(best(j)[:, 8:16], values(j))
                link(ins)
                for j in range(n):
                    ins = dve.max_index(index(j)[:, 8:16], best(j)[:, 8:16], values(j))
                link(ins)

            for n in range(HC):
                dve.wait_ge(sem("pk_sc"), n + 5)
                best16(QT, lambda tt: s_all[:, (n * QT + tt) * NK:(n * QT + tt + 1) * NK],
                       lambda tt: top_s[:, tt, n // 2, n % 2, :], lambda tt: top_i[:, tt, n // 2, n % 2, :])

                if n % 2:
                    h = n // 2
                    for first, rows, cols, out in ((0, ROWS, PK, cand[:, :, 0:WIDE]), (ROWS, PK - ROWS, COLS, cand[:, :, WIDE:])):
                        grid = [P, QT, rows, cols]
                        ins = dve.tensor_tensor(out.rearrange("p i (a b) -> p i a b", b=cols),
                                                top_s[:, :, h, 0, first:first + rows].unsqueeze(3).to_broadcast(grid),
                                                top_s[:, :, h, 1, 0:cols].unsqueeze(2).to_broadcast(grid), ALU.add)
                    link(ins)
                    best16(QT, lambda tt: cand[:, tt, :], lambda tt: best_s[:, tt, h, :], lambda tt: best_j[:, tt, h, :])
                    if h == PH // 2 - 1:
                        dve.sem_inc(sem("first_lists"), 1)

            def places(tt):
                place = best_j[:, tt]
                link(dve.tensor_copy(top_f[:, :, :, :].rearrange("p j h k -> p h j k"), top_i[:, tt, :, :, :]))
                dve.tensor_scalar(wide_u[:, :, :], place, 4, None, ALU.logical_shift_right)
                dve.tensor_scalar(tall_u[:, :, :], place, 2, None, ALU.logical_shift_right)
                link(dve.tensor_copy(place_f[:, :, :], place))
                dve.tensor_copy(wide_row[:, :, :], wide_u[:, :, :])
                dve.tensor_copy(tall_row[:, :, :], tall_u[:, :, :])
                link(dve.tensor_scalar(is_tall[:, :, :], place_f[:, :, :], WIDE - 0.5, None, ALU.is_gt))
                wide_col = j_half[:, 1, :, :]
                dve.scalar_tensor_tensor(out=tall_col[:, :, :], in0=tall_row[:, :, :], scalar=-float(COLS), in1=place_f[:, :, :],
                                         op0=ALU.mult, op1=ALU.add)
                dve.scalar_tensor_tensor(out=wide_col, in0=wide_row[:, :, :], scalar=-float(PK), in1=place_f[:, :, :],
                                         op0=ALU.mult, op1=ALU.add)
                link(dve.scalar_tensor_tensor(out=tall_row[:, :, :], in0=tall_row[:, :, :], scalar=float(ROWS - WIDE // COLS),
                                              in1=wide_row[:, :, :], op0=ALU.add, op1=ALU.subtract))
                dve.tensor_tensor(tall_row[:, :, :], tall_row[:, :, :], is_tall[:, :, :], ALU.mult)
                link(dve.tensor_tensor(tall_col[:, :, :], tall_col[:, :, :], wide_col, ALU.subtract))
                dve.tensor_tensor(j_half[:, 0, :, :], wide_row[:, :, :], tall_row[:, :, :], ALU.add)
                link(dve.tensor_tensor(tall_col[:, :, :], tall_col[:, :, :], is_tall[:, :, :], ALU.mult))
                link(dve.tensor_tensor(wide_col, wide_col, tall_col[:, :, :], ALU.add))

            def mark_places():
                spread = j_half[:, :, :, :].rearrange("p j h k -> p (j h) k").unsqueeze(3).to_broadcast([P, 2 * PH, PK, PK])
                places = iota16[:, :].unsqueeze(1).unsqueeze(1).to_broadcast([P, 2 * PH, PK, PK])
                link(dve.tensor_tensor(one_hot[:, :, :, :], places, spread, ALU.is_equal))

            def keys(tt):
                listed = top_f[:, :, :, :].rearrange("p j h k -> p (j h) k").unsqueeze(2).to_broadcast([P, 2 * PH, PK, PK])
                link(dve.tensor_tensor(one_hot[:, :, :, :], one_hot[:, :, :, :], listed, ALU.mult))
                width = PK // 2
                while width > 1:
                    link(dve.tensor_tensor(one_hot[:, :, :, :width], one_hot[:, :, :, :width], one_hot[:, :, :, width:2 * width],
                                           ALU.add))
                    width //= 2
                dve.wait_ge(sem("pk_t"), tt + 1)
                dve.tensor_tensor(chosen[:, 0:2, :].rearrange("p j (h k) -> p (j h) k", h=PH), one_hot[:, :, :, 0],
                                  one_hot[:, :, :, 1], ALU.add)
                if tt == 0:
                    weights()
                dve.tensor_copy(chosen[:, 2, :], best_e[:, tt, :, :].rearrange("p h k -> p (h k)"))\
                   .then_inc(sem("pk_keys"), 1)

            def weights():
                dve.wait_ge(sem("pk_gexp"), 1)
                link(dve.tensor_reduce(g_stat[:, 0, :, :], best_e[:, :, :, :], AX_X, ALU.add))
                link(dve.reciprocal(g_stat[:, 1, :, :], g_stat[:, 0, :, :]))
                link(dve.tensor_tensor(best_e[:, :, :, :], best_e[:, :, :, :],
                                       g_stat[:, 1, :, :].unsqueeze(3).to_broadcast(all_best), ALU.mult))

            def hit_batches(tt, first, quads):
                def quad(i):
                    for n in range(4):
                        dve.wait_ge(sem("a_rows"), i * 4 + (tt * NB8 + n + 1))
                        dve.wait_ge(sem("b_rows"), i * 4 + (tt * NB8 + n + 1))
                        shape = [P, 2, NK, BT]
                        keys = turned_keys[:, :, bass.ds(i * (4 * BT) + (tt * P + BT * n), BT)]
                        dve.tensor_tensor(hits[n][:, :, :, :], key_rows[:, :, :].unsqueeze(1).to_broadcast(shape),
                                          keys.unsqueeze(2).to_broadcast(shape), ALU.is_equal).then_inc(sem("hits_done"), 1)

                if quads == 1:
                    quad(first)
                else:
                    with dve.Fori(first, first + quads) as i:
                        quad(i)

            all_best = [P, QT, PH, PK]
            dve.tensor_tensor(best_e[:, :, :, :], best_s, best_s[:, :, :, 0].unsqueeze(3).to_broadcast(all_best),
                              ALU.subtract).then_inc(sem("pk_gsub"), 1)
            places(0)
            mark_places()
            keys(0)
            link(dve.tensor_copy(key_rows[:, :, :], iota_key[:, :].unsqueeze(2).to_broadcast([P, NK, BT])))
            dve.wait_ge(sem("act_done"), 4)
            for tt in range(QT):
                dve.wait_ge(sem("pk_idx"), tt + 2)
                if tt < QT - 1:
                    hit_batches(tt, 0, 1)
                    places(tt + 1)
                    hit_batches(tt, 1, 1)
                    mark_places()
                    hit_batches(tt, 2, 1)
                    keys(tt + 1)
                    hit_batches(tt, 3, 1)
                else:
                    hit_batches(tt, 0, NB8 // 4)

            def weighted(i, n):
                s = n % 4
                dve.wait_ge(sem("ge"), i * 4 + (n + 5))
                if s % 2 == 0:
                    dve.wait_ge(sem(f"g_loaded{s // 2}"), i * 16 + 16 * (n // 4 + 1))
                h = h_raw[s][:, :].rearrange("p (g t) -> p g t", t=TG)
                dve.tensor_tensor(h, h, g_in[s // 2][:, :, s % 2, :], ALU.mult).then_inc(sem("h_f"), 1)
                dve.wait_ge(sem("h_hi"), i * 4 + (n + 1))
                dve.tensor_tensor(h_lo[s][:, :], h_raw[s][:, :], h_hi[s][:, :].bitcast(F32), ALU.subtract)\
                   .then_inc(sem("h_lo"), 1)

            def add_outputs(i, b):
                for m in range(KD):
                    dve.wait_ge(sem("out_done"), i * 16 + (16 + 8 * b + m + 1))
                    dve.tensor_tensor(resid[:, m, :], att_bank[m % 4][:, :], resid[:, m, :], ALU.add)\
                       .then_inc(sem("out_free"), 1)

            def quad(i, last):
                for b in range(2):
                    add_outputs(i, b)
                    if b == 0 or not last:
                        weighted(i, 2 * b + 2)
                        weighted(i, 2 * b + 3)

            weighted(0, 0)
            weighted(0, 1)
            with dve.Fori(0, QUADS - 1) as i:
                quad(i, False)
            quad(QUADS - 1, True)
            dve.wait_ge(sem("n6_std"), 1)
            chain.link(dve.reciprocal(out_rstd[:, :], out_std[:, :]))
            for k in range(KD):
                dve.scalar_tensor_tensor(out=out_sq[:, k, :], in0=resid[:, k, :], scalar=col("norm_final", k),
                                         in1=out_rstd[:, :], op0=ALU.mult, op1=ALU.mult).then_inc(sem("n6_out"), 1)

        def store_output(sp):
            for k in range(KD):
                sp.wait_ge(sem("n6_out"), k + 1)
                sp.dma_start(io["out_t"][:, k, :], out_sq[:, k, :]).then_inc(sem("out_stored"), 16)
            sp.wait_ge(sem("out_stored"), 16 * KD)
        block = ctx.enter_context(nc.Block())
        @block.sync
        def _(sp):
            for half in range(2):
                ks_ = slice(half * KD // 2, (half + 1) * KD // 2)
                sp.dma_start(resid[:, ks_, :], io["x_t"][:, ks_, :]).then_inc(sem(f"x_loaded{half}"), 16)
            load_blocks(sp, 0, 1)
            sp.dma_start(params[:, :], io["params"]).then_inc(sem("params_loaded"), 16)
            block12_loads(sp, LAYER["peer_q"]["block"] + 2)
            peer_loads(sp)
            store_output(sp)

        @block.gpsimd
        def _(pool):
            make_consts(pool)
            block1_pool(pool)
            block2_pool(pool)
            block3_pool(pool)

        @block.scalar
        def _(act):
            block1_act(act)
            block2_act(act)
            block3_act(act)

        @block.vector
        def _(dve):
            chain = Chain(dve, "dve_step")
            block1_dve(dve, chain)
            block2_dve(dve, chain)
            block3_dve(dve, chain)

        @block.tensor
        def _(pe):
            block1_pe(pe)
            block2_pe(pe)
            block3_pe(pe)


def blocks_of(w, kt, columns):
    w = np.asarray(w).reshape(kt, P, -1)
    return [np.concatenate([w[:, :, a:b] for a, b in part], axis=2).transpose(1, 0, 2).reshape(P, -1) for part in columns]


def lay_out(i):
    f = {k: np.asarray(v) for k, v in i.items()}
    w_in, w_mix, w_up, w_down = f["w_in"][0], f["w_in_2"][0], f["w_up"][0], f["w_down"][0]

    def runs(first, n, width):
        return [[(first + width * b, first + width * (b + 1))] for b in range(n)]

    def side_by_side(a, b, n):
        return [[(a + P * j, a + P * (j + 1)), (b + P * j, b + P * (j + 1))] for j in range(n)]

    A = AW
    kv = 4 * A
    gb = kv + 6 * P
    ga = gb + NSA_H * 3
    branches = np.concatenate([f["w_branch_a_2"][0], f["w_branch_b_2"][0]])
    split = FHALF[0] * P
    parts = {
        "in_fm": blocks_of(w_in, KD, runs(0, 4, 256) + side_by_side(3 * A, 3 * A + CW, CT)),
        "in_v": blocks_of(w_in, KD, runs(2 * A, 2, 256)),
        "out1": blocks_of(f["w_out"][0], KD, runs(0, 4, 256)),
        "up0": blocks_of(w_up, KD, side_by_side(0, FF, FT)[:FHALF[0]]),
        "down0": blocks_of(w_down[:split], FHALF[0], runs(0, 8, P)),
        "up1": blocks_of(w_up, KD, side_by_side(0, FF, FT)[FHALF[0]:]),
        "down1": blocks_of(w_down[split:], FHALF[1], runs(0, 8, P)),
        "mix_fm": blocks_of(w_mix, KD, runs(0, 4, 256) + runs(3 * A, 2, 256) + [
            [(kv, kv + 2 * P)], [(kv + 2 * P, kv + 3 * P), (kv + 4 * P, kv + 5 * P)]]),
        "mix_tm": blocks_of(w_mix, KD, runs(2 * A, 2, 256) + [
            [(kv + 3 * P, kv + 4 * P), (kv + 5 * P, kv + 6 * P)], [(gb, gb + 256)]]),
        "gates": blocks_of(w_mix, KD, side_by_side(ga, ga + D, KD)),
        "branch": blocks_of(branches, KD, runs(0, 4, 256)),
        "out2": blocks_of(f["w_out_2"][0], KD, runs(0, 4, 256)),
        "cross_q": blocks_of(f["w_cross_q_2"][0], KD, runs(0, 2, 256)),
        "cross_k": blocks_of(f["w_cross_kv_2"][0], KD, runs(0, 2, 256)),
        "cross_v": blocks_of(f["w_cross_kv_2"][0], KD, runs(AW, 2, 256)),
        "cross_o": blocks_of(f["w_cross_o_2"][0], AW // P, runs(0, 2, 512)),
        "peer_q": blocks_of(f["peer_wq_2"][0], KD, runs(0, 8, 256)),
    }
    w_small = np.zeros((len(TILES_AFTER), P, BLK), np.float32)
    for name, blocks in parts.items():
        for b, w in enumerate(blocks):
            w_small[LAYER[name]["block"] + b, :, :w.shape[1]] = w

    def tiles(v):
        return v.reshape(-1, P).T

    def channel_taps(v):
        return v.reshape(v.shape[0], -1, P).transpose(2, 1, 0).reshape(P, -1)

    def twice(v):
        return np.concatenate([v, v])

    params = np.concatenate([
        tiles(f["norm1_g"]), tiles(f["norm2_g"]), tiles(f["norm_mix_2"]), tiles(f["norm_cross_2"]),
        tiles(f["norm_mem_2"]), tiles(f["norm_ffn_2"]), tiles(f["norm_final_2"]),
        twice(f["q_norm_g"].T), twice(f["k_norm_g"].T), channel_taps(f["conv_dw_w"][0]), tiles(f["conv_dw_b"]),
        tiles(f["conv_ln_g"]), tiles(f["conv_ln_b"]), channel_taps(f["ffn_dw_w"][0]), tiles(f["ffn_dw_b"]),
        tiles(f["diff_subln_2"]), twice(f["nsa_cmp_pos_2"][0].T), twice(f["diff_lambda_2"][0].T)], axis=1)

    def feature_major(x):
        return x.T.reshape(KD, P, -1).transpose(1, 0, 2)

    def both(k, v, shape):
        return np.stack([f[k][0].reshape(shape).transpose(1, 0, 2), f[v][0].reshape(shape).transpose(1, 0, 2)])

    return {
        "x_t": feature_major(f["x"][0]), "mem_t": feature_major(f["mem_2"][0]), "params": params, "w_small": w_small,
        "cmp_w1": both("nsa_ck_w1_2", "nsa_cv_w1_2", (CMP // 2, P, CMP_HID)),
        "cmp_w2": both("nsa_ck_w2_2", "nsa_cv_w2_2", (CMP_HID // P, P, HD)),
        "subkeys_t": f["peer_subkeys_2"][0].reshape(2 * PH, NK, P).transpose(2, 0, 1),
        "expert_u": f["peer_u_2"][0].reshape(NK, NK, KD, P).transpose(1, 3, 2, 0),
        "expert_v": f["peer_v_2"][0].reshape(NK, NK, D).transpose(1, 0, 2),
    }


def kernel(**inputs):
    import concourse.bacc as bacc
    from concourse.bass_utils import run_bass_kernel_spmd

    arrays = {k: np.ascontiguousarray(v) for k, v in lay_out(inputs).items()}
    nc = bacc.Bacc("TRN2", target_bir_lowering=False, num_devices=1)
    io = {}
    for name, shape in INPUTS:
        assert arrays[name].shape == shape and arrays[name].dtype == np.float32
        io[name] = nc.dram_tensor(name, shape, F32, kind="ExternalInput").ap()
    for name, shape in OUTPUTS:
        io[name] = nc.dram_tensor(name, shape, F32, kind="ExternalOutput").ap()
    build_program(nc, io)
    out = run_bass_kernel_spmd(nc, [arrays], core_ids=[0]).results[0]["out_t"]
    return np.ascontiguousarray(out.transpose(2, 1, 0).reshape(1, S, D))
```
